# Optimizing a Trainium2 kernel written in Bass

```python
import math
import jax, jax.numpy as jnp
from jax import lax
import numpy as np

D_MODEL = 1024
BATCH = 1
SEQ = 512
DEPTH = 2

HEAD_DIM = 64
N_Q_HEADS = 8
N_KV_HEADS = 2
GQA_GROUP = N_Q_HEADS // N_KV_HEADS
ATTN_WIDTH = N_Q_HEADS * HEAD_DIM
KV_WIDTH = N_KV_HEADS * HEAD_DIM
N_CONV_GROUPS = 8
CONV_WIDTH = N_CONV_GROUPS * HEAD_DIM
MIX_WIDTH = ATTN_WIDTH + CONV_WIDTH
CONV_K = 3
WINDOW = 128
BLOCK = 128
D_FF = 2816
NORM_EPS = 1e-6

Q_END = ATTN_WIDTH
K_END = Q_END + KV_WIDTH
V_END = K_END + KV_WIDTH
CB_END = V_END + CONV_WIDTH
CC_END = CB_END + CONV_WIDTH
CH_END = CC_END + CONV_WIDTH
IN_WIDTH = CH_END


def rms_norm(x, gain):
    xf = x.astype(jnp.float32)
    inv = lax.rsqrt(jnp.mean(xf * xf, axis=-1, keepdims=True) + NORM_EPS)
    return (xf * inv).astype(x.dtype) * gain

def swiglu(h, w_gate, w_up, w_down):
    return (jax.nn.silu(h @ w_gate) * (h @ w_up)) @ w_down

def alibi_slopes(n_heads):
    return jnp.exp2(-8.0 * jnp.arange(1, n_heads + 1, dtype=jnp.float32) / n_heads)

def short_conv(b_gate, c_gate, h_conv, conv_w):
    u = c_gate * h_conv
    w = conv_w.astype(u.dtype)[:, None, :]
    y = lax.conv_general_dilated(
        u, w, window_strides=(1,), padding=[(CONV_K - 1, 0)],
        dimension_numbers=("NWC", "WIO", "NWC"), feature_group_count=CONV_WIDTH)
    return b_gate * y

def sliding_window_attention(q, k, v, sink):
    bsz, seq = q.shape[0], q.shape[1]
    nb = seq // BLOCK
    qb = q.reshape(bsz, nb, BLOCK, N_KV_HEADS, GQA_GROUP, HEAD_DIM)
    kb = k.reshape(bsz, nb, BLOCK, N_KV_HEADS, HEAD_DIM)
    vb = v.reshape(bsz, nb, BLOCK, N_KV_HEADS, HEAD_DIM)
    pad = ((0, 0), (1, 0), (0, 0), (0, 0), (0, 0))
    k_band = jnp.concatenate([jnp.pad(kb, pad)[:, :-1], kb], axis=2)
    v_band = jnp.concatenate([jnp.pad(vb, pad)[:, :-1], vb], axis=2)

    scale = 1.0 / math.sqrt(HEAD_DIM)
    scores = jnp.einsum("bnqkgd,bnskd->bnkgqs", qb, k_band).astype(jnp.float32) * scale

    qi = jnp.arange(BLOCK)[:, None]
    kj = jnp.arange(2 * BLOCK)[None, :]
    dist = qi + BLOCK - kj
    in_window = (dist >= 0) & (dist < WINDOW)
    blk = jnp.arange(nb)[:, None, None]
    mask = in_window[None] & ((blk > 0) | (kj[None] >= BLOCK))

    slopes = alibi_slopes(N_Q_HEADS).reshape(N_KV_HEADS, GQA_GROUP)
    bias = -slopes[:, :, None, None] * dist.astype(jnp.float32)[None, None]
    scores = scores + bias[None, None]
    mask_b = mask[None, :, None, None]
    scores = jnp.where(mask_b, scores, -jnp.inf)

    sink_l = sink.astype(jnp.float32).reshape(1, 1, N_KV_HEADS, GQA_GROUP, 1, 1)
    m = jnp.maximum(jnp.max(scores, axis=-1, keepdims=True), sink_l)
    p = jnp.where(mask_b, jnp.exp(scores - m), 0.0)
    denom = jnp.sum(p, axis=-1, keepdims=True) + jnp.exp(sink_l - m)
    probs = (p / denom).astype(v.dtype)
    out = jnp.einsum("bnkgqs,bnskd->bnqkgd", probs, v_band)
    return out.reshape(bsz, seq, ATTN_WIDTH)

def first_inputs(seed: int = 0) -> dict:
    key = jax.random.key(seed)
    ks = jax.random.split(key, 20)
    f32 = jnp.float32

    def w(k, shape, fan_in):
        return jax.random.normal(k, shape, f32) * (fan_in ** -0.5)

    def gain(k, shape):
        return 1.0 + 0.05 * jax.random.normal(k, shape, f32)

    return {
        "x": jax.random.normal(ks[0], (BATCH, SEQ, D_MODEL), f32),
        "ffn1_norm": gain(ks[1], (DEPTH, D_MODEL)),
        "ffn1_wg": w(ks[2], (DEPTH, D_MODEL, D_FF), D_MODEL),
        "ffn1_wu": w(ks[3], (DEPTH, D_MODEL, D_FF), D_MODEL),
        "ffn1_wd": w(ks[4], (DEPTH, D_FF, D_MODEL), D_FF),
        "mix_norm": gain(ks[5], (DEPTH, D_MODEL)),
        "w_in": w(ks[6], (DEPTH, D_MODEL, IN_WIDTH), D_MODEL),
        "conv_w": w(ks[7], (DEPTH, CONV_K, CONV_WIDTH), CONV_K),
        "attn_sink": 0.5 * jax.random.normal(ks[8], (DEPTH, N_Q_HEADS), f32),
        "w_out": w(ks[9], (DEPTH, MIX_WIDTH, D_MODEL), MIX_WIDTH),
        "ffn2_norm": gain(ks[10], (DEPTH, D_MODEL)),
        "ffn2_wg": w(ks[11], (DEPTH, D_MODEL, D_FF), D_MODEL),
        "ffn2_wu": w(ks[12], (DEPTH, D_MODEL, D_FF), D_MODEL),
        "ffn2_wd": w(ks[13], (DEPTH, D_FF, D_MODEL), D_FF),
        "final_norm": gain(ks[14], (D_MODEL,)),
    }

def first_block(x, ffn1_norm, ffn1_wg, ffn1_wu, ffn1_wd, mix_norm, w_in, conv_w,
              attn_sink, w_out, ffn2_norm, ffn2_wg, ffn2_wu, ffn2_wd, final_norm):
    bsz, seq, _ = x.shape
    for l in range(DEPTH):
        x = x + 0.5 * swiglu(rms_norm(x, ffn1_norm[l]), ffn1_wg[l], ffn1_wu[l], ffn1_wd[l])

        h = rms_norm(x, mix_norm[l])
        z = h @ w_in[l]
        q = z[..., :Q_END].reshape(bsz, seq, N_Q_HEADS, HEAD_DIM)
        k = z[..., Q_END:K_END].reshape(bsz, seq, N_KV_HEADS, HEAD_DIM)
        v = z[..., K_END:V_END].reshape(bsz, seq, N_KV_HEADS, HEAD_DIM)
        attn_out = sliding_window_attention(q, k, v, attn_sink[l])
        conv_out = short_conv(z[..., V_END:CB_END], z[..., CB_END:CC_END],
                              z[..., CC_END:CH_END], conv_w[l])
        x = x + jnp.concatenate([attn_out, conv_out], axis=-1) @ w_out[l]

        x = x + 0.5 * swiglu(rms_norm(x, ffn2_norm[l]), ffn2_wg[l], ffn2_wu[l], ffn2_wd[l])
    return rms_norm(x, final_norm)


DEPTH_2 = 1

CONV_CH = D_MODEL // 2
CONV_WIDTH_2 = 31
MLA_HEADS = 8
QK_NOPE = D_MODEL // 16
QK_ROPE = D_MODEL // 32
V_DIM = D_MODEL // 16
Q_LORA = 3 * D_MODEL // 8
KV_LORA = D_MODEL // 4
N_BRANCH = 2
IN_COLS = 2 * CONV_CH + Q_LORA + KV_LORA + QK_ROPE + N_BRANCH * D_MODEL
MEM_LEN = 256
X_HEADS = 4
X_HEAD_DIM = D_MODEL // 8
D_FF_2 = 4 * D_MODEL
Q_BLOCK = 128
ROPE_THETA = 10000.0
EPS = 1e-6


def rms_norm_2(x, g):
    xf = x.astype(jnp.float32)
    y = xf * lax.rsqrt(jnp.mean(xf * xf, axis=-1, keepdims=True) + EPS)
    return (y * g.astype(jnp.float32)).astype(x.dtype)

def layer_norm(x, g, b):
    xf = x.astype(jnp.float32)
    mu = jnp.mean(xf, axis=-1, keepdims=True)
    var = jnp.mean(jnp.square(xf - mu), axis=-1, keepdims=True)
    y = (xf - mu) * lax.rsqrt(var + EPS)
    return (y * g.astype(jnp.float32) + b.astype(jnp.float32)).astype(x.dtype)

def rope_tables(positions):
    half = QK_ROPE // 2
    inv_freq = ROPE_THETA ** (-jnp.arange(half, dtype=jnp.float32) / half)
    ang = positions.astype(jnp.float32)[..., None] * inv_freq
    return jnp.cos(ang), jnp.sin(ang)

def apply_rope(t, cos, sin):
    half = t.shape[-1] // 2
    t1, t2 = t[..., :half], t[..., half:]
    c, s = cos.astype(t.dtype), sin.astype(t.dtype)
    return jnp.concatenate([t1 * c - t2 * s, t2 * c + t1 * s], axis=-1)

def conformer_conv(conv_in, conv_w, conv_b, ln_g, ln_b, w_conv_out):
    a, gt = jnp.split(conv_in, 2, axis=-1)
    z = a * jax.nn.sigmoid(gt)
    rhs = conv_w.astype(z.dtype).reshape(CONV_WIDTH_2, 1, CONV_CH)
    z = lax.conv_general_dilated(
        z, rhs, window_strides=(1,), padding=[(CONV_WIDTH_2 - 1, 0)],
        dimension_numbers=("NWC", "WIO", "NWC"), feature_group_count=CONV_CH)
    z = z + conv_b
    z = layer_norm(z, ln_g, ln_b)
    z = jax.nn.silu(z)
    return z @ w_conv_out

def mla_attention(c_q, c_kv, k_rope_raw, cos, sin, q_norm_g, w_uq, kv_norm_g, w_ukv, w_mla_out):
    B, S, _ = c_q.shape
    q = rms_norm_2(c_q, q_norm_g) @ w_uq
    q = q.reshape(B, S, MLA_HEADS, QK_NOPE + QK_ROPE)
    q_nope, q_rope = q[..., :QK_NOPE], q[..., QK_NOPE:]
    q_rope = apply_rope(q_rope, cos[:, :, None, :], sin[:, :, None, :])
    kv = rms_norm_2(c_kv, kv_norm_g) @ w_ukv
    kv = kv.reshape(B, S, MLA_HEADS, QK_NOPE + V_DIM)
    k_nope, v = kv[..., :QK_NOPE], kv[..., QK_NOPE:]
    k_rope = apply_rope(k_rope_raw, cos, sin)

    scale = (QK_NOPE + QK_ROPE) ** -0.5
    n_blk = S // Q_BLOCK
    qn = (q_nope * scale).reshape(B, n_blk, Q_BLOCK, MLA_HEADS, QK_NOPE).transpose(1, 0, 2, 3, 4)
    qr = (q_rope * scale).reshape(B, n_blk, Q_BLOCK, MLA_HEADS, QK_ROPE).transpose(1, 0, 2, 3, 4)
    key_idx = jnp.arange(S)
    neg = jnp.finfo(jnp.float32).min

    def attend(args):
        qn_b, qr_b, blk = args
        s = jnp.einsum("bqhd,bkhd->bhqk", qn_b, k_nope, preferred_element_type=jnp.float32)
        s = s + jnp.einsum("bqhr,bkr->bhqk", qr_b, k_rope, preferred_element_type=jnp.float32)
        q_idx = blk * Q_BLOCK + jnp.arange(Q_BLOCK)
        mask = key_idx[None, :] <= q_idx[:, None]
        s = jnp.where(mask[None, None], s, neg)
        p = jax.nn.softmax(s, axis=-1).astype(v.dtype)
        return jnp.einsum("bhqk,bkhd->bqhd", p, v)

    o = lax.map(attend, (qn, qr, jnp.arange(n_blk)))
    o = o.transpose(1, 0, 2, 3, 4).reshape(B, S, MLA_HEADS * V_DIM)
    return o @ w_mla_out

def memory_cross_attention(u, mem_n, w_xq, w_xkv, w_xo):
    B, S, _ = u.shape
    q = (u @ w_xq).reshape(B, S, X_HEADS, X_HEAD_DIM) * (X_HEAD_DIM ** -0.5)
    kv = (mem_n @ w_xkv).reshape(B, MEM_LEN, 2, X_HEADS, X_HEAD_DIM)
    k, v = kv[:, :, 0], kv[:, :, 1]
    s = jnp.einsum("bqhd,bkhd->bhqk", q, k, preferred_element_type=jnp.float32)
    p = jax.nn.softmax(s, axis=-1).astype(v.dtype)
    o = jnp.einsum("bhqk,bkhd->bqhd", p, v).reshape(B, S, X_HEADS * X_HEAD_DIM)
    return o @ w_xo

def second_inputs(seed: int = 0) -> dict:
    key = jax.random.key(seed)
    ks = jax.random.split(key, 32)
    f32 = jnp.float32

    def w(k, shape, fan_in):
        return jax.random.normal(k, shape, f32) * (fan_in ** -0.5)

    def gain(k, shape):
        return 1.0 + 0.02 * jax.random.normal(k, shape, f32)

    L = DEPTH_2
    x = jax.random.normal(ks[0], (BATCH, SEQ, D_MODEL), f32)
    mem = jax.random.normal(ks[1], (BATCH, MEM_LEN, D_MODEL), f32)
    offsets = jax.random.randint(ks[2], (BATCH, 1), 0, 4096, dtype=jnp.int32)
    positions = offsets + jnp.arange(SEQ, dtype=jnp.int32)[None, :]
    return {
        "x": x,
        "mem": mem,
        "positions": positions,
        "norm_mix_g": gain(ks[3], (L, D_MODEL)),
        "w_in": w(ks[4], (L, D_MODEL, IN_COLS), D_MODEL),
        "conv_w": w(ks[5], (L, CONV_WIDTH_2, CONV_CH), CONV_WIDTH_2),
        "conv_b": 0.02 * jax.random.normal(ks[6], (L, CONV_CH), f32),
        "conv_ln_g": gain(ks[7], (L, CONV_CH)),
        "conv_ln_b": 0.02 * jax.random.normal(ks[8], (L, CONV_CH), f32),
        "w_conv_out": w(ks[9], (L, CONV_CH, D_MODEL), CONV_CH),
        "q_norm_g": gain(ks[10], (L, Q_LORA)),
        "w_uq": w(ks[11], (L, Q_LORA, MLA_HEADS * (QK_NOPE + QK_ROPE)), Q_LORA),
        "kv_norm_g": gain(ks[12], (L, KV_LORA)),
        "w_ukv": w(ks[13], (L, KV_LORA, MLA_HEADS * (QK_NOPE + V_DIM)), KV_LORA),
        "w_mla_out": w(ks[14], (L, MLA_HEADS * V_DIM, D_MODEL), MLA_HEADS * V_DIM),
        "w_out": w(ks[15], (L, D_MODEL, D_MODEL), D_MODEL),
        "norm_xattn_g": gain(ks[16], (L, D_MODEL)),
        "norm_mem_g": gain(ks[17], (L, D_MODEL)),
        "w_xq": w(ks[18], (L, D_MODEL, X_HEADS * X_HEAD_DIM), D_MODEL),
        "w_xkv": w(ks[19], (L, D_MODEL, 2 * X_HEADS * X_HEAD_DIM), D_MODEL),
        "w_xo": w(ks[20], (L, X_HEADS * X_HEAD_DIM, D_MODEL), X_HEADS * X_HEAD_DIM),
        "norm_mlp_g": gain(ks[21], (L, D_MODEL)),
        "w_mlp1": w(ks[22], (L, D_MODEL, D_FF_2), D_MODEL),
        "w_mlp2": w(ks[23], (L, D_FF_2, D_MODEL), D_FF_2),
        "final_norm_g": gain(ks[24], (D_MODEL,)),
    }

def second_block(x, mem, positions, norm_mix_g, w_in, conv_w, conv_b, conv_ln_g, conv_ln_b,
              w_conv_out, q_norm_g, w_uq, kv_norm_g, w_ukv, w_mla_out, w_out,
              norm_xattn_g, norm_mem_g, w_xq, w_xkv, w_xo, norm_mlp_g, w_mlp1, w_mlp2,
              final_norm_g):
    cos, sin = rope_tables(positions)
    B, S, _ = x.shape
    cut = np.cumsum([2 * CONV_CH, Q_LORA, KV_LORA, QK_ROPE]).tolist()
    h = x
    for l in range(DEPTH_2):
        u = rms_norm_2(h, norm_mix_g[l])
        proj = u @ w_in[l]
        conv_in, c_q, c_kv, k_rope_raw, gate_logits = jnp.split(proj, cut, axis=-1)
        conv_out = conformer_conv(conv_in, conv_w[l], conv_b[l], conv_ln_g[l], conv_ln_b[l],
                                  w_conv_out[l])
        mla_out = mla_attention(c_q, c_kv, k_rope_raw, cos, sin, q_norm_g[l], w_uq[l],
                                kv_norm_g[l], w_ukv[l], w_mla_out[l])
        gates = jax.nn.sigmoid(gate_logits).reshape(B, S, N_BRANCH, D_MODEL)
        merged = gates[:, :, 0] * conv_out + gates[:, :, 1] * mla_out
        h = h + merged @ w_out[l]
        u = rms_norm_2(h, norm_xattn_g[l])
        mem_n = rms_norm_2(mem, norm_mem_g[l])
        h = h + memory_cross_attention(u, mem_n, w_xq[l], w_xkv[l], w_xo[l])
        u = rms_norm_2(h, norm_mlp_g[l])
        h = h + jnp.square(jax.nn.relu(u @ w_mlp1[l])) @ w_mlp2[l]
    return rms_norm_2(h, final_norm_g)


def setup_inputs(seed=0):
    out = dict(first_inputs(seed))
    for name, value in second_inputs(seed + 1).items():
        if name != "x":
            out[name + "_2"] = value
    return out


def reference(
    x, ffn1_norm, ffn1_wg, ffn1_wu, ffn1_wd, mix_norm, w_in, conv_w, attn_sink, w_out,
    ffn2_norm, ffn2_wg, ffn2_wu, ffn2_wd, final_norm, mem_2, positions_2, norm_mix_g_2, w_in_2,
    conv_w_2, conv_b_2, conv_ln_g_2, conv_ln_b_2, w_conv_out_2, q_norm_g_2, w_uq_2, kv_norm_g_2,
    w_ukv_2, w_mla_out_2, w_out_2, norm_xattn_g_2, norm_mem_g_2, w_xq_2, w_xkv_2, w_xo_2,
    norm_mlp_g_2, w_mlp1_2, w_mlp2_2, final_norm_g_2,
):
    x = first_block(
        x, ffn1_norm, ffn1_wg, ffn1_wu, ffn1_wd, mix_norm, w_in, conv_w, attn_sink, w_out,
        ffn2_norm, ffn2_wg, ffn2_wu, ffn2_wd, final_norm,
    )
    return second_block(
        x, mem_2, positions_2, norm_mix_g_2, w_in_2, conv_w_2, conv_b_2, conv_ln_g_2,
        conv_ln_b_2, w_conv_out_2, q_norm_g_2, w_uq_2, kv_norm_g_2, w_ukv_2, w_mla_out_2,
        w_out_2, norm_xattn_g_2, norm_mem_g_2, w_xq_2, w_xkv_2, w_xo_2, norm_mlp_g_2, w_mlp1_2,
        w_mlp2_2, final_norm_g_2,
    )


_drawn_inputs = setup_inputs


def setup_inputs(seed=0):
    import zlib

    import numpy as np

    out = dict(_drawn_inputs(seed))
    spreads = {}
    factors = {'attn_sink': 4.452,
     'norm_mix_g_2': 6.8,
     'conv_b_2': 4.358,
     'conv_ln_g_2': 7.323,
     'conv_ln_b_2': 8.0,
     'q_norm_g_2': 8.0,
     'kv_norm_g_2': 8.0,
     'norm_xattn_g_2': 8.0,
     'norm_mem_g_2': 8.0,
     'norm_mlp_g_2': 10.12,
     'final_norm_g_2': 8.003}
    for name, (base, spread) in spreads.items():
        noise = np.random.default_rng([zlib.crc32(name.encode()), seed]).standard_normal(out[name].shape)
        drawn = base * np.exp(spread * noise) if base else spread * noise
        out[name] = __import__('jax').numpy.asarray(drawn.astype(out[name].dtype))
    for name, factor in factors.items():
        out[name] = (out[name] * factor).astype(out[name].dtype)
    return out
```

```python
from contextlib import ExitStack

import concourse.bass as bass
from concourse import mybir

P = 128
ALU = mybir.AluOpType
ACT = mybir.ActivationFunctionType
AX = mybir.AxisListType
F32 = mybir.dt.float32
F32R = mybir.dt.float32r
ds = bass.ds

RING = 4
AHEAD = 3
UNIT = 8 * P
LANDED = 64
MASKED = 1e30


def build(nc, t, out):
    S, D = t["x"].shape[1:]
    L, _, FF = t["ffn1_wg"].shape
    KC = D // P
    TB = S // P
    FC = FF // P
    EPS = 1e-6
    HD = 64
    H1 = t["attn_sink"].shape[1]
    G1 = H1 // 2
    CW = t["conv_w"].shape[2]
    CC = CW // P
    Q0, K0, V0 = 0, H1 * HD, H1 * HD + P
    CB0 = V0 + P
    STEPS1 = 2 * TB

    ML = t["mem_2"].shape[1]
    MB = ML // P
    TAPS = t["conv_w_2"].shape[1]
    QL = t["q_norm_g_2"].shape[1]
    KVL = t["kv_norm_g_2"].shape[1]
    QC, KVC = QL // P, KVL // P
    ROPE = 32
    HALF = ROPE // 2
    NOPE = 64
    QK = NOPE + ROPE
    H2 = t["w_uq_2"].shape[2] // QK
    H3 = 4
    FF2 = t["w_mlp1_2"].shape[2]
    FP = FF2 // P // 2
    A0, GT0, CQ0 = 0, CW, 2 * CW
    CKV0 = CQ0 + QL
    KR0 = CKV0 + KVL
    GL0 = KR0 + ROPE
    PADZ = 32
    ZW = PADZ + S
    MLA_STEPS = 2 * H2
    BLOCKS = ((0, TB - 1), (1, TB - 2))

    ctx = ExitStack()
    with ctx:
        def sem(name):
            return ctx.enter_context(nc.semaphore(name))

        base = (nc.sbuf_base + 31) // 32 * 32
        at = [base]

        def sb(name, cols, dt=F32, off=None, rows=P):
            if off is None:
                off = -(-at[0] // 32) * 32
                at[0] = off + cols * 4
            return nc.alloc_sbuf_tensor_at(name, [rows, cols], dt, offset=off)

        x = sb("x", KC * S)
        X_AT = at[0]
        xhi = sb("xhi", KC * S, F32R)
        xlo = sb("xlo", KC * S, F32R)
        raw = sb("raw", RING * UNIT)
        whi = sb("whi", RING * UNIT, F32R)
        wlo = sb("wlo", RING * UNIT, F32R)
        ident = sb("ident", P)
        ones = sb("ones", P)
        acc = sb("acc", S)
        sqt = sb("sqt", S)
        var = sb("var", S)
        inv = sb("inv", S)
        gains = sb("gains", 13 * KC)
        inv6 = sb("inv6", S)
        rope = sb("rope", S)
        mask = sb("mask", P)
        cw2 = sb("cw2", TAPS * CC)
        cvec = sb("cvec", 3 * CC)
        lgain = sb("lgain", QC + KVC)
        frow = sb("frow", 2 * P, rows=1)
        fcol = sb("fcol", 2)
        st2 = sb("st2", 32)
        pos = sb("pos", S, mybir.dt.int32)
        cw1 = sb("cw1", L * 3 * CC)
        sink = sb("sink", L * H1)
        nsink = sb("nsink", L * H1)
        dist = sb("dist", 2 * P)
        tmp = [sb(f"tmp{i}", S) for i in range(4)]
        st = sb("st", 4 * 8)
        region = at[0]
        hhi = sb("hhi", FC * S, F32R)
        hlo = sb("hlo", FC * S, F32R)
        assert at[0] <= nc.sbuf_usable_end, (at[0], nc.sbuf_usable_end)
        top = at[0]

        at[0] = region
        xin = sb("xin", TB * D)
        at[0] = region
        yhi = sb("yhi", KC * S, F32R)
        ylo = sb("ylo", KC * S, F32R)
        qhi = sb("qhi", 4 * S, F32R)
        qlo = sb("qlo", 4 * S, F32R)
        khi = sb("khi", S, F32R)
        klo = sb("klo", S, F32R)
        vhi = sb("vhi", S, F32R)
        vlo = sb("vlo", S, F32R)
        sc = [sb(f"sc{i}", 8 * P) for i in range(2)]
        pthi = sb("pthi", 8 * P, F32R)
        ptlo = sb("ptlo", 8 * P, F32R)
        upad = [sb(f"upad{i}", S + 8) for i in range(2)]
        cy = [sb(f"cy{i}", S) for i in range(2)]
        assert at[0] <= top, (at[0] - top)

        at[0] = region
        gates = sb("gates", 2 * KC * S)
        sq7 = sb("sq7", KC * S, off=region)
        lath = sb("lath", (QC + KVC) * S, F32R)
        latl = sb("latl", (QC + KVC) * S, F32R)
        zpad = sb("zpad", CC * ZW, off=at[0])
        chi = sb("chi", CC * S, F32R)
        clo = sb("clo", CC * S, F32R)
        latf = sb("latf", (QC + KVC) * S, off=at[0])
        v2h = sb("v2h", TB * S, F32R)
        v2l = sb("v2l", TB * S, F32R)
        zc = sb("zc", CC * S, off=at[0])
        p2 = [sb(f"p2_{i}", 5 * P) for i in range(2)]
        pt2h = sb("pt2h", 5 * P, F32R)
        pt2l = sb("pt2l", 5 * P, F32R)
        assert at[0] <= nc.sbuf_usable_end, (at[0], nc.sbuf_usable_end)
        at[0] = X_AT
        q2h = sb("q2h", 2 * S, F32R)
        q2l = sb("q2l", 2 * S, F32R)
        k2h = sb("k2h", 2 * S, F32R)
        k2l = sb("k2l", 2 * S, F32R)
        a2h = sb("a2h", CC * S, F32R)
        a2l = sb("a2l", CC * S, F32R)
        mgh = xhi
        at[0] = v2h.manual_sbuf_range[0]
        mgl = sb("mgl", KC * S, F32R)
        at[0] = X_AT
        p3 = [sb(f"p3_{i}", 8 * P) for i in range(2)]
        pt3h = sb("pt3h", 8 * P, F32R)
        pt3l = sb("pt3l", 8 * P, F32R)
        at[0] = region
        xbh = sb("xbh", KC * S, F32R)
        xbl = sb("xbl", KC * S, F32R)
        memr = sb("memr", MB * D)
        mscr = sb("mscr", MB * D, off=at[0])
        mth = sb("mth", KC * ML, F32R)
        mtl = sb("mtl", KC * ML, F32R)
        q3h = sb("q3h", H3 * S, F32R)
        q3l = sb("q3l", H3 * S, F32R)
        k3h = sb("k3h", H3 * ML, F32R)
        k3l = sb("k3l", H3 * ML, F32R)
        v3h = sb("v3h", MB * H3 * P, F32R)
        v3l = sb("v3l", MB * H3 * P, F32R)
        assert at[0] <= nc.sbuf_usable_end, (at[0], nc.sbuf_usable_end)
        at[0] = region
        a3h = sb("a3h", H3 * S, F32R)
        a3l = sb("a3l", H3 * S, F32R)
        at[0] = region
        mhi = sb("mhi", FP * S, F32R)
        mlo = sb("mlo", FP * S, F32R)

        bank = [ctx.enter_context(nc.psum_tensor(f"bank{i}", [P, 512], F32)) for i in range(3)]
        psS = ctx.enter_context(nc.psum_tensor("psS", [P, 1024], F32))
        psT = ctx.enter_context(nc.psum_tensor("psT", [P, 1024], F32))
        psO = ctx.enter_context(nc.psum_tensor("psO", [P, 512], F32))
        gate_b = [bank[0], psS[:, 0:512]]
        up_b = [bank[1], bank[2]]
        down_b = [psT[:, 0:512], psT[:, 512:1024]]

        def b(ap):
            return ap[:, :] if not isinstance(ap, bass.AP) else ap

        landed = [sem(f"landed{i}") for i in range(RING)]
        s_hi = sem("weights_hi_ready")
        s_split = sem("weights_split")
        s_used = sem("weights_used")
        s_par = sem("params_landed")
        s_par2 = sem("params2_landed")
        s_xin = sem("x_landed")
        s_const = sem("consts_ready")
        s_ident = sem("ident_zeroed")
        s_xt = sem("x_transposed")
        s_x = sem("x_ready")
        s_xh = sem("xhi_ready")
        s_xl = sem("xlo_ready")
        s_sqm = sem("square_made")
        s_sq = sem("squares_summed")
        s_ss = sem("sum_of_squares")
        s_var = sem("variance_ready")
        s_rt = sem("root_ready")
        s_nst = sem("newton_step")
        s_inv = sem("inv_ready")
        s_gs = sem("gate_scaled")
        s_si = sem("silu_done")
        s_us = sem("up_scaled")
        s_h = sem("hidden_ready")
        s_hh = sem("hidden_hi_ready")
        s_hl = sem("hidden_lo_ready")
        s_ns = sem("nsink_ready")
        s_vs = sem("v_scaled")
        s_vt = sem("v_transposed")
        s_vh = sem("vhi_ready")
        s_vl = sem("vlo_ready")
        s_qs = sem("qk_scaled")
        s_qh = sem("qk_hi_ready")
        s_ql = sem("qk_lo_ready")
        a_sc = sem("scores_done")
        a_bi = sem("scores_biased")
        a_rm = sem("row_max_made")
        a_mx = sem("max_with_sink")
        a_sd = sem("shift_ready")
        a_ex = sem("exp_done")
        a_dn = sem("denominator_ready")
        a_rd = sem("reciprocal_ready")
        a_pr = sem("probs_ready")
        a_tt = sem("probs_transposed")
        a_th = sem("probs_hi_ready")
        a_tl = sem("probs_lo_ready")
        a_pv = sem("pv_done")
        a_oh = sem("attn_hi_ready")
        a_ol = sem("attn_lo_ready")
        c_ev = sem("conv_part_scaled")
        c_u = sem("conv_input_ready")
        c_t2 = sem("conv_tap2_done")
        c_t1 = sem("conv_tap1_done")
        c_t0 = sem("conv_tap0_done")
        c_y = sem("conv_gated")
        c_yh = sem("conv_hi_ready")
        c_yl = sem("conv_lo_ready")
        s_pad = sem("pads_zeroed")
        s_i2 = sem("w_in2_scaled")
        s_g67 = sem("gain_product_ready")
        s_v7 = sem("variance7_step")
        s_i67 = sem("inv67_ready")
        s_q7 = sem("squares7_ready")
        s_z = sem("glu_ready")
        s_zp = sem("glu_pads_zeroed")
        s_th = sem("glu_tanh_done")
        s_tap = sem("dve_tap_done")
        s_pm = sem("tap_product_ready")
        s_pa = sem("tap_added")
        s_gt = sem("gate_tanh_done")
        s_lq = sem("latent_squared")
        s_ln = sem("latent_normed")
        s_lh = sem("latent_hi_ready")
        s_ll = sem("latent_lo_ready")
        s_fr = sem("freq_row_ready")
        s_ft = sem("freq_turned")
        s_fc = sem("freq_column_ready")
        s_ro = sem("rope_step")
        s_rr = sem("rope_angles_ready")
        s_rs = sem("rope_table_ready")
        s_mk = sem("mask_ready")
        s_lsum = sem("layer_norm_sum")
        s_lm = sem("layer_norm_mean")
        s_ld = sem("layer_norm_centred")
        s_lsq = sem("layer_norm_squared")
        s_ly = sem("layer_norm_scaled")
        s_la = sem("layer_norm_affine")
        s_lt = sem("conv_tanh_done")
        s_lc = sem("conv_silu_done")
        s_ch = sem("conv2_hi_ready")
        s_cl = sem("conv2_lo_ready")
        s_v2 = sem("v2_projected")
        s_v2h = sem("v2_hi_ready")
        s_v2l = sem("v2_lo_ready")
        s_kr = sem("k_rope_step")
        s_krh = sem("k_rope_hi_ready")
        s_krl = sem("k_rope_lo_ready")
        h_cp = sem("q_nope_copied")
        h_rp = sem("q_rope_step")
        h_hi = sem("head_hi_ready")
        h_lo = sem("head_lo_ready")
        b_sc = sem("mla_scores_done")
        b_mk = sem("mla_scores_masked")
        b_mx = sem("mla_max_ready")
        b_ex = sem("mla_exp_done")
        b_rd = sem("mla_reciprocal_ready")
        b_pr = sem("mla_probs_ready")
        b_tt = sem("mla_probs_transposed")
        b_th = sem("mla_probs_hi_ready")
        b_tl = sem("mla_probs_lo_ready")
        b_pv = sem("mla_pv_done")
        b_oh = sem("mla_out_hi_ready")
        b_ol = sem("mla_out_lo_ready")
        s_ga = sem("branches_gated")
        s_mg = sem("branches_merged")
        s_mgh = sem("merged_hi_ready")
        s_mgl = sem("merged_lo_ready")
        s_memin = sem("mem_landed")
        s_msq = sem("mem_squared")
        s_mv = sem("mem_variance_ready")
        s_mr = sem("mem_root_ready")
        s_mst = sem("mem_newton_step")
        s_mn = sem("mem_normed")
        s_mt = sem("mem_transposed")
        s_mh = sem("mem_hi_ready")
        s_ml = sem("mem_lo_ready")
        s_x2 = sem("cross_q_scaled")
        s_x2h = sem("cross_q_hi_ready")
        s_x2l = sem("cross_q_lo_ready")
        s_k3h = sem("cross_k_hi_ready")
        s_k3l = sem("cross_k_lo_ready")
        s_v3h = sem("cross_v_hi_ready")
        s_v3l = sem("cross_v_lo_ready")
        d_sc = sem("cross_scores_done")
        d_mx = sem("cross_max_ready")
        d_ex = sem("cross_exp_done")
        d_rd = sem("cross_reciprocal_ready")
        d_pr = sem("cross_probs_ready")
        d_tt = sem("cross_probs_transposed")
        d_th = sem("cross_probs_hi_ready")
        d_tl = sem("cross_probs_lo_ready")
        d_pv = sem("cross_pv_done")
        d_oh = sem("cross_out_hi_ready")
        d_ol = sem("cross_out_lo_ready")
        m_r = sem("mlp_relu_done")
        m_sq = sem("mlp_squared")
        m_hi = sem("mlp_hi_ready")
        m_lo = sem("mlp_lo_ready")
        s_o = sem("out_scaled")
        s_ot = sem("out_transposed")
        s_oc = sem("out_copied")
        s_out = [sem(f"out_written{i}") for i in range(2)]

        U_GU = 2 * FC
        U_FFN = U_GU + 3 * KC
        U_MIX = 8 + 3 * CC + KC
        U_LAYER = 2 * U_FFN + U_MIX
        C_IN = L * U_LAYER
        IN_UNITS = 2 * CC + QC + KVC + 1 + 2 * KC
        C_MLA = C_IN + IN_UNITS
        C_MRG = C_MLA + 1 + H2
        C_OUT = C_MRG + KC
        C_XQ = C_OUT + KC
        C_XK = C_XQ + H3
        C_XV = C_XK + H3
        C_XO = C_XV + KC // 2
        C_MLP = C_XO + KC // 2
        U_PASS = FP + 2 * KC
        C_END = C_MLP + 2 * U_PASS
        ORDER = [(k, i) for i in range(CC) for k in ("a", "g")] + [("q", i) for i in range(QC)] \
            + [("kv", i) for i in range(KVC)] + [("kr", 0)] + [("gate", i) for i in range(2 * KC)]
        U_KR = 2 * CC + QC + KVC
        U_GATE = U_KR + 1
        FINAL1, SUM7, LATQ, LATKV, LNVAR, XATTN, MLPN, FINAL2 = range(3 * L, 3 * L + 8)
        G67, GX, GM, G6, GF, GMEM, G7 = range(3 * L, 3 * L + 7)
        POOL_TAPS = [(i, k) for i in (1, 3) for k in range(1, TAPS)]
        DVE_TAPS = [(i, k) for i in (0, 2) for k in range(TAPS)]
        TAP_LAST = U_GATE + 2 * KC - 5
        assert U_LAYER % RING == 0 and U_GU % RING == 0 and (3 * 4) % RING == 0

        def slot(c):
            return c % RING

        def wcols(buf, c, k, n=P):
            a = slot(c) * UNIT + k * P
            return buf[:, a:a + n]

        def chunk(buf, c, lo=0, n=S):
            return buf[:, c * S + lo:c * S + lo + n]

        PAR2 = 13

        def chunk_z(i, k):
            a = i * ZW + PADZ - (TAPS - 1) + k
            return zpad[:, a:a + S]

        block = ctx.enter_context(nc.Block())

        @block.sync
        def _(sp):
            def slot_free(c, q):
                sp.wait_ge(s_split, q + (c + 1))

            def dst(c, k0, k1):
                a = slot(c) * UNIT
                return raw[:, a + k0 * P:a + k1 * P].rearrange("p (k n) -> p k n", n=P)

            def load(c, q, src):
                slot_free(c, q)
                sp.dma_start(dst(c, 0, src.shape[1]), src).then_inc(landed[slot(c)], LANDED)

            def cols(w, l, k0, k1, j0):
                v = w[ds(l, 1), k0 * P:k1 * P, ds(j0, P)]
                return v.rearrange("o (k p) n -> p (o k) n", p=P)

            def ffn(c0, q0, l, wg, wu, wd):
                with sp.Fori(0, FC // 2) as it:
                    for p in range(2):
                        for j, w in enumerate((wg, wu)):
                            load(c0 + 2 * p + j, q0 + it * 4, cols(w, l, 0, KC, it * (2 * P) + p * P))
                with sp.Fori(0, 2) as mi:
                    for m in range(4):
                        for j in range(3):
                            load(c0 + U_GU + 3 * m + j, q0 + mi * 12,
                                 cols(wd, l, 8 * j, min(8 * j + 8, FC), mi * (4 * P) + m * P))

            sp.dma_start(xin[:, :].rearrange("p (i d) -> p i d", i=TB),
                         t["x"].rearrange("o (i p) d -> p (o i) d", p=P)).then_inc(s_xin, 16)
            with sp.Fori(0, L) as l:
                q = l * U_LAYER
                ffn(0, q, l, t["ffn1_wg"], t["ffn1_wu"], t["ffn1_wd"])
                c = U_FFN
                w = t["w_in"]
                for col in (V0, K0):
                    for k in (0, 4):
                        load(c, q, cols(w, l, k, k + 4, col))
                        c += 1
                for i in range(4):
                    slot_free(c, q)
                    d = dst(c, 0, KC)
                    for g in (1, 0):
                        src = w[ds(l, 1), :, Q0 + g * 4 * HD + i * HD:Q0 + g * 4 * HD + (i + 1) * HD]
                        sp.dma_start(d[:, :, g * HD:(g + 1) * HD],
                                     src.rearrange("o (k p) n -> p (o k) n", p=P)
                                     ).then_inc(landed[slot(c)], 32)
                    c += 1
                for i in range(CC):
                    for part in range(3):
                        load(c, q, cols(w, l, 0, KC, CB0 + part * CW + i * P))
                        c += 1
                for m in range(KC):
                    slot_free(c, q)
                    d = dst(c, 0, KC)
                    wo = t["w_out"]
                    for g in range(2):
                        src = wo[ds(l, 1), g * 4 * HD:(g + 1) * 4 * HD, m * P:(m + 1) * P]
                        sp.dma_start(d[g * HD:(g + 1) * HD, 0:4, :],
                                     src.rearrange("o (k p) n -> p (o k) n", p=HD)
                                     ).then_inc(landed[slot(c)], 16)
                    sp.dma_start(d[:, 4:8, :], cols(wo, l, 4, 8, m * P)).then_inc(landed[slot(c)], 32)
                    c += 1
                ffn(c, q, l, t["ffn2_wg"], t["ffn2_wu"], t["ffn2_wd"])


            def c2(w, k0, k1, j0, n=P):
                return w[0, k0 * P:k1 * P, ds(j0, n)].rearrange("(k p) n -> p k n", p=P)

            w = t["w_in_2"]
            first = {"a": A0, "g": GT0, "q": CQ0, "kv": CKV0, "gate": GL0}
            for j, (kind, i) in enumerate(ORDER):
                c = C_IN + j
                if kind != "kr":
                    load(c, 0, c2(w, 0, KC, first[kind] + i * P))
                    continue
                slot_free(c, 0)
                d = dst(c, 0, KC)
                for a, col, n, inc in ((64, KR0, ROPE, 32), (96, KR0 + HALF, HALF, 16), (96 + HALF, KR0, HALF, 16)):
                    sp.dma_start(d[:, :, a:a + n], c2(w, 0, KC, col, n)).then_inc(landed[slot(c)], inc)
            c = C_MLA
            slot_free(c, 0)
            vw = t["w_ukv_2"][0].rearrange("(k p) (h t n) -> p k h t n", p=P, t=2, n=HD)
            a = slot(c) * UNIT
            for k in range(KVC):
                sp.dma_start(raw[:, a + k * S:a + (k + 1) * S].rearrange("p (h n) -> p h n", n=HD),
                             vw[:, k, :, 1, :]).then_inc(landed[slot(c)], 32)
            for h in range(H2):
                c = C_MLA + 1 + h
                slot_free(c, 0)
                dq, dk = dst(c, 0, QC), dst(c, QC, QC + KVC)
                wq, r0 = t["w_uq_2"], h * QK + NOPE
                for a, col, n in ((0, h * QK, QK), (QK, r0 + HALF, HALF), (QK + HALF, r0, HALF)):
                    sp.dma_start(dq[:, :, a:a + n], c2(wq, 0, QC, col, n)).then_inc(landed[slot(c)], 16)
                sp.dma_start(dk, c2(t["w_ukv_2"], 0, KVC, h * P)).then_inc(landed[slot(c)], 16)
            for m in range(KC):
                c = C_MRG + m
                slot_free(c, 0)
                for a, w in ((0, "w_conv_out_2"), (4, "w_mla_out_2")):
                    sp.dma_start(dst(c, a, a + 4), c2(t[w], 0, 4, m * P)).then_inc(landed[slot(c)], 32)
            for m in range(KC):
                load(C_OUT + m, 0, c2(t["w_out_2"], 0, KC, m * P))
                if m == 0:
                    sp.wait_ge(s_used, C_MRG + 1)
                    sp.dma_start(memr[:, :].rearrange("p (i d) -> p i d", i=MB),
                                 t["mem_2"].rearrange("o (i p) d -> p (o i) d", p=P)).then_inc(s_memin, 16)
            for h in range(H3):
                load(C_XQ + h, 0, c2(t["w_xq_2"], 0, KC, h * P))
            for h in range(H3):
                load(C_XK + h, 0, c2(t["w_xkv_2"], 0, KC, h * P))
            for j in range(KC // 2):
                c = C_XV + j
                slot_free(c, 0)
                a = slot(c) * UNIT
                sp.dma_start(raw[:, a:a + UNIT].rearrange("p (k n) -> p k n", k=2),
                             c2(t["w_xkv_2"], 2 * j, 2 * j + 2, H3 * P, H3 * P)).then_inc(landed[slot(c)], LANDED)
            for j in range(KC // 2):
                c = C_XO + j
                slot_free(c, 0)
                for i in range(2):
                    sp.dma_start(dst(c, 4 * i, 4 * i + 4), c2(t["w_xo_2"], 0, 4, (2 * j + i) * P)
                                 ).then_inc(landed[slot(c)], 32)
            for ps in range(2):
                c0 = C_MLP + ps * U_PASS
                with sp.Fori(0, FP // 4) as it:
                    for j in range(4):
                        load(c0 + j, it * 4, c2(t["w_mlp1_2"], 0, KC, it * (4 * P) + (ps * FP + j) * P))
                with sp.Fori(0, KC // 2) as mi:
                    for m in range(2):
                        for j in range(2):
                            k0 = ps * FP + 8 * j
                            load(c0 + FP + 2 * m + j, mi * 4, c2(t["w_mlp2_2"], k0, k0 + 8, mi * (2 * P) + m * P))
            for j in range(AHEAD):
                load(C_END + j, 0, c2(t["w_out_2"], 0, KC, 0))

            ov = out.rearrange("o (i p) d -> p (o i) d", p=P)
            for n in range(2 * TB):
                sp.wait_ge(s_oc, n + 1)
                sp.dma_start(ov[:, n // 2, n % 2 * 512:(n % 2 + 1) * 512], tmp[n % 2][:, :]).then_inc(s_out[n % 2], 16)
            for i in range(2):
                sp.wait_ge(s_out[i], 16 * TB)

        @block.tensor
        def _(pe):
            def unit(c, q, dest, tiles, rhs_hi, rhs_lo, start=True, stop=True, ready=None):
                pe.wait_ge(s_split, q + (c + 1 + RING))
                for k in range(tiles):
                    if ready is not None:
                        ready(k)
                    a, b_ = wcols(whi, c, k), wcols(wlo, c, k)
                    pe.matmul(dest, a, rhs_hi(k), start=start and k == 0, stop=False)
                    pe.matmul(dest, a, rhs_lo(k), start=False, stop=False)
                    mm = pe.matmul(dest, b_, rhs_hi(k), start=False, stop=stop and k == tiles - 1)
                mm.then_inc(s_used, 1)

            def norm_sum(N):
                pe.wait_ge(s_sq, N * KC + KC)
                pe.matmul(psO[:, :], ones[:, :], acc[:, :], start=True, stop=True).then_inc(s_ss, 1)

            def xk(k0=0):
                return (lambda k: chunk(xhi, k0 + k)), (lambda k: chunk(xlo, k0 + k))

            def ffn(c0, q0, N, fb):
                def pair(q, f, first):
                    for p in range(2):
                        c = c0 + 2 * p
                        if not (first and p == 0):
                            pe.wait_ge(s_gs, f + p)
                        ready = (lambda k: pe.wait_ge(s_xl, N * KC + (k + 1))) if first and p == 0 else None
                        unit(c, q, b(gate_b[p][:, :]), KC, *xk(), ready=ready)
                        if first and p == 0:
                            norm_sum(N)
                        if not (first and p == 0):
                            pe.wait_ge(s_us, f + p)
                        unit(c + 1, q, b(up_b[p][:, :]), KC, *xk())
                pair(q0, fb, True)
                with pe.Fori(1, FC // 2) as it:
                    pair(q0 + it * 4, fb + it * 2, False)
                with pe.Fori(0, 2) as mi:
                    for m in range(4):
                        pe.wait_ge(s_x, (N + 1) * KC + mi * 4 + (m - 1) if m else (N + 1) * KC + mi * 4 - 1)
                        for j in range(3):
                            tiles = min(8, FC - 8 * j)
                            pe.wait_ge(s_hl, fb + (8 * j + tiles))
                            unit(c0 + U_GU + 3 * m + j, q0 + mi * 12, down_b[m % 2], tiles,
                                 lambda k, j=j: chunk(hhi, 8 * j + k), lambda k, j=j: chunk(hlo, 8 * j + k),
                                 start=j == 0, stop=j == 2)

            def scores(l, s):
                blk, g = s // 2, s % 2
                n = P if blk == 0 else 2 * P
                k0 = max(blk - 1, 0) * P
                if s:
                    pe.wait_ge(a_bi, l * STEPS1 + s)
                for h in range(4):
                    dest = psS[:, h * 256:h * 256 + n]
                    rows = slice(g * HD, (g + 1) * HD)
                    qs = slice(h * S + blk * P, h * S + (blk + 1) * P)
                    ks = slice(k0, k0 + n)
                    pe.matmul(dest, qhi[rows, qs], khi[rows, ks], start=True, stop=False)
                    pe.matmul(dest, qhi[rows, qs], klo[rows, ks], start=False, stop=False)
                    mm = pe.matmul(dest, qlo[rows, qs], khi[rows, ks], start=False, stop=True)
                mm.then_inc(a_sc, 1)

            def turn(l, s):
                blk = s // 2
                n = 1 if blk == 0 else 2
                pe.wait_ge(a_pr, l * STEPS1 + s + 1)
                if s:
                    pe.wait_ge(a_tl, l * STEPS1 + s)
                for h in range(4):
                    for j in range(n):
                        mm = pe.transpose(psT[:, (h * n + j) * P:(h * n + j + 1) * P],
                                          sc[s % 2][:, h * 256 + j * P:h * 256 + (j + 1) * P], ident[:, :])
                mm.then_inc(a_tt, 1)

            def pv(l, s):
                blk = s // 2
                n = 1 if blk == 0 else 2
                pe.wait_ge(a_tl, l * STEPS1 + s + 1)
                if s:
                    pe.wait_ge(a_ol, l * STEPS1 + s)
                for h in range(4):
                    dest = psO[:, h * P:(h + 1) * P]
                    for j in range(n):
                        kb = blk - n + 1 + j
                        vs = slice(kb * P, (kb + 1) * P)
                        ps = slice((h * n + j) * P, (h * n + j + 1) * P)
                        pe.matmul(dest, vhi[:, vs], pthi[:, ps], start=j == 0, stop=False)
                        pe.matmul(dest, vhi[:, vs], ptlo[:, ps], start=False, stop=False)
                        mm = pe.matmul(dest, vlo[:, vs], pthi[:, ps], start=False, stop=j == n - 1)
                mm.then_inc(a_pv, 1)

            def mix(l, q, N):
                c = U_FFN
                ev = l * (6 + 3 * CC)
                for i, dest in ((0, bank[0]), (1, bank[1])):
                    for k0 in (0, 4):
                        ready = None
                        if i == 0:
                            ready = lambda k, k0=k0: pe.wait_ge(s_xl, N * KC + (k0 + k + 1))
                        unit(c, q, dest[:, :], 4, *xk(k0), start=k0 == 0, stop=k0 == 4, ready=ready)
                        c += 1
                        if i == 0 and k0 == 4:
                            norm_sum(N)
                for i in range(4):
                    if i == 1:
                        pe.wait_ge(s_vs, l + 1)
                    if i >= 2:
                        pe.wait_ge(s_qs, l * 5 + i - 1)
                    unit(c, q, bank[(2 + i) % 3][:, :], KC, *xk())
                    c += 1
                    if i == 1:
                        for j in range(TB):
                            mm = pe.transpose(psT[:, j * P:(j + 1) * P], tmp[0][:, j * P:(j + 1) * P], ident[:, :])
                        mm.then_inc(s_vt, 1)
                for u in range(3 * CC):
                    if u < 3:
                        pe.wait_ge(s_qs, l * 5 + min(3 + u, 5))
                    else:
                        pe.wait_ge(c_ev, l * 3 * CC + u - 2)
                    unit(c, q, bank[u % 3][:, :], KC, *xk())
                    c += 1
                    if 0 <= u - 3 < STEPS1:
                        pv(l, u - 3)
                    if 0 <= u - 2 < STEPS1:
                        turn(l, u - 2)
                    if u < STEPS1:
                        if u == 0:
                            pe.wait_ge(s_ql, l * 5 + 5)
                            pe.wait_ge(s_vl, l + 1)
                        scores(l, u)
                for m in range(KC):
                    if m >= 2:
                        pe.wait_ge(s_x, (N + 1) * KC + m - 1)
                    if m == 0:
                        pe.wait_ge(a_ol, l * STEPS1 + STEPS1)
                        pe.wait_ge(s_split, q + (c + 1 + RING))
                        for i, k in enumerate(range(KC)):
                            if k >= 4:
                                pe.wait_ge(c_yl, l * CC + k - 3)
                            pe.matmul(down_b[0], wcols(whi, c, k), chunk(yhi, k), start=i == 0, stop=False)
                            pe.matmul(down_b[0], wcols(whi, c, k), chunk(ylo, k), start=False, stop=False)
                            mm = pe.matmul(down_b[0], wcols(wlo, c, k), chunk(yhi, k), start=False, stop=i == KC - 1)
                        mm.then_inc(s_used, 1)
                    else:
                        unit(c, q, down_b[m % 2], KC, lambda k: chunk(yhi, k), lambda k: chunk(ylo, k))
                    c += 1
                return c

            pe.wait_ge(s_const, 3)
            pe.wait_ge(s_xin, 16)
            for c in range(KC):
                if c >= 2:
                    pe.wait_ge(s_x, c - 1)
                for i in range(TB):
                    mm = pe.transpose(down_b[c % 2][:, i * P:(i + 1) * P],
                                      xin[:, i * D + c * P:i * D + (c + 1) * P], ident[:, :])
                mm.then_inc(s_xt, 1)
            with pe.Fori(0, L) as l:
                q = l * U_LAYER
                N = l * 3
                ffn(0, q, N, l * (2 * FC))
                c = mix(l, q, N + 1)
                ffn(c, q, N + 2, l * (2 * FC) + FC)

            def ones_sum(dest, terms):
                for i, a in enumerate(terms):
                    mm = pe.matmul(dest, ones[:, :], a, start=i == 0, stop=i == len(terms) - 1)
                return mm

            for u in range(IN_UNITS):
                if u >= 3:
                    pe.wait_ge(s_i2, u - 2)
                ready = None
                if u == 0:
                    ready = lambda k: pe.wait_ge(s_xl, FINAL1 * KC + k + 1)
                unit(C_IN + u, 0, bank[u % 3][:, :], KC, *xk(), ready=ready)
                if u == 0:
                    norm_sum(FINAL1)
                if u == 1:
                    pe.wait_ge(s_q7, KC)
                    ones_sum(psS[:, 0:S], [chunk(sq7, m) for m in range(KC)]).then_inc(s_ss, 1)
                if u == 6:
                    pe.wait_ge(s_fr, 3)
                    for i in range(2):
                        mm = pe.transpose(psT[:, i:i + 1], frow[0:1, i * P:(i + 1) * P], ident[0:1, 0:1])
                    mm.then_inc(s_ft, 1)
                if u == U_GATE + 2:
                    pe.wait_ge(s_lq, QC)
                    ones_sum(psO[:, :], [chunk(gates, KC + m) for m in range(QC)]).then_inc(s_ss, 1)
                if u == U_GATE + 3:
                    pe.wait_ge(s_lq, QC + KVC)
                    ones_sum(psS[:, 512:1024], [chunk(gates, KC + QC + m) for m in range(KVC)]).then_inc(s_ss, 1)
                if u == TAP_LAST + 1:
                    pe.wait_ge(s_tap, len(DVE_TAPS))
                    pe.wait_ge(s_pa, len(POOL_TAPS))
                    ones_sum(psS[:, 0:S], [chunk(zc, i) for i in range(CC)]).then_inc(s_lsum, 1)
                if u == TAP_LAST + 3:
                    pe.wait_ge(s_lsq, CC)
                    ones_sum(psO[:, :], [tmp[2][:, :], tmp[3][:, :], acc[:, :], sqt[:, :]]).then_inc(s_ss, 1)

            pe.wait_ge(s_ll, QC + KVC)
            pe.wait_ge(s_split, C_MLA + 1 + RING)
            a = slot(C_MLA) * UNIT
            for i in range(TB):
                if i == 0:
                    pe.wait_ge(s_i2, IN_UNITS)
                if i == 3:
                    pe.wait_ge(s_v2l, 1)
                dest = bank[i % 3][:, :]
                for k in range(KVC):
                    lh, ll = chunk(lath, QC + k, i * P, P), chunk(latl, QC + k, i * P, P)
                    wh, wl = whi[:, a + k * S:a + (k + 1) * S], wlo[:, a + k * S:a + (k + 1) * S]
                    pe.matmul(dest, lh, wh, start=k == 0, stop=False)
                    pe.matmul(dest, lh, wl, start=False, stop=False)
                    mm = pe.matmul(dest, ll, wh, start=False, stop=k == KVC - 1)
                if i < TB - 1:
                    mm.then_inc(s_v2, 1)
            mm.then_inc(s_used, 1)

            def project(h):
                c = C_MLA + 1 + h
                pe.wait_ge(s_split, c + 1 + RING)
                if h == 0:
                    pe.wait_ge(s_v2l, TB)
                else:
                    pe.wait_ge(h_lo, h)
                for dest, k0, n, l0 in ((bank[0], 0, QC, 0), (bank[1], QC, KVC, QC)):
                    for k in range(n):
                        wh, wl = wcols(whi, c, k0 + k), wcols(wlo, c, k0 + k)
                        pe.matmul(dest[:, :], wh, chunk(lath, l0 + k), start=k == 0, stop=False)
                        pe.matmul(dest[:, :], wh, chunk(latl, l0 + k), start=False, stop=False)
                        mm = pe.matmul(dest[:, :], wl, chunk(lath, l0 + k), start=False, stop=k == n - 1)
                mm.then_inc(s_used, 1)

            def mla_scores(s):
                h, g = s // 2, s % 2 
                bb = h % 2 * S
                pe.wait_ge(h_lo, h + 1)
                if s == 0:
                    pe.wait_ge(s_krl, 2)
                if s:
                    pe.wait_ge(b_ex, s)
                for half, i in enumerate(BLOCKS[g]):
                    n = (i + 1) * P
                    dest = psS[:, half * 512:half * 512 + n]
                    qs, ks = slice(bb + i * P, bb + (i + 1) * P), slice(bb, bb + n)
                    pe.matmul(dest, q2h[0:QK, qs], k2h[0:QK, ks], start=True, stop=False)
                    pe.matmul(dest, q2h[0:QK, qs], k2l[0:QK, ks], start=False, stop=False)
                    mm = pe.matmul(dest, q2l[0:QK, qs], k2h[0:QK, ks], start=False, stop=True)
                mm.then_inc(b_sc, 1)

            def mla_turn(s):
                pe.wait_ge(b_pr, s + 1)
                if s:
                    pe.wait_ge(b_tl, s)
                for j in range(TB + 1):
                    mm = pe.transpose(psT[:, j * P:(j + 1) * P], p2[s % 2][:, j * P:(j + 1) * P], ident[:, :])
                mm.then_inc(b_tt, 1)

            def mla_pv(s):
                h, g = s // 2, s % 2
                pe.wait_ge(b_tl, s + 1)
                if s:
                    pe.wait_ge(b_ol, s)
                j = 0
                for half, i in enumerate(BLOCKS[g]):
                    dest = psO[:, half * P:(half + 1) * P]
                    for k in range(i + 1):
                        vs = slice(k * S + h // 2 * P, k * S + (h // 2 + 1) * P)
                        ps = slice(j * P, (j + 1) * P)
                        pe.matmul(dest, v2h[:, vs], pt2h[:, ps], start=k == 0, stop=False)
                        pe.matmul(dest, v2h[:, vs], pt2l[:, ps], start=False, stop=False)
                        mm = pe.matmul(dest, v2l[:, vs], pt2h[:, ps], start=False, stop=k == i)
                        j += 1
                mm.then_inc(b_pv, 1)

            project(0)
            for s in range(MLA_STEPS + 2):
                if s >= 2:
                    mla_pv(s - 2)
                if 1 <= s <= MLA_STEPS:
                    mla_turn(s - 1)
                if s < MLA_STEPS:
                    mla_scores(s)
                    if s % 2 == 0 and s // 2 + 1 < H2:
                        project(s // 2 + 1)

            for m in range(KC):
                c = C_MRG + m
                pe.wait_ge(s_split, c + 1 + RING)
                if m == 0:
                    pe.wait_ge(s_cl, CC)
                    pe.wait_ge(b_ol, MLA_STEPS)
                else:
                    if m >= 2:
                        pe.wait_ge(s_ga, 2 * (m - 1))
                for j, dest, rh, rl in ((0, gate_b[m % 2], chi, clo), (1, up_b[m % 2], a2h, a2l)):
                    for k in range(4):
                        wh, wl = wcols(whi, c, 4 * j + k), wcols(wlo, c, 4 * j + k)
                        pe.matmul(b(dest[:, :]), wh, chunk(rh, k), start=k == 0, stop=False)
                        pe.matmul(b(dest[:, :]), wh, chunk(rl, k), start=False, stop=False)
                        mm = pe.matmul(b(dest[:, :]), wl, chunk(rh, k), start=False, stop=k == 3)
                mm.then_inc(s_used, 1)
            for m in range(KC):
                if m >= 2:
                    pe.wait_ge(s_x, (FINAL1 + 1) * KC + m - 1)
                ready = (lambda k: pe.wait_ge(s_mgl, k + 1)) if m == 0 else None
                unit(C_OUT + m, 0, down_b[m % 2], KC, lambda k: chunk(mgh, k), lambda k: chunk(mgl, k), ready=ready)
                if m in (2, 5):
                    r = m // 5
                    pe.wait_ge(s_mn, MB)
                    if r:
                        pe.wait_ge(s_ml, 4)
                    for i in range(4):
                        for j in range(MB):
                            cc = 4 * r + i
                            mm = pe.transpose(psS[:, i * ML + j * P:i * ML + (j + 1) * P],
                                              memr[:, j * D + cc * P:j * D + (cc + 1) * P], ident[:, :])
                    mm.then_inc(s_mt, 1)

            for j in range(H3):
                if j >= 3:
                    pe.wait_ge(s_x2, j - 2)
                ready = (lambda k: pe.wait_ge(s_xl, (FINAL1 + 1) * KC + k + 1)) if j == 0 else None
                unit(C_XQ + j, 0, bank[j % 3][:, :], KC, lambda k: chunk(xbh, k), lambda k: chunk(xbl, k), ready=ready)
                if j == 0:
                    pe.wait_ge(s_sq, (FINAL1 + 2) * KC)
                    pe.matmul(psO[:, :], ones[:, :], acc[:, :], start=True, stop=True).then_inc(s_ss, 1)
            pe.wait_ge(s_ml, KC)
            for j in range(H3):
                if j < 3:
                    pe.wait_ge(s_x2, 2 + j)
                else:
                    pe.wait_ge(s_k3l, j - 2)
                unit(C_XK + j, 0, bank[(H3 + j) % 3][:, 0:ML], KC,
                     lambda k: mth[:, k * ML:(k + 1) * ML], lambda k: mtl[:, k * ML:(k + 1) * ML])

            def cross_scores(s):
                if s:
                    pe.wait_ge(d_ex, s)
                else:
                    pe.wait_ge(s_k3l, H3)
                    pe.wait_ge(s_x2l, H3)
                for h in range(H3):
                    dest = psS[:, h * ML:(h + 1) * ML]
                    qs, ks = slice(h * S + s * P, h * S + (s + 1) * P), slice(h * ML, (h + 1) * ML)
                    pe.matmul(dest, q3h[:, qs], k3h[:, ks], start=True, stop=False)
                    pe.matmul(dest, q3h[:, qs], k3l[:, ks], start=False, stop=False)
                    mm = pe.matmul(dest, q3l[:, qs], k3h[:, ks], start=False, stop=True)
                mm.then_inc(d_sc, 1)

            def cross_v(j):
                c = C_XV + j
                pe.wait_ge(s_split, c + 1 + RING)
                a = slot(c) * UNIT
                for i in range(MB):
                    for k in range(2):
                        kk = 2 * j + k
                        ms = slice(kk * ML + i * P, kk * ML + (i + 1) * P)
                        ws = slice(a + k * S, a + (k + 1) * S)
                        dest = bank[2 * (1 - i)][:, :]
                        pe.matmul(dest, mth[:, ms], whi[:, ws], start=kk == 0, stop=False)
                        pe.matmul(dest, mth[:, ms], wlo[:, ws], start=False, stop=False)
                        mm = pe.matmul(dest, mtl[:, ms], whi[:, ws], start=False, stop=kk == KC - 1)
                mm.then_inc(s_used, 1)

            def cross_turn(s):
                pe.wait_ge(d_pr, s + 1)
                for j in range(8):
                    mm = pe.transpose(psT[:, j * P:(j + 1) * P], p3[s % 2][:, j * P:(j + 1) * P], ident[:, :])
                mm.then_inc(d_tt, 1)

            def cross_pv(s):
                pe.wait_ge(d_tl, s + 1)
                if s:
                    pe.wait_ge(d_ol, s)
                else:
                    pe.wait_ge(s_v3l, MB)
                for h in range(H3):
                    dest = psO[:, h * P:(h + 1) * P]
                    for j in range(MB):
                        vs = slice(j * S + h * P, j * S + (h + 1) * P)
                        ps = slice((h * MB + j) * P, (h * MB + j + 1) * P)
                        pe.matmul(dest, v3h[:, vs], pt3h[:, ps], start=j == 0, stop=False)
                        pe.matmul(dest, v3h[:, vs], pt3l[:, ps], start=False, stop=False)
                        mm = pe.matmul(dest, v3l[:, vs], pt3h[:, ps], start=False, stop=j == MB - 1)
                mm.then_inc(d_pv, 1)

            cross_scores(0)
            cross_v(0)
            cross_scores(1)
            cross_v(1)
            cross_v(2)
            cross_turn(0)
            cross_v(3)
            cross_scores(2)
            cross_pv(0)
            cross_turn(1)
            cross_scores(3)
            cross_pv(1)
            cross_turn(2)
            cross_pv(2)
            cross_turn(3)
            cross_pv(3)
            pe.wait_ge(d_ol, TB)
            for j in range(KC // 2):
                c = C_XO + j
                pe.wait_ge(s_split, c + 1 + RING)
                for i in range(2):
                    if j:
                        pe.wait_ge(s_x, (FINAL1 + 2) * KC + 2 * j + i - 1)
                    for k in range(4):
                        wh, wl = wcols(whi, c, 4 * i + k), wcols(wlo, c, 4 * i + k)
                        pe.matmul(down_b[i], wh, chunk(a3h, k), start=k == 0, stop=False)
                        pe.matmul(down_b[i], wh, chunk(a3l, k), start=False, stop=False)
                        mm = pe.matmul(down_b[i], wl, chunk(a3h, k), start=False, stop=k == 3)
                mm.then_inc(s_used, 1)

            mlp_b = [bank[0][:, :], bank[1][:, :], bank[2][:, :], psS[:, 0:S]]
            for ps in range(2):
                c0 = C_MLP + ps * U_PASS

                def four(c, q, f, first):
                    for j in range(4):
                        if not first or j >= 2:
                            pe.wait_ge(m_r, f + (j - 1))
                        ready = None
                        if first and ps == 0 and j == 0:
                            ready = lambda k: pe.wait_ge(s_xl, (FINAL1 + 2) * KC + k + 1)
                        unit(c + j, q, mlp_b[j], KC, *xk(), ready=ready)
                        if first and ps == 0 and j == 0:
                            pe.wait_ge(s_sq, (FINAL1 + 3) * KC)
                            pe.matmul(psO[:, :], ones[:, :], acc[:, :], start=True, stop=True).then_inc(s_ss, 1)
                four(c0, 0, ps * FP, True)
                with pe.Fori(1, FP // 4) as it:
                    four(c0, it * 4, it * 4 + ps * FP, False)
                with pe.Fori(0, KC // 2) as mi:
                    for m in range(2):
                        pe.wait_ge(s_x, mi * 2 + ((FINAL1 + 3 + ps) * KC + m - 1))
                        for j in range(2):
                            pe.wait_ge(m_lo, ps * FP + 8 * j + 8)
                            unit(c0 + FP + 2 * m + j, mi * 4, down_b[m], 8,
                                 lambda k, j=j: chunk(mhi, 8 * j + k), lambda k, j=j: chunk(mlo, 8 * j + k),
                                 start=j == 0, stop=j == 1)
            pe.wait_ge(s_sq, (FINAL1 + 4) * KC)
            pe.matmul(psO[:, :], ones[:, :], acc[:, :], start=True, stop=True).then_inc(s_ss, 1)
            pe.wait_ge(s_o, KC)
            for i in range(TB):
                for hf in range(2):
                    n = 2 * i + hf
                    if n >= 2:
                        pe.wait_ge(s_oc, n - 1)
                    for c in range(4):
                        mm = pe.transpose(down_b[hf][:, c * P:(c + 1) * P],
                                          x[:, (4 * hf + c) * S + i * P:(4 * hf + c) * S + (i + 1) * P], ident[:, :])
                    mm.then_inc(s_ot, 1)

        @block.scalar
        def _(act):
            def split(c, q):
                act.wait_ge(landed[slot(c)], q * (LANDED // RING) + LANDED * (c // RING + 1))
                if c >= RING:
                    act.wait_ge(s_used, q + (c - RING + 1))
                a = slot(c) * UNIT
                act.activation(whi[:, a:a + UNIT], raw[:, a:a + UNIT], ACT.Copy).then_inc(s_hi, 1)

            def root(N, dest=inv):
                act.wait_ge(s_var, N + 1)
                act.activation(dest[:, :], var[:, :], ACT.Sqrt).then_inc(s_rt, 1)

            def x_hi(N, m, dest=xhi):
                act.wait_ge(s_x, N * KC + m + 1)
                act.activation(dest[:, ds(m * S, S)], x[:, ds(m * S, S)], ACT.Copy,
                               scale=gains[:, ds(N * KC + m, 1)]).then_inc(s_xh, 1)

            def ffn(c0, q0, N, fb, next_x):
                def pair(q, f, fi, first):
                    for p in range(2):
                        c = c0 + 2 * p
                        split(c + AHEAD, q)
                        if first and p == 0:
                            root(N)
                        act.wait_ge(s_gs, f + p + 1)
                        act.activation(tmp[p][:, :], tmp[p][:, :], ACT.Silu).then_inc(s_si, 1)
                        split(c + 1 + AHEAD, q)
                        act.wait_ge(s_h, f + p + 1)
                        act.activation(hhi[:, ds((fi + p) * S, S)], tmp[2 + p][:, :], ACT.Copy).then_inc(s_hh, 1)
                pair(q0, fb, 0, True)
                with act.Fori(1, FC // 2) as it:
                    pair(q0 + it * 4, fb + it * 2, it * 2, False)
                with act.Fori(0, 2) as mi:
                    for m in range(4):
                        for j in range(3):
                            split(c0 + U_GU + 3 * m + j + AHEAD, q0 + mi * 12)
                        if next_x:
                            x_hi(N + 1, mi * 4 + m)

            def mix(l, q, N):
                c = U_FFN
                split(c + AHEAD, q)
                split(c + 1 + AHEAD, q)
                root(N)
                c += 2
                for i in range(5):
                    for _ in range(2 if i == 0 else 1):
                        split(c + AHEAD, q)
                        c += 1
                    if i == 2:
                        act.wait_ge(s_vt, l + 1)
                        act.activation(vhi[:, :], psT[:, 0:S], ACT.Copy).then_inc(s_vh, 1)
                    act.wait_ge(s_qs, l * 5 + i + 1)
                    dest = khi[:, :] if i == 0 else chunk(qhi, i - 1)
                    act.activation(dest, tmp[1 + i % 2][:, :], ACT.Copy).then_inc(s_qh, 1)
                for u in range(3 * CC + 1):
                    if u < 3 * CC:
                        split(c + AHEAD, q)
                        c += 1
                    if 0 <= u - 3 < STEPS1:
                        s = u - 3
                        blk, g = s // 2, s % 2
                        act.wait_ge(a_pv, l * STEPS1 + s + 1)
                        rows = slice(g * HD, (g + 1) * HD)
                        act.activation(yhi[rows, 0:4 * S].rearrange("p (c n) -> p c n", c=4)[:, :, blk * P:(blk + 1) * P],
                                       psO[rows, :].rearrange("p (c n) -> p c n", c=4), ACT.Copy).then_inc(a_oh, 1)
                    if 0 <= u - 2 < STEPS1:
                        s = u - 2
                        n = 512 if s < 2 else 1024
                        act.wait_ge(a_tt, l * STEPS1 + s + 1)
                        act.activation(pthi[:, 0:n], psT[:, 0:n], ACT.Copy).then_inc(a_th, 1)
                    if u < STEPS1:
                        n = P if u < 2 else 2 * P
                        act.wait_ge(a_sd, l * STEPS1 + u + 1)
                        for h in range(4):
                            a = sc[u % 2][:, h * 256:h * 256 + n]
                            act.activation(a, a, ACT.Exp, bias=st[:, 4 + h:5 + h], accum_out=st[:, 12 + h:13 + h])
                        act.activation(st[:, 16:20], st[:, 8:12], ACT.Exp).then_inc(a_ex, 1)
                    if u % 3 == 0 and u >= 3:
                        i = u // 3 - 1
                        act.wait_ge(c_u, l * CC + i + 1)
                        act.activation(cy[i % 2][:, :], upad[i % 2][:, 2:2 + S], ACT.Copy,
                                       scale=cw1[:, ds(l * (3 * CC) + 2 * CC + i, 1)]).then_inc(c_t2, 1)
                        act.wait_ge(c_y, l * CC + i + 1)
                        act.activation(chunk(yhi, 4 + i), cy[i % 2][:, :], ACT.Copy).then_inc(c_yh, 1)
                for m in range(KC):
                    split(c + AHEAD, q)
                    c += 1
                    x_hi(N + 1, m)
                return c

            with nc.allow_non_contiguous_dma(reason="small vectors, one value per partition"):
                gv = gains[:, 0:6 * KC].rearrange("p (l j c) -> p l j c", l=L, j=3)
                for j, name in enumerate(("ffn1_norm", "mix_norm", "ffn2_norm")):
                    for l in range(L):
                        act.dma_start(gv[:, l, j, :], t[name][l, :].rearrange("(c p) -> p c", p=P)).then_inc(s_par, 16)
                act.dma_start(cw1[:, :], t["conv_w"].rearrange("l t (c p) -> p (l t c)", p=P)).then_inc(s_par, 16)
                act.dma_start(sink[:, :], t["attn_sink"].rearrange("l h -> (l h)").partition_broadcast(P)).then_inc(s_par, 16)
                col = lambda v: v.rearrange("(c p) -> p c", p=P)
                gc = lambda j: gains[:, j * KC:(j + 1) * KC]
                for dest, v in ((gc(G6), t["final_norm"]), (gc(G7), t["norm_mix_g_2"][0]), (gc(GX), t["norm_xattn_g_2"][0]),
                                (gc(GM), t["norm_mlp_g_2"][0]), (gc(GF), t["final_norm_g_2"]), (gc(GMEM), t["norm_mem_g_2"][0]),
                                (cvec[:, 0:CC], t["conv_b_2"][0]), (cvec[:, CC:2 * CC], t["conv_ln_g_2"][0]),
                                (cvec[:, 2 * CC:3 * CC], t["conv_ln_b_2"][0]), (lgain[:, 0:QC], t["q_norm_g_2"][0]),
                                (lgain[:, QC:QC + KVC], t["kv_norm_g_2"][0])):
                    act.dma_start(dest, col(v)).then_inc(s_par2, 16)
                act.dma_start(cw2[:, :], t["conv_w_2"][0].rearrange("t (c p) -> p (t c)", p=P)).then_inc(s_par2, 16)
                act.dma_start(pos[:, :], t["positions_2"][0].partition_broadcast(P)).then_inc(s_par2, 16)
            for c in range(AHEAD):
                act.wait_ge(landed[c], LANDED)
                a = c * UNIT
                act.activation(whi[:, a:a + UNIT], raw[:, a:a + UNIT], ACT.Copy).then_inc(s_hi, 1)
            act.wait_ge(s_par, 16 * 8)
            with act.Fori(0, L) as l:
                q = l * U_LAYER
                N = l * 3
                for m in range(KC):
                    x_hi(N, m)
                ffn(0, q, N, l * (2 * FC), True)
                c = mix(l, q, N + 1)
                ffn(c, q, N + 2, l * (2 * FC) + FC, False)

            act.wait_ge(s_par2, 16 * PAR2)
            act.wait_ge(s_g67, 1)
            for m in range(KC):
                x_hi(FINAL1, m)
            for m in range(KC):
                act.activation(chunk(sq7, m), chunk(x, m), ACT.Square,
                               scale=gains[:, G6 * KC + m:G6 * KC + m + 1]).then_inc(s_q7, 1)
            taps = [(i, k) for i in (1, 3) for k in range(TAPS)]
            done = adds = 0
            for u, (kind, i) in enumerate(ORDER):
                if u == 0:
                    split(C_IN + AHEAD, 0)
                    split(C_IN + 1 + AHEAD, 0)
                    root(FINAL1, inv6)
                    root(SUM7)
                if u >= 2:
                    split(C_IN + u + AHEAD, 0)
                if kind in ("g", "q", "kv", "gate"):
                    act.wait_ge(s_i2, u + 1)
                if kind == "g":
                    g = tmp[2 + i % 2][:, :]
                    act.activation(g, g, ACT.Tanh, scale=0.5).then_inc(s_th, 1)
                if kind in ("q", "kv"):
                    j = i + (QC if kind == "kv" else 0)
                    act.activation(chunk(gates, KC + j), chunk(latf, j), ACT.Square).then_inc(s_lq, 1)
                if kind == "gate":
                    act.activation(chunk(gates, i), chunk(gates, i), ACT.Tanh, scale=0.5).then_inc(s_gt, 1)
                if u == 10:
                    act.wait_ge(s_rr, 1)
                    for r in (64, 96):
                        act.activation(rope[r:r + 32, :], rope[r:r + 32, :], ACT.Sin).then_inc(s_rs, 1)
                if u == U_GATE + 3:
                    root(LATQ, tmp[2])
                if u == U_GATE + 4:
                    root(LATKV, tmp[3])
                    for j in range(QC + KVC):
                        act.wait_ge(s_ln, j + 1)
                        act.activation(chunk(lath, j), chunk(latf, j), ACT.Copy).then_inc(s_lh, 1)
                if 4 <= u <= TAP_LAST:
                    left = TAP_LAST + 1 - u
                    for _ in range(-(-(len(taps) - done) // left)):
                        ci, k = taps[done]
                        if k == 0:
                            act.wait_ge(s_z, ci + 1)
                            act.wait_ge(s_zp, 1)
                        z = chunk_z(ci, k)
                        wk = cw2[:, k * CC + ci:k * CC + ci + 1]
                        if k == 0:
                            act.activation(chunk(zc, ci), z, ACT.Identity, bias=cvec[:, ci:ci + 1], scale=wk).then_inc(s_pm, 1)
                        else:
                            if adds >= 2:
                                act.wait_ge(s_pa, adds - 1)
                            prod = (acc, sqt)[adds % 2]
                            act.activation(prod[:, :], z, ACT.Copy, scale=wk).then_inc(s_pm, 1)
                            adds += 1
                        done += 1
                if u == TAP_LAST + 2:
                    for j, d in enumerate((tmp[2], tmp[3], acc, sqt)):
                        act.wait_ge(s_ld, j + 1)
                        act.activation(d[:, :], chunk(zc, j), ACT.Square).then_inc(s_lsq, 1)
            root(LNVAR, tmp[1])
            for i in range(CC + 1):
                if i < CC:
                    z = chunk(zc, i)
                    act.wait_ge(s_ly, i + 1)
                    act.activation(z, z, ACT.Identity, bias=cvec[:, 2 * CC + i:2 * CC + i + 1],
                                   scale=cvec[:, CC + i:CC + i + 1]).then_inc(s_la, 1)
                    act.wait_ge(s_la, i + 1)
                    if i >= 2:
                        act.wait_ge(s_lc, i - 1)
                    act.activation(tmp[2 + i % 2][:, :], z, ACT.Tanh, scale=0.5).then_inc(s_lt, 1)
                if i >= 1:
                    act.wait_ge(s_lc, i)
                    act.activation(chunk(chi, i - 1), chunk(zc, i - 1), ACT.Copy, scale=0.5).then_inc(s_ch, 1)

            act.wait_ge(s_kr, 3)
            for j in range(2):
                act.activation(k2h[NOPE:QK, j * S:(j + 1) * S], tmp[0][NOPE:QK, :], ACT.Copy).then_inc(s_krh, 1)
            split(C_MLA + AHEAD, 0)
            for i in range(TB):
                if i < TB - 1:
                    act.wait_ge(s_v2, i + 1)
                else:
                    act.wait_ge(s_used, C_MLA + 1)
                act.activation(chunk(v2h, i), bank[i % 3][:, :], ACT.Copy).then_inc(s_v2h, 1)

            def head(h):
                bb = h % 2 * S
                split(C_MLA + 1 + h + AHEAD, 0)
                act.wait_ge(s_used, C_MLA + 2 + h)
                act.activation(tmp[0][0:NOPE, :], bank[0][0:NOPE, :], ACT.Copy).then_inc(h_cp, 1)
                act.activation(k2h[0:NOPE, bb:bb + S], bank[1][0:NOPE, :], ACT.Copy).then_inc(h_hi, 1)
                act.wait_ge(h_rp, 3 * h + 3)
                act.wait_ge(h_cp, h + 1)
                act.activation(q2h[0:QK, bb:bb + S], tmp[0][0:QK, :], ACT.Copy, scale=QK ** -0.5).then_inc(h_hi, 1)

            head(0)
            for s in range(MLA_STEPS + 2):
                if s >= 2:
                    r = s - 2
                    h, (i1, i2) = r // 2, BLOCKS[r % 2]
                    rows = slice(h % 2 * HD, h % 2 * HD + HD)
                    act.wait_ge(b_pv, r + 1)
                    act.activation(chunk(a2h, h // 2)[rows].rearrange("p (i n) -> p i n", n=P)[:, i1:i2 + 1:i2 - i1, :],
                                   psO[rows, 0:2 * P].rearrange("p (i n) -> p i n", n=P), ACT.Copy).then_inc(b_oh, 1)
                if 1 <= s <= MLA_STEPS:
                    act.wait_ge(b_tt, s)
                    act.activation(pt2h[:, :], psT[:, 0:(TB + 1) * P], ACT.Copy).then_inc(b_th, 1)
                if s < MLA_STEPS:
                    o, pc = 0, s % 2 * 8
                    act.wait_ge(b_mx, s + 1)
                    for half, i in enumerate(BLOCKS[s % 2]):
                        n = (i + 1) * P
                        e = act.activation(p2[s % 2][:, o:o + n], psS[:, half * 512:half * 512 + n], ACT.Exp,
                                           bias=st2[:, pc + half:pc + half + 1], accum_out=st2[:, pc + 2 + half:pc + 3 + half])
                        o += n
                    e.then_inc(b_ex, 1)
                    if s % 2 == 0 and s // 2 + 1 < H2:
                        head(s // 2 + 1)

            for m in range(KC):
                split(C_MRG + m + AHEAD, 0)
                act.wait_ge(s_mg, m + 1)
                act.activation(chunk(mgh, m), tmp[2 + m % 2][:, :], ACT.Copy, scale=0.5).then_inc(s_mgh, 1)
            for m in range(KC):
                split(C_OUT + m + AHEAD, 0)
                if m == 1:
                    act.wait_ge(s_memin, 16)
                    for i in range(MB):
                        e = act.activation(mscr[:, i * D:(i + 1) * D], memr[:, i * D:(i + 1) * D], ACT.Square,
                                           accum_out=st2[:, 16 + i:17 + i])
                    e.then_inc(s_msq, 1)
                    act.wait_ge(s_mv, 1)
                    act.activation(st2[:, 20:22], st2[:, 18:20], ACT.Sqrt).then_inc(s_mr, 1)
                if m in (3, 6):
                    r = m // 6
                    act.wait_ge(s_mt, r + 1)
                    for i in range(4):
                        cc = 4 * r + i
                        act.activation(mth[:, cc * ML:(cc + 1) * ML], psS[:, i * ML:(i + 1) * ML], ACT.Copy,
                                       scale=gains[:, GMEM * KC + cc:GMEM * KC + cc + 1]).then_inc(s_mh, 1)
                x_hi(FINAL1 + 1, m, xbh)

            for j in range(H3):
                split(C_XQ + j + AHEAD, 0)
                if j == 0:
                    root(XATTN)
                act.wait_ge(s_x2, j + 1)
                act.activation(chunk(q3h, j), tmp[j % 2][:, :], ACT.Copy).then_inc(s_x2h, 1)
            for j in range(H3):
                split(C_XK + j + AHEAD, 0)
                act.wait_ge(s_used, C_XK + j + 1)
                act.activation(k3h[:, j * ML:(j + 1) * ML], bank[(H3 + j) % 3][:, 0:ML], ACT.Copy).then_inc(s_k3h, 1)

            def cross_exp(s):
                pc = s % 2 * 16
                act.wait_ge(d_mx, s + 1)
                for h in range(H3):
                    hs = slice(h * ML, (h + 1) * ML)
                    e = act.activation(p3[s % 2][:, hs], psS[:, hs], ACT.Exp, bias=st[:, pc + h:pc + h + 1],
                                       accum_out=st[:, pc + 4 + h:pc + 5 + h])
                e.then_inc(d_ex, 1)

            def cross_hi(s):
                act.wait_ge(d_tt, s + 1)
                act.activation(pt3h[:, :], psT[:, :], ACT.Copy).then_inc(d_th, 1)

            def cross_out(s):
                act.wait_ge(d_pv, s + 1)
                act.activation(a3h[:, :].rearrange("p (h n) -> p h n", h=H3)[:, :, s * P:(s + 1) * P],
                               psO[:, :].rearrange("p (h n) -> p h n", h=H3), ACT.Copy).then_inc(d_oh, 1)

            cross_exp(0)
            split(C_XV + AHEAD, 0)
            cross_exp(1)
            split(C_XV + 1 + AHEAD, 0)
            split(C_XV + 2 + AHEAD, 0)
            cross_hi(0)
            split(C_XV + 3 + AHEAD, 0)
            act.wait_ge(s_used, C_XV + KC // 2)
            for i in range(MB):
                act.activation(chunk(v3h, i), bank[2 * (1 - i)][:, :], ACT.Copy).then_inc(s_v3h, 1)
            cross_exp(2)
            cross_out(0)
            cross_hi(1)
            cross_exp(3)
            cross_out(1)
            cross_hi(2)
            cross_out(2)
            cross_hi(3)
            cross_out(3)
            for j in range(KC // 2):
                split(C_XO + j + AHEAD, 0)
                for i in range(2):
                    x_hi(FINAL1 + 2, 2 * j + i)

            for ps in range(2):
                c0 = C_MLP + ps * U_PASS

                def four(c, q, fi, first):
                    for j in range(4):
                        split(c + j + AHEAD, q)
                        if first and ps == 0 and j == 0:
                            root(MLPN)
                        f = fi + (ps * FP + j)
                        act.wait_ge(m_r, f + 1)
                        act.activation(tmp[2 + j % 2][:, :], tmp[j % 2][:, :], ACT.Square).then_inc(m_sq, 1)
                        act.wait_ge(m_sq, f + 1)
                        act.activation(mhi[:, ds((fi + j) * S, S)], tmp[2 + j % 2][:, :], ACT.Copy).then_inc(m_hi, 1)
                four(c0, 0, 0, True)
                with act.Fori(1, FP // 4) as it:
                    four(c0, it * 4, it * 4, False)
                with act.Fori(0, KC // 2) as mi:
                    for j in range(4):
                        split(c0 + FP + j + AHEAD, mi * 4)
            root(FINAL2)

        @block.vector
        def _(dve):
            def split(c, q):
                dve.wait_ge(s_hi, q + c + 1)
                a = slot(c) * UNIT
                dve.tensor_tensor(wlo[:, a:a + UNIT], raw[:, a:a + UNIT], whi[:, a:a + UNIT].bitcast(F32),
                                  ALU.subtract).then_inc(s_split, 1)

            def inverse(N, total=None, n=D, dest=inv):
                dve.wait_ge(s_ss, N + 1)
                dve.tensor_scalar(var[:, :], psO[:, :] if total is None else total, 1.0 / n, EPS,
                                  ALU.mult, ALU.add).then_inc(s_var, 1)
                newton(N, dest)

            def newton(N, dest):
                dve.wait_ge(s_rt, N + 1)
                dve.reciprocal(dest[:, :], dest[:, :]).then_inc(s_nst, 1)
                dve.wait_ge(s_nst, N * 4 + 1)
                dve.tensor_tensor(var[:, :], var[:, :], dest[:, :], ALU.mult).then_inc(s_nst, 1)
                dve.wait_ge(s_nst, N * 4 + 2)
                dve.tensor_tensor(var[:, :], var[:, :], dest[:, :], ALU.mult).then_inc(s_nst, 1)
                dve.wait_ge(s_nst, N * 4 + 3)
                dve.tensor_scalar(var[:, :], var[:, :], -0.5, 1.5, ALU.mult, ALU.add).then_inc(s_nst, 1)
                dve.wait_ge(s_nst, N * 4 + 4)
                dve.tensor_tensor(dest[:, :], var[:, :], dest[:, :], ALU.mult).then_inc(s_inv, 1)
                dve.wait_ge(s_inv, N + 1)

            def x_lo(N, m, lo=xlo, hi=xhi):
                dve.wait_ge(s_xh, N * KC + m + 1)
                dve.scalar_tensor_tensor(lo[:, ds(m * S, S)], x[:, ds(m * S, S)], gains[:, ds(N * KC + m, 1)],
                                         hi[:, ds(m * S, S)].bitcast(F32), ALU.mult, ALU.subtract).then_inc(s_xl, 1)

            def ffn(c0, q0, N, fb, next_x):
                def pair(q, f, fi, first):
                    for p in range(2):
                        c = c0 + 2 * p
                        split(c + AHEAD, q)
                        if first and p == 0:
                            inverse(N)
                        dve.wait_ge(s_used, q + c + 1)
                        dve.tensor_tensor(tmp[p][:, :], b(gate_b[p][:, :]), inv[:, :], ALU.mult).then_inc(s_gs, 1)
                        split(c + 1 + AHEAD, q)
                        dve.wait_ge(s_used, q + c + 2)
                        dve.tensor_tensor(tmp[2 + p][:, :], b(up_b[p][:, :]), inv[:, :], ALU.mult).then_inc(s_us, 1)
                        dve.wait_ge(s_us, f + p + 1)
                        dve.wait_ge(s_si, f + p + 1)
                        dve.tensor_tensor(tmp[2 + p][:, :], tmp[2 + p][:, :], tmp[p][:, :], ALU.mult).then_inc(s_h, 1)
                        dve.wait_ge(s_hh, f + p + 1)
                        dve.tensor_tensor(hlo[:, ds((fi + p) * S, S)], tmp[2 + p][:, :],
                                          hhi[:, ds((fi + p) * S, S)].bitcast(F32), ALU.subtract).then_inc(s_hl, 1)
                pair(q0, fb, 0, True)
                with dve.Fori(1, FC // 2) as it:
                    pair(q0 + it * 4, fb + it * 2, it * 2, False)
                with dve.Fori(0, 2) as mi:
                    for m in range(4):
                        for j in range(3):
                            split(c0 + U_GU + 3 * m + j + AHEAD, q0 + mi * 12)
                        dve.wait_ge(s_used, q0 + mi * 12 + (c0 + U_GU + 3 * m + 3))
                        xm = x[:, ds((mi * 4 + m) * S, S)]
                        dve.scalar_tensor_tensor(xm, down_b[m % 2], 0.5, xm, ALU.mult, ALU.add).then_inc(s_x, 1)
                        if next_x:
                            x_lo(N + 1, mi * 4 + m)

            def mix(l, q, N):
                c = U_FFN
                split(c + AHEAD, q)
                split(c + 1 + AHEAD, q)
                inverse(N)
                dve.wait_ge(s_used, q + c + 2)
                dve.tensor_tensor(tmp[0][:, :], bank[0][:, :], inv[:, :], ALU.mult).then_inc(s_vs, 1)
                c += 2
                for i in range(5):
                    for _ in range(2 if i == 0 else 1):
                        split(c + AHEAD, q)
                        c += 1
                    dve.wait_ge(s_used, q + c)
                    dve.scalar_tensor_tensor(tmp[1 + i % 2][:, :], bank[(1 + i) % 3][:, :], HD ** -0.5 if i else 1.0,
                                             inv[:, :], ALU.mult, ALU.mult).then_inc(s_qs, 1)
                    if i == 2:
                        dve.wait_ge(s_vh, l + 1)
                        dve.tensor_tensor(vlo[:, :], psT[:, 0:S], vhi[:, :].bitcast(F32), ALU.subtract).then_inc(s_vl, 1)
                    dve.wait_ge(s_qh, l * 5 + i + 1)
                    hi = khi[:, :] if i == 0 else chunk(qhi, i - 1)
                    lo = klo[:, :] if i == 0 else chunk(qlo, i - 1)
                    dve.tensor_tensor(lo, tmp[1 + i % 2][:, :], hi.bitcast(F32), ALU.subtract).then_inc(s_ql, 1)
                for i in range(2):
                    last = dve.memset(upad[i][:, 0:2], 0.0)
                last.then_inc(s_pad, 1)
                for u in range(3 * CC + 1):
                    if u < 3 * CC:
                        split(c + AHEAD, q)
                    if 1 <= u and u - 1 < STEPS1:
                        s = l * STEPS1 + (u - 1)
                        dve.wait_ge(a_ex, s + 1)
                        dve.tensor_tensor(st[:, 20:24], st[:, 12:16], st[:, 16:20], ALU.add).then_inc(a_dn, 1)
                        dve.wait_ge(a_dn, s + 1)
                        r = 24 + 4 * ((u - 1) % 2)
                        dve.reciprocal(st[:, r:r + 4], st[:, 20:24]).then_inc(a_rd, 1)
                    if u < 3 * CC:
                        dve.wait_ge(s_used, q + c + 1)
                        c += 1
                        if u % 3 == 0 and u >= 6:
                            dve.wait_ge(c_y, l * CC + u // 3 - 1)
                        dest = tmp[(0, 1)[u // 3 % 2] if u % 3 == 0 else 1 + u % 3]
                        if u % 3 and u >= 3:
                            dve.wait_ge(c_u, l * CC + u // 3)
                        dve.tensor_tensor(dest[:, :], bank[u % 3][:, :], inv[:, :], ALU.mult).then_inc(c_ev, 1)
                    if 0 <= u - 3 < STEPS1:
                        s = u - 3
                        blk, g = s // 2, s % 2
                        dve.wait_ge(a_oh, l * STEPS1 + s + 1)
                        rows = slice(g * HD, (g + 1) * HD)
                        ys = slice(blk * P, (blk + 1) * P)
                        dve.tensor_tensor(ylo[rows, 0:4 * S].rearrange("p (c n) -> p c n", c=4)[:, :, ys],
                                          psO[rows, :].rearrange("p (c n) -> p c n", c=4),
                                          yhi[rows, 0:4 * S].bitcast(F32).rearrange("p (c n) -> p c n", c=4)[:, :, ys],
                                          ALU.subtract).then_inc(a_ol, 1)
                    if 0 <= u - 2 < STEPS1:
                        s = u - 2
                        n = 512 if s < 2 else 1024
                        dve.wait_ge(a_th, l * STEPS1 + s + 1)
                        dve.tensor_tensor(ptlo[:, 0:n], psT[:, 0:n], pthi[:, 0:n].bitcast(F32),
                                          ALU.subtract).then_inc(a_tl, 1)
                    if u < STEPS1:
                        s = l * STEPS1 + u
                        g = u % 2
                        n = P if u < 2 else 2 * P
                        dve.wait_ge(a_sc, s + 1)
                        for h in range(4):
                            slope = 2.0 ** (-8.0 * (g * 4 + h + 1) / H1)
                            a = sc[u % 2][:, h * 256:h * 256 + n]
                            last = dve.scalar_tensor_tensor(a, dist[:, 2 * P - n:2 * P], -slope, psS[:, h * 256:h * 256 + n],
                                                            ALU.mult, ALU.add)
                        last.then_inc(a_bi, 1)
                        dve.wait_ge(a_bi, s + 1)
                        dve.tensor_reduce(st[:, 0:4], sc[u % 2][:, :].rearrange("p (h n) -> p h n", h=4)[:, :, 0:n],
                                          AX.X, ALU.max, negate=True).then_inc(a_rm, 1)
                        dve.wait_ge(a_rm, s + 1)
                        ns = nsink[:, ds(l * H1 + g * 4, 4)]
                        dve.tensor_tensor(st[:, 4:8], st[:, 0:4], ns, ALU.min).then_inc(a_mx, 1)
                        dve.wait_ge(a_mx, s + 1)
                        dve.tensor_tensor(st[:, 8:12], st[:, 4:8], ns, ALU.subtract).then_inc(a_sd, 1)
                    if u % 3 == 0 and u >= 3:
                        i = u // 3 - 1
                        y = cy[i % 2][:, :]
                        dve.wait_ge(c_t2, l * CC + i + 1)
                        dve.scalar_tensor_tensor(y, upad[i % 2][:, 1:1 + S], cw1[:, ds(l * (3 * CC) + CC + i, 1)], y,
                                                 ALU.mult, ALU.add).then_inc(c_t1, 1)
                        dve.wait_ge(c_t1, l * CC + i + 1)
                        dve.scalar_tensor_tensor(y, upad[i % 2][:, 0:S], cw1[:, ds(l * (3 * CC) + i, 1)], y,
                                                 ALU.mult, ALU.add).then_inc(c_t0, 1)
                        dve.wait_ge(c_yh, l * CC + i + 1)
                        dve.tensor_tensor(chunk(ylo, 4 + i), y, chunk(yhi, 4 + i).bitcast(F32),
                                          ALU.subtract).then_inc(c_yl, 1)
                for m in range(KC):
                    split(c + AHEAD, q)
                    c += 1
                    dve.wait_ge(s_used, q + c)
                    dve.tensor_tensor(chunk(x, m), down_b[m % 2], chunk(x, m), ALU.add).then_inc(s_x, 1)
                    x_lo(N + 1, m)
                return c

            dve.memset(ones[:, :], 1.0).then_inc(s_const, 1)
            dve.memset(st[:, :], 0.0).then_inc(s_split, RING)
            for c in range(KC):
                dve.wait_ge(s_xt, c + 1)
                dve.tensor_copy(chunk(x, c), down_b[c % 2]).then_inc(s_x, 1)
            for c in range(AHEAD):
                split(c, 0)
            dve.wait_ge(s_par, 16 * 8)
            dve.tensor_scalar(nsink[:, :], sink[:, :], -1.0, None, ALU.mult).then_inc(s_ns, 1)
            dve.wait_ge(s_ns, 1)
            dve.wait_ge(s_const, 3)
            with dve.Fori(0, L) as l:
                q = l * U_LAYER
                N = l * 3
                for m in range(KC):
                    x_lo(N, m)
                ffn(0, q, N, l * (2 * FC), True)
                c = mix(l, q, N + 1)
                ffn(c, q, N + 2, l * (2 * FC) + FC, False)

            dve.wait_ge(s_par2, 16 * PAR2)
            dve.tensor_tensor(gains[:, G67 * KC:(G67 + 1) * KC], gains[:, G6 * KC:(G6 + 1) * KC],
                              gains[:, G7 * KC:(G7 + 1) * KC], ALU.mult).then_inc(s_g67, 1)
            dve.wait_ge(s_g67, 1)
            for m in range(KC):
                x_lo(FINAL1, m)
            split(C_IN + AHEAD, 0)
            split(C_IN + 1 + AHEAD, 0)
            inverse(FINAL1, dest=inv6)
            dve.wait_ge(s_ss, SUM7 + 1)
            dve.tensor_scalar(var[:, :], psS[:, 0:S], 1.0 / D, None, ALU.mult).then_inc(s_v7, 1)
            for j in range(2):
                dve.wait_ge(s_v7, j + 1)
                dve.tensor_tensor(var[:, :], var[:, :], inv6[:, :], ALU.mult).then_inc(s_v7, 1)
            dve.wait_ge(s_v7, 3)
            dve.tensor_scalar(var[:, :], var[:, :], EPS, None, ALU.add).then_inc(s_var, 1)
            newton(SUM7, inv)
            dve.tensor_tensor(inv[:, :], inv[:, :], inv6[:, :], ALU.mult).then_inc(s_i67, 1)
            dve.wait_ge(s_i67, 1)
            done = 0
            for u, (kind, i) in enumerate(ORDER):
                if u >= 2:
                    split(C_IN + u + AHEAD, 0)
                dve.wait_ge(s_used, C_IN + u + 1)
                ps = bank[u % 3][:, :]
                if kind == "a":
                    dve.scalar_tensor_tensor(tmp[i % 2][:, :], ps, 0.5, inv[:, :], ALU.mult, ALU.mult).then_inc(s_i2, 1)
                else:
                    dest = {"g": tmp[2 + i % 2][:, :], "q": chunk(latf, i % QC), "kv": chunk(latf, QC + i % KVC),
                            "kr": tmp[0][:, :], "gate": chunk(gates, i)}[kind]
                    dve.tensor_tensor(dest, ps, inv[:, :], ALU.mult).then_inc(s_i2, 1)
                if kind == "g":
                    dve.wait_ge(s_th, i + 1)
                    dve.scalar_tensor_tensor(zpad[:, i * ZW + PADZ:(i + 1) * ZW], tmp[2 + i % 2][:, :], 1.0,
                                             tmp[i % 2][:, :], ALU.add, ALU.mult).then_inc(s_z, 1)
                if u in (4, 5):
                    for m in range(4 * (u - 4), 4 * (u - 3)):
                        last = dve.scalar_tensor_tensor(chunk(x, m), chunk(x, m), gains[:, G6 * KC + m:G6 * KC + m + 1],
                                                        inv6[:, :], ALU.mult, ALU.mult)
                if u == 7:
                    dve.wait_ge(s_ft, 1)
                    dve.tensor_copy(fcol[:, :], psT[:, 0:2]).then_inc(s_fc, 1)
                    dve.wait_ge(s_fc, 1)
                if u == 9:
                    r, n = rope[64:128, :], inv6[64:128, :]
                    MAGIC = 1.5 * 2.0 ** 23
                    C1, C2 = 6.28125, 1.93500518798828125e-3
                    C3 = 6.283185307179586 - C1 - C2
                    dve.tensor_scalar(r, pos[64:128, :], fcol[64:128, 0:1], None, ALU.mult).then_inc(s_ro, 1)
                    dve.wait_ge(s_ro, 1)
                    dve.tensor_scalar(n, r, 1.0 / 6.283185307179586, MAGIC, ALU.mult, ALU.add).then_inc(s_ro, 1)
                    dve.wait_ge(s_ro, 2)
                    dve.tensor_scalar(n, n, -MAGIC, None, ALU.add).then_inc(s_ro, 1)
                    for j, cst in enumerate((C1, C2, C3)):
                        dve.wait_ge(s_ro, 3 + j)
                        dve.scalar_tensor_tensor(r, n, -cst, r, ALU.mult, ALU.add).then_inc(s_ro, 1)
                    dve.wait_ge(s_ro, 6)
                    dve.tensor_scalar(r, r, 3.1415925, -3.1415925, ALU.min, ALU.max).then_inc(s_ro, 1)
                    c, nn = rope[64:96, :], inv6[64:96, :]
                    dve.wait_ge(s_ro, 7)
                    dve.scalar_tensor_tensor(nn, c, -1.0, c, ALU.mult, ALU.max).then_inc(s_ro, 1)
                    dve.wait_ge(s_ro, 8)
                    dve.tensor_scalar(c, nn, -1.0, 1.5707963267948966, ALU.mult, ALU.add).then_inc(s_rr, 1)
                if u == 11:
                    dve.wait_ge(s_rs, 2)
                    dve.tensor_scalar(rope[96:128, :], rope[96:128, :], fcol[96:128, 1:2], None, ALU.mult).then_inc(s_rs, 1)
                    dve.wait_ge(s_rs, 3)
                if u == U_GATE + 3:
                    inverse(LATQ, n=QL, dest=tmp[2])
                if u == U_GATE + 4:
                    inverse(LATKV, total=psS[:, 512:1024], n=KVL, dest=tmp[3])
                    for j in range(QC + KVC):
                        f = chunk(latf, j)
                        dve.scalar_tensor_tensor(f, f, lgain[:, j:j + 1], (tmp[2] if j < QC else tmp[3])[:, :],
                                                 ALU.mult, ALU.mult).then_inc(s_ln, 1)
                    for j in range(QC + KVC):
                        dve.wait_ge(s_lh, j + 1)
                        dve.tensor_tensor(chunk(latl, j), chunk(latf, j), chunk(lath, j).bitcast(F32),
                                          ALU.subtract).then_inc(s_ll, 1)
                if 3 <= u <= TAP_LAST:
                    left = TAP_LAST + 1 - u
                    for _ in range(-(-(len(DVE_TAPS) - done) // left)):
                        ci, k = DVE_TAPS[done]
                        if k == 0:
                            dve.wait_ge(s_zp, 1)
                            dve.tensor_scalar(chunk(zc, ci), chunk_z(ci, k), cw2[:, k * CC + ci:k * CC + ci + 1],
                                              cvec[:, ci:ci + 1], ALU.mult, ALU.add).then_inc(s_tap, 1)
                        else:
                            dve.wait_ge(s_tap, done)
                            dve.scalar_tensor_tensor(chunk(zc, ci), chunk_z(ci, k), cw2[:, k * CC + ci:k * CC + ci + 1],
                                                     chunk(zc, ci), ALU.mult, ALU.add).then_inc(s_tap, 1)
                        done += 1
                if u == TAP_LAST + 2:
                    dve.wait_ge(s_lsum, 1)
                    dve.tensor_scalar(tmp[1][:, :], psS[:, 0:S], 1.0 / CW, None, ALU.mult).then_inc(s_lm, 1)
                    dve.wait_ge(s_lm, 1)
                    for j in range(CC):
                        dve.tensor_tensor(chunk(zc, j), chunk(zc, j), tmp[1][:, :], ALU.subtract).then_inc(s_ld, 1)
            inverse(LNVAR, n=CW, dest=tmp[1])
            for i in range(CC):
                dve.tensor_tensor(chunk(zc, i), chunk(zc, i), tmp[1][:, :], ALU.mult).then_inc(s_ly, 1)
            for i in range(CC):
                z = chunk(zc, i)
                dve.wait_ge(s_lt, i + 1)
                dve.scalar_tensor_tensor(z, tmp[2 + i % 2][:, :], 1.0, z, ALU.add, ALU.mult).then_inc(s_lc, 1)
                dve.wait_ge(s_ch, i + 1)
                dve.scalar_tensor_tensor(chunk(clo, i), z, 0.5, chunk(chi, i).bitcast(F32), ALU.mult,
                                         ALU.subtract).then_inc(s_cl, 1)

            kr, kx = tmp[0][NOPE:QK, :], tmp[1][NOPE:QK, :]
            dve.tensor_tensor(kr, kr, rope[NOPE:QK, :], ALU.mult).then_inc(s_kr, 1)
            dve.tensor_tensor(kx, tmp[0][QK:P, :], rope[QK:P, :], ALU.mult).then_inc(s_kr, 1)
            dve.wait_ge(s_kr, 2)
            dve.tensor_tensor(kr, kr, kx, ALU.add).then_inc(s_kr, 1)
            for j in range(2):
                dve.wait_ge(s_krh, j + 1)
                ks = slice(j * S, (j + 1) * S)
                dve.tensor_tensor(k2l[NOPE:QK, ks], kr, k2h[NOPE:QK, ks].bitcast(F32), ALU.subtract).then_inc(s_krl, 1)
            split(C_MLA + AHEAD, 0)
            for i in range(TB):
                dve.wait_ge(s_v2h, i + 1)
                dve.tensor_tensor(chunk(v2l, i), bank[i % 3][:, :], chunk(v2h, i).bitcast(F32),
                                  ALU.subtract).then_inc(s_v2l, 1)

            def head(h):
                bb = h % 2 * S
                split(C_MLA + 1 + h + AHEAD, 0)
                dve.wait_ge(s_used, C_MLA + 2 + h)
                if h == 0:
                    dve.wait_ge(s_krh, 2)
                    dve.wait_ge(s_krl, 2)
                r, rx = tmp[0][NOPE:QK, :], tmp[1][NOPE:QK, :]
                dve.tensor_tensor(r, bank[0][NOPE:QK, :], rope[NOPE:QK, :], ALU.mult).then_inc(h_rp, 1)
                dve.tensor_tensor(rx, bank[0][QK:P, :], rope[QK:P, :], ALU.mult).then_inc(h_rp, 1)
                dve.wait_ge(h_rp, 3 * h + 2)
                dve.tensor_tensor(r, r, rx, ALU.add).then_inc(h_rp, 1)
                dve.wait_ge(h_hi, 2 * h + 1)
                dve.tensor_tensor(k2l[0:NOPE, bb:bb + S], bank[1][0:NOPE, :], k2h[0:NOPE, bb:bb + S].bitcast(F32),
                                  ALU.subtract)
                dve.wait_ge(h_hi, 2 * h + 2)
                dve.scalar_tensor_tensor(q2l[0:QK, bb:bb + S], tmp[0][0:QK, :], QK ** -0.5,
                                         q2h[0:QK, bb:bb + S].bitcast(F32), ALU.mult, ALU.subtract).then_inc(h_lo, 1)

            head(0)
            dve.wait_ge(s_mk, 2)
            for s in range(MLA_STEPS + 2):
                if 1 <= s <= MLA_STEPS:
                    pc = (s - 1) % 2 * 8
                    dve.wait_ge(b_ex, s)
                    dve.reciprocal(st2[:, pc + 4:pc + 6], st2[:, pc + 2:pc + 4]).then_inc(b_rd, 1)
                if s >= 2:
                    r = s - 2
                    h, (i1, i2) = r // 2, BLOCKS[r % 2]
                    rows = slice(h % 2 * HD, h % 2 * HD + HD)
                    dve.wait_ge(b_oh, r + 1)
                    view = lambda a: chunk(a, h // 2)[rows].rearrange("p (i n) -> p i n", n=P)[:, i1:i2 + 1:i2 - i1, :]
                    dve.tensor_tensor(view(a2l), psO[rows, 0:2 * P].rearrange("p (i n) -> p i n", n=P),
                                      view(a2h).bitcast(F32), ALU.subtract).then_inc(b_ol, 1)
                if 1 <= s <= MLA_STEPS:
                    dve.wait_ge(b_th, s)
                    dve.tensor_tensor(pt2l[:, :], psT[:, 0:(TB + 1) * P], pt2h[:, :].bitcast(F32),
                                      ALU.subtract).then_inc(b_tl, 1)
                if s < MLA_STEPS:
                    pc = s % 2 * 8
                    dve.wait_ge(b_sc, s + 1)
                    for half, i in enumerate(BLOCKS[s % 2]):
                        a = psS[:, half * 512 + i * P:half * 512 + (i + 1) * P]
                        dve.tensor_tensor(a, a, mask[:, :], ALU.add).then_inc(b_mk, 1)
                    for half, i in enumerate(BLOCKS[s % 2]):
                        dve.wait_ge(b_mk, 2 * s + 1 + half)
                        e = dve.tensor_reduce(st2[:, pc + half:pc + half + 1], psS[:, half * 512:half * 512 + (i + 1) * P],
                                              AX.X, ALU.max, negate=True)
                    e.then_inc(b_mx, 1)
                    if s % 2 == 0 and s // 2 + 1 < H2:
                        head(s // 2 + 1)

            dve.wait_ge(s_gt, 2 * KC)
            for m in range(KC):
                split(C_MRG + m + AHEAD, 0)
                dve.wait_ge(s_used, C_MRG + m + 1)
                t1, t2 = tmp[m % 2][:, :], tmp[2 + m % 2][:, :]
                dve.scalar_tensor_tensor(t1, chunk(gates, m), 1.0, b(gate_b[m % 2][:, :]), ALU.add, ALU.mult).then_inc(s_ga, 1)
                dve.scalar_tensor_tensor(t2, chunk(gates, KC + m), 1.0, b(up_b[m % 2][:, :]), ALU.add, ALU.mult).then_inc(s_ga, 1)
                dve.wait_ge(s_ga, 2 * m + 2)
                dve.tensor_tensor(t2, t2, t1, ALU.add).then_inc(s_mg, 1)
                dve.wait_ge(s_mgh, m + 1)
                dve.scalar_tensor_tensor(chunk(mgl, m), t2, 0.5, chunk(mgh, m).bitcast(F32), ALU.mult,
                                         ALU.subtract).then_inc(s_mgl, 1)
            for m in range(KC):
                split(C_OUT + m + AHEAD, 0)
                if m == 1:
                    v, y = st2[:, 18:20], st2[:, 20:22]
                    dve.wait_ge(s_msq, 1)
                    dve.tensor_scalar(v, st2[:, 16:18], 1.0 / D, EPS, ALU.mult, ALU.add).then_inc(s_mv, 1)
                    dve.wait_ge(s_mr, 1)
                    dve.reciprocal(y, y).then_inc(s_mst, 1)
                    for j in range(2):
                        dve.wait_ge(s_mst, j + 1)
                        dve.tensor_tensor(v, v, y, ALU.mult).then_inc(s_mst, 1)
                    dve.wait_ge(s_mst, 3)
                    dve.tensor_scalar(v, v, -0.5, 1.5, ALU.mult, ALU.add).then_inc(s_mst, 1)
                    dve.wait_ge(s_mst, 4)
                    dve.tensor_tensor(y, v, y, ALU.mult).then_inc(s_mst, 1)
                    dve.wait_ge(s_mst, 5)
                    for i in range(MB):
                        mr = memr[:, i * D:(i + 1) * D]
                        dve.tensor_scalar(mr, mr, st2[:, 20 + i:21 + i], None, ALU.mult).then_inc(s_mn, 1)
                if m in (3, 6):
                    r = m // 6
                    for i in range(4):
                        cc = 4 * r + i
                        ms = slice(cc * ML, (cc + 1) * ML)
                        dve.wait_ge(s_mh, cc // 2 * 2 + 2)
                        dve.scalar_tensor_tensor(mtl[:, ms], psS[:, i * ML:(i + 1) * ML],
                                                 gains[:, GMEM * KC + cc:GMEM * KC + cc + 1], mth[:, ms].bitcast(F32),
                                                 ALU.mult, ALU.subtract).then_inc(s_ml, 1)
                dve.wait_ge(s_used, C_OUT + m + 1)
                dve.tensor_tensor(chunk(x, m), down_b[m % 2], chunk(x, m), ALU.add).then_inc(s_x, 1)
                x_lo(FINAL1 + 1, m, xbl, xbh)

            for j in range(H3):
                split(C_XQ + j + AHEAD, 0)
                if j == 0:
                    inverse(XATTN)
                dve.wait_ge(s_used, C_XQ + j + 1)
                dve.scalar_tensor_tensor(tmp[j % 2][:, :], bank[j % 3][:, :], P ** -0.5, inv[:, :], ALU.mult,
                                         ALU.mult).then_inc(s_x2, 1)
                dve.wait_ge(s_x2h, j + 1)
                dve.tensor_tensor(chunk(q3l, j), tmp[j % 2][:, :], chunk(q3h, j).bitcast(F32), ALU.subtract).then_inc(s_x2l, 1)
            for j in range(H3):
                split(C_XK + j + AHEAD, 0)
                dve.wait_ge(s_k3h, j + 1)
                ks = slice(j * ML, (j + 1) * ML)
                dve.tensor_tensor(k3l[:, ks], bank[(H3 + j) % 3][:, 0:ML], k3h[:, ks].bitcast(F32), ALU.subtract).then_inc(s_k3l, 1)

            def cross_max(s):
                pc = s % 2 * 16
                dve.wait_ge(d_sc, s + 1)
                dve.tensor_reduce(st[:, pc:pc + 4], psS[:, :].rearrange("p (h n) -> p h n", h=H3), AX.X, ALU.max,
                                  negate=True).then_inc(d_mx, 1)

            def cross_rden(s):
                pc = s % 2 * 16
                dve.wait_ge(d_ex, s + 1)
                dve.reciprocal(st[:, pc + 8:pc + 12], st[:, pc + 4:pc + 8]).then_inc(d_rd, 1)

            def cross_lo(s):
                dve.wait_ge(d_th, s + 1)
                dve.tensor_tensor(pt3l[:, :], psT[:, :], pt3h[:, :].bitcast(F32), ALU.subtract).then_inc(d_tl, 1)

            def cross_out(s):
                dve.wait_ge(d_oh, s + 1)
                view = lambda a: a[:, :].rearrange("p (h n) -> p h n", h=H3)[:, :, s * P:(s + 1) * P]
                dve.tensor_tensor(view(a3l), psO[:, :].rearrange("p (h n) -> p h n", h=H3), view(a3h).bitcast(F32),
                                  ALU.subtract).then_inc(d_ol, 1)

            cross_max(0)
            split(C_XV + AHEAD, 0)
            cross_rden(0)
            cross_max(1)
            split(C_XV + 1 + AHEAD, 0)
            split(C_XV + 2 + AHEAD, 0)
            cross_rden(1)
            cross_lo(0)
            split(C_XV + 3 + AHEAD, 0)
            for i in range(MB):
                dve.wait_ge(s_v3h, i + 1)
                dve.tensor_tensor(chunk(v3l, i), bank[2 * (1 - i)][:, :], chunk(v3h, i).bitcast(F32),
                                  ALU.subtract).then_inc(s_v3l, 1)
            cross_max(2)
            cross_rden(2)
            cross_out(0)
            cross_lo(1)
            cross_max(3)
            cross_rden(3)
            cross_out(1)
            cross_lo(2)
            cross_out(2)
            cross_lo(3)
            cross_out(3)
            for j in range(KC // 2):
                split(C_XO + j + AHEAD, 0)
                dve.wait_ge(s_used, C_XO + j + 1)
                for i in range(2):
                    m = 2 * j + i
                    dve.tensor_tensor(chunk(x, m), down_b[i], chunk(x, m), ALU.add).then_inc(s_x, 1)
                    x_lo(FINAL1 + 2, m)

            mlp_b = [bank[0][:, :], bank[1][:, :], bank[2][:, :], psS[:, 0:S]]
            for ps in range(2):
                c0 = C_MLP + ps * U_PASS

                def four(c, q, fi, first):
                    for j in range(4):
                        split(c + j + AHEAD, q)
                        if first and ps == 0 and j == 0:
                            inverse(MLPN)
                        f = fi + (ps * FP + j)
                        dve.wait_ge(s_used, q + (c + j + 1))
                        dve.scalar_tensor_tensor(tmp[j % 2][:, :], mlp_b[j], 0.0, inv[:, :], ALU.max, ALU.mult).then_inc(m_r, 1)
                        dve.wait_ge(m_hi, f + 1)
                        hs = ds((fi + j) * S, S)
                        dve.tensor_tensor(mlo[:, hs], tmp[2 + j % 2][:, :], mhi[:, hs].bitcast(F32), ALU.subtract).then_inc(m_lo, 1)
                four(c0, 0, 0, True)
                with dve.Fori(1, FP // 4) as it:
                    four(c0, it * 4, it * 4, False)
                with dve.Fori(0, KC // 2) as mi:
                    for m in range(2):
                        for j in range(2):
                            split(c0 + FP + 2 * m + j + AHEAD, mi * 4)
                        dve.wait_ge(s_used, mi * 4 + (c0 + FP + 2 * m + 2))
                        xm = x[:, ds(mi * (2 * S) + m * S, S)]
                        dve.tensor_tensor(xm, down_b[m], xm, ALU.add).then_inc(s_x, 1)
            inverse(FINAL2)
            for m in range(KC):
                dve.scalar_tensor_tensor(chunk(x, m), chunk(x, m), gains[:, GF * KC + m:GF * KC + m + 1], inv[:, :],
                                         ALU.mult, ALU.mult).then_inc(s_o, 1)
            for n in range(2 * TB):
                dve.wait_ge(s_ot, n + 1)
                if n >= 2:
                    dve.wait_ge(s_out[n % 2], 16 * (n // 2))
                dve.tensor_copy(tmp[n % 2][:, :], down_b[n % 2]).then_inc(s_oc, 1)

        @block.gpsimd
        def _(pool):
            def squares(N, r=None):
                r = N if r is None else r
                for m in range(KC):
                    pool.wait_ge(s_x, N * KC + m + 1)
                    xm = chunk(x, m)
                    if m == 0:
                        pool.tensor_tensor(acc[:, :], xm, xm, ALU.mult).then_inc(s_sq, 1)
                        continue
                    pool.wait_ge(s_sq, r * KC + m)
                    pool.tensor_tensor(sqt[:, :], xm, xm, ALU.mult).then_inc(s_sqm, 1)
                    pool.wait_ge(s_sqm, r * (KC - 1) + m)
                    pool.tensor_tensor(acc[:, :], acc[:, :], sqt[:, :], ALU.add).then_inc(s_sq, 1)

            def mix(l):
                for u in range(3 * CC + 1):
                    if 1 <= u and u - 1 < STEPS1:
                        s = u - 1
                        n = P if s < 2 else 2 * P
                        pool.wait_ge(a_rd, l * STEPS1 + s + 1)
                        a = sc[s % 2][:, :].rearrange("p (h n) -> p h n", h=4)[:, :, 0:n]
                        r = 24 + 4 * (s % 2)
                        pool.tensor_tensor(a, a, st[:, r:r + 4].unsqueeze(2).to_broadcast([P, 4, n]),
                                           ALU.mult).then_inc(a_pr, 1)
                    if u % 3 == 2:
                        i = u // 3
                        if i == 0:
                            pool.wait_ge(s_pad, l + 1)
                        if i >= 2:
                            pool.wait_ge(c_t0, l * CC + i - 1)
                        pool.wait_ge(c_ev, l * 3 * CC + 3 * i + 3)
                        pool.tensor_tensor(upad[i % 2][:, 2:2 + S], tmp[2][:, :], tmp[3][:, :], ALU.mult).then_inc(c_u, 1)
                    if u % 3 == 0 and u >= 3:
                        i = u // 3 - 1
                        pool.wait_ge(c_t0, l * CC + i + 1)
                        pool.tensor_tensor(cy[i % 2][:, :], cy[i % 2][:, :], tmp[i % 2][:, :], ALU.mult).then_inc(c_y, 1)

            pool.memset(ident[:, :], 0.0).then_inc(s_ident, 1)
            pool.wait_ge(s_ident, 1)
            pool.affine_select(out=ident[:, :], in_=ident[:, :], compare_op=ALU.not_equal, fill=1.0,
                               base=0, pattern=[[-1, P]], channel_multiplier=1).then_inc(s_const, 1)
            pool.iota(dist[:, :], [[-1, 2 * P]], base=P, channel_multiplier=1,
                      allow_small_or_imprecise_dtypes=True).then_inc(s_ident, 1)
            pool.wait_ge(s_ident, 2)
            pool.affine_select(out=dist[:, :], in_=dist[:, :], compare_op=ALU.is_ge, fill=MASKED,
                               base=P, pattern=[[-1, 2 * P]], channel_multiplier=1).then_inc(s_ident, 1)
            pool.wait_ge(s_ident, 3)
            pool.affine_select(out=dist[:, :], in_=dist[:, :], compare_op=ALU.is_gt, fill=MASKED,
                               base=0, pattern=[[1, 2 * P]], channel_multiplier=-1).then_inc(s_const, 1)
            for i in range(HALF):
                f = pool.memset(frow[0:1, i:P:HALF], 10000.0 ** (-i / HALF))
            f.then_inc(s_fr, 1)
            pool.memset(frow[0:1, P:2 * P], 1.0).then_inc(s_fr, 1)
            pool.wait_ge(s_fr, 2)
            pool.memset(frow[0:1, P + QK:P + QK + HALF], -1.0).then_inc(s_fr, 1)
            pool.memset(mask[:, :], 0.0).then_inc(s_mk, 1)
            pool.wait_ge(s_mk, 1)
            pool.affine_select(out=mask[:, :], in_=mask[:, :], compare_op=ALU.is_ge, fill=-MASKED,
                               base=0, pattern=[[-1, P]], channel_multiplier=1).then_inc(s_mk, 1)
            with pool.Fori(0, L) as l:
                squares(l * 3)
                squares(l * 3 + 1)
                mix(l)
                squares(l * 3 + 2)
            squares(FINAL1)
            pool.memset(zpad[:, :].rearrange("p (i n) -> p i n", i=CC)[:, :, 0:PADZ], 0.0).then_inc(s_zp, 1)
            for a, (i, k) in enumerate(POOL_TAPS):
                pool.wait_ge(s_pm, a + 2 + (i == 3))
                if k >= 2:
                    pool.wait_ge(s_pa, a)
                pool.tensor_tensor(chunk(zc, i), chunk(zc, i), (acc, sqt)[a % 2][:, :], ALU.add).then_inc(s_pa, 1)
            for s in range(MLA_STEPS):
                o, pc = 0, s % 2 * 8
                pool.wait_ge(b_rd, s + 1)
                for half, i in enumerate(BLOCKS[s % 2]):
                    a = p2[s % 2][:, o:o + (i + 1) * P]
                    e = pool.tensor_tensor(a, a, st2[:, pc + 4 + half:pc + 5 + half].to_broadcast([P, (i + 1) * P]), ALU.mult)
                    o += (i + 1) * P
                e.then_inc(b_pr, 1)
            squares(FINAL1 + 1)
            for s in range(TB):
                pc = s % 2 * 16
                pool.wait_ge(d_rd, s + 1)
                a = p3[s % 2][:, :].rearrange("p (h n) -> p h n", h=H3)
                pool.tensor_tensor(a, a, st[:, pc + 8:pc + 12].unsqueeze(2).to_broadcast([P, H3, ML]), ALU.mult).then_inc(d_pr, 1)
            squares(FINAL1 + 2)
            squares(FINAL1 + 4, FINAL1 + 3)



_NAMES = ["x", "ffn1_norm", "ffn1_wg", "ffn1_wu", "ffn1_wd", "mix_norm", "w_in", "conv_w", "attn_sink", "w_out",
          "ffn2_norm", "ffn2_wg", "ffn2_wu", "ffn2_wd", "final_norm", "mem_2", "positions_2", "norm_mix_g_2", "w_in_2",
          "conv_w_2", "conv_b_2", "conv_ln_g_2", "conv_ln_b_2", "w_conv_out_2", "q_norm_g_2", "w_uq_2", "kv_norm_g_2",
          "w_ukv_2", "w_mla_out_2", "w_out_2", "norm_xattn_g_2", "norm_mem_g_2", "w_xq_2", "w_xkv_2", "w_xo_2",
          "norm_mlp_g_2", "w_mlp1_2", "w_mlp2_2", "final_norm_g_2"]


def kernel(**inputs):
    import numpy as _np
    import concourse.bacc as _bacc
    from concourse import mybir as _mybir
    from concourse.bass_utils import run_bass_kernel_spmd as _run

    nc = _bacc.Bacc("TRN2", target_bir_lowering=False, num_devices=1,
                    dynamic_dma_scratch_size=2048)
    arrays, t = {}, {}
    for name in _NAMES:
        a = _np.ascontiguousarray(inputs[name])
        arrays[f"in_{name}"] = a
        t[name] = nc.dram_tensor(f"in_{name}", a.shape, _mybir.dt.from_np(a.dtype), kind="ExternalInput").ap()
    out = nc.dram_tensor("out_0", inputs["x"].shape, _mybir.dt.float32, kind="ExternalOutput").ap()
    build(nc, t, out)
    r = _run(nc, [arrays], core_ids=[0])
    return r.results[0]["out_0"]
```

```python
from contextlib import ExitStack

import concourse.bass as bass
from concourse import mybir

P = 128
ALU = mybir.AluOpType
ACT = mybir.ActivationFunctionType
AX = mybir.AxisListType
F32 = mybir.dt.float32
F32R = mybir.dt.float32r
ds = bass.ds

RING = 4
AHEAD = 3
UNIT = 8 * P
LANDED = 64
MASKED = 1e30


def build(nc, t, out):
    S, D = t["x"].shape[1:]
    L, _, FF = t["ffn1_wg"].shape
    KC = D // P
    TB = S // P
    FC = FF // P
    EPS = 1e-6
    HD = 64
    H1 = t["attn_sink"].shape[1]
    G1 = H1 // 2
    CW = t["conv_w"].shape[2]
    CC = CW // P
    Q0, K0, V0 = 0, H1 * HD, H1 * HD + P
    CB0 = V0 + P
    STEPS1 = 2 * TB

    ML = t["mem_2"].shape[1]
    MB = ML // P
    TAPS = t["conv_w_2"].shape[1]
    QL = t["q_norm_g_2"].shape[1]
    KVL = t["kv_norm_g_2"].shape[1]
    QC, KVC = QL // P, KVL // P
    ROPE = 32
    HALF = ROPE // 2
    NOPE = 64
    QK = NOPE + ROPE
    H2 = t["w_uq_2"].shape[2] // QK
    H3 = 4
    FF2 = t["w_mlp1_2"].shape[2]
    FP = FF2 // P // 2
    A0, GT0, CQ0 = 0, CW, 2 * CW
    CKV0 = CQ0 + QL
    KR0 = CKV0 + KVL
    GL0 = KR0 + ROPE
    PADZ = 32
    ZW = PADZ + S
    MLA_STEPS = 2 * H2
    BLOCKS = ((0, TB - 1), (1, TB - 2))

    ctx = ExitStack()
    with ctx:
        def sem(name):
            return ctx.enter_context(nc.semaphore(name))

        base = (nc.sbuf_base + 31) // 32 * 32
        at = [base]

        def sb(name, cols, dt=F32, off=None, rows=P):
            if off is None:
                off = -(-at[0] // 32) * 32
                at[0] = off + cols * 4
            return nc.alloc_sbuf_tensor_at(name, [rows, cols], dt, offset=off)

        x = sb("x", KC * S)
        X_AT = at[0]
        xhi = sb("xhi", KC * S, F32R)
        xlo = sb("xlo", KC * S, F32R)
        raw = sb("raw", RING * UNIT)
        whi = sb("whi", RING * UNIT, F32R)
        wlo = sb("wlo", RING * UNIT, F32R)
        ident = sb("ident", P)
        ones = sb("ones", P)
        P2_AT = at[0]
        acc = sb("acc", S)
        sqt = sb("sqt", S)
        inv = sb("inv", S)
        var = sb("var", S)
        gains = sb("gains", 13 * KC)
        inv6 = sb("inv6", S)
        rope = sb("rope", S)
        mask = sb("mask", P)
        identr = sb("identr", P, F32R)
        maskr = sb("maskr", P, F32R)
        cw2 = sb("cw2", TAPS * CC)
        cvec = sb("cvec", 3 * CC)
        lgain = sb("lgain", QC + KVC)
        frow = sb("frow", 2 * P, rows=1)
        fcol = sb("fcol", 2)
        st2 = sb("st2", 32)
        fin = sb("fin", 2 * TB)
        pos = sb("pos", S, mybir.dt.int32)
        cw1 = sb("cw1", L * 3 * CC)
        sink = sb("sink", L * H1)
        nsink = sb("nsink", L * H1)
        dist = sb("dist", 2 * P)
        tmp = [sb(f"tmp{i}", S) for i in range(4)]
        st = sb("st", 4 * 8)
        region = at[0]
        hhi = sb("hhi", FC * S, F32R)
        hlo = sb("hlo", FC * S, F32R)
        assert at[0] <= nc.sbuf_usable_end, (at[0], nc.sbuf_usable_end)
        top = at[0]

        at[0] = region
        xin = sb("xin", TB * D)
        at[0] = region
        yhi = sb("yhi", KC * S, F32R)
        ylo = sb("ylo", KC * S, F32R)
        qhi = sb("qhi", 4 * S, F32R)
        qlo = sb("qlo", 4 * S, F32R)
        khi = sb("khi", S, F32R)
        klo = sb("klo", S, F32R)
        vhi = sb("vhi", S, F32R)
        vlo = sb("vlo", S, F32R)
        sc = [sb(f"sc{i}", 8 * P) for i in range(2)]
        pthi = sb("pthi", 8 * P, F32R)
        ptlo = sb("ptlo", 8 * P, F32R)
        upad = [sb(f"upad{i}", S + 8) for i in range(2)]
        cy = [sb(f"cy{i}", S) for i in range(2)]
        assert at[0] <= top, (at[0] - top)

        at[0] = region
        gates = sb("gates", 2 * KC * S)
        sq7 = sb("sq7", KC * S, off=region)
        lath = sb("lath", (QC + KVC) * S, F32R)
        latl = sb("latl", (QC + KVC) * S, F32R)
        zpad = sb("zpad", CC * ZW, off=at[0])
        chi = sb("chi", CC * S, F32R)
        clo = sb("clo", CC * S, F32R)
        latf = sb("latf", (QC + KVC) * S, off=at[0])
        v2h = sb("v2h", TB * S, F32R)
        v2l = sb("v2l", TB * S, F32R)
        zc = sb("zc", CC * S)
        pt2h = sb("pt2h", 5 * P, F32R)
        pt2l = sb("pt2l", 5 * P, F32R)
        assert at[0] <= nc.sbuf_usable_end, (at[0], nc.sbuf_usable_end)
        at[0] = P2_AT
        p2 = [sb(f"p2_{i}", 5 * P) for i in range(2)]
        assert at[0] <= var.manual_sbuf_range[0]
        at[0] = X_AT
        q2h = sb("q2h", 2 * S, F32R)
        q2l = sb("q2l", 2 * S, F32R)
        k2h = sb("k2h", 2 * S, F32R)
        k2l = sb("k2l", 2 * S, F32R)
        a2h = sb("a2h", CC * S, F32R)
        a2l = sb("a2l", CC * S, F32R)
        mgh = xhi
        at[0] = v2h.manual_sbuf_range[0]
        mgl = sb("mgl", KC * S, F32R)
        at[0] = X_AT
        p3 = [sb(f"p3_{i}", 8 * P) for i in range(2)]
        pt3h = sb("pt3h", 8 * P, F32R)
        pt3l = sb("pt3l", 8 * P, F32R)
        at[0] = region
        xbh = sb("xbh", KC * S, F32R)
        xbl = sb("xbl", KC * S, F32R)
        memr = sb("memr", MB * D)
        mscr = sb("mscr", MB * D, off=at[0])
        mth = sb("mth", KC * ML, F32R)
        mtl = sb("mtl", KC * ML, F32R)
        q3h = sb("q3h", H3 * S, F32R)
        q3l = sb("q3l", H3 * S, F32R)
        k3h = sb("k3h", H3 * ML, F32R)
        k3l = sb("k3l", H3 * ML, F32R)
        v3h = sb("v3h", MB * H3 * P, F32R)
        v3l = sb("v3l", MB * H3 * P, F32R)
        assert at[0] <= nc.sbuf_usable_end, (at[0], nc.sbuf_usable_end)
        at[0] = region
        a3h = sb("a3h", H3 * S, F32R)
        a3l = sb("a3l", H3 * S, F32R)
        at[0] = region
        mhi = sb("mhi", FP * S, F32R)
        mlo = sb("mlo", FP * S, F32R)
        xg = sb("xg", KC * S, off=X_AT)
        assert at[0] + 2 * KC * S * 2 <= nc.sbuf_usable_end, at[0]
        yout = sb("yout", 2 * TB * 512, off=at[0])

        bank = [ctx.enter_context(nc.psum_tensor(f"bank{i}", [P, 512], F32)) for i in range(3)]
        psS = ctx.enter_context(nc.psum_tensor("psS", [P, 1024], F32))
        psT = ctx.enter_context(nc.psum_tensor("psT", [P, 1024], F32))
        psO = ctx.enter_context(nc.psum_tensor("psO", [P, 512], F32))
        gate_b = [bank[0], psS[:, 0:512]]
        up_b = [bank[1], bank[2]]
        down_b = [psT[:, 0:512], psT[:, 512:1024]]
        out_b = [bank[0][:, :], bank[1][:, :], bank[2][:, :], psS[:, 0:512], psS[:, 512:1024]] + down_b
        xo_b = down_b + [bank[1][:, :], psS[:, 0:512]]
        in_b = [bank[0][:, :], bank[1][:, :], bank[2][:, :], down_b[0], down_b[1]]
        v2_b = [psO[:, :], bank[2][:, :], down_b[0], down_b[1]]

        def b(ap):
            return ap[:, :] if not isinstance(ap, bass.AP) else ap

        landed = [sem(f"landed{i}") for i in range(RING)]
        s_hi = sem("weights_hi_ready")
        s_split = sem("weights_split")
        s_used = sem("weights_used")
        s_first = sem("first_params_landed")
        s_par = sem("params_landed")
        s_par2 = sem("params2_landed")
        s_xin = [sem(f"x_landed{i}") for i in range(2)]
        s_const = sem("consts_ready")
        s_ident = sem("ident_zeroed")
        s_xt = sem("x_transposed")
        s_x = sem("x_ready")
        s_xh = sem("xhi_ready")
        s_xl = sem("xlo_ready")
        s_sqm = sem("square_made")
        s_sq = sem("squares_summed")
        s_ss = sem("sum_of_squares")
        s_var = sem("variance_ready")
        s_rt = sem("root_ready")
        s_nst = sem("newton_step")
        s_inv = sem("inv_ready")
        s_gs = sem("gate_scaled")
        s_si = sem("silu_done")
        s_us = sem("up_scaled")
        s_h = sem("hidden_ready")
        s_hh = sem("hidden_hi_ready")
        s_hl = sem("hidden_lo_ready")
        s_ns = sem("nsink_ready")
        s_vs = sem("v_scaled")
        s_vt = sem("v_transposed")
        s_vh = sem("vhi_ready")
        s_vl = sem("vlo_ready")
        s_qs = sem("qk_scaled")
        s_qh = sem("qk_hi_ready")
        s_ql = sem("qk_lo_ready")
        a_sc = sem("scores_done")
        a_bi = sem("scores_biased")
        a_rm = sem("row_max_made")
        a_mx = sem("max_with_sink")
        a_sd = sem("shift_ready")
        a_ex = sem("exp_done")
        a_dn = sem("denominator_ready")
        a_rd = sem("reciprocal_ready")
        a_pr = sem("probs_ready")
        a_tt = sem("probs_transposed")
        a_th = sem("probs_hi_ready")
        a_tl = sem("probs_lo_ready")
        a_pv = sem("pv_done")
        a_oh = sem("attn_hi_ready")
        a_ol = sem("attn_lo_ready")
        c_ev = sem("conv_part_scaled")
        c_u = sem("conv_input_ready")
        c_t2 = sem("conv_tap2_done")
        c_t1 = sem("conv_tap1_done")
        c_t0 = sem("conv_tap0_done")
        c_y = sem("conv_gated")
        c_yh = sem("conv_hi_ready")
        c_yl = sem("conv_lo_ready")
        s_pad = sem("pads_zeroed")
        s_i2 = sem("w_in2_scaled")
        s_g67 = sem("gain_product_ready")
        s_xg = sem("x_times_gain")
        s_v7 = sem("variance7_step")
        s_q7 = sem("squares7_ready")
        s_z = sem("glu_ready")
        s_zp = sem("glu_pads_zeroed")
        s_th = sem("glu_tanh_done")
        s_tap = sem("dve_tap_done")
        s_pm = sem("tap_product_ready")
        s_pa = sem("tap_added")
        s_gt = sem("gate_tanh_done")
        s_lq = sem("latent_squared")
        s_ln = sem("latent_normed")
        s_lh = sem("latent_hi_ready")
        s_ll = sem("latent_lo_ready")
        s_fr = sem("freq_row_ready")
        s_ft = sem("freq_turned")
        s_fc = sem("freq_column_ready")
        s_ro = sem("rope_step")
        s_rr = sem("rope_angles_ready")
        s_rs = sem("rope_table_ready")
        s_mk = sem("mask_ready")
        s_lsum = sem("layer_norm_sum")
        s_lm = sem("layer_norm_mean")
        s_ld = sem("layer_norm_centred")
        s_lsq = sem("layer_norm_squared")
        s_ly = sem("layer_norm_scaled")
        s_lc = sem("conv_silu_done")
        s_ch = sem("conv2_hi_ready")
        s_cl = sem("conv2_lo_ready")
        s_v2 = sem("v2_projected")
        s_v2h = sem("v2_hi_ready")
        s_v2l = sem("v2_lo_ready")
        s_kr = sem("k_rope_step")
        s_krh = sem("k_rope_hi_ready")
        s_krl = sem("k_rope_lo_ready")
        h_cp = sem("q_nope_copied")
        h_rp = sem("q_rope_step")
        h_hi = sem("head_hi_ready")
        h_lo = sem("head_lo_ready")
        b_sc = sem("mla_scores_done")
        s_mkr = sem("rounded_mask_ready")
        b_mx = sem("mla_max_ready")
        b_ex = sem("mla_exp_done")
        b_rd = sem("mla_reciprocal_ready")
        b_pr = sem("mla_probs_ready")
        b_tt = sem("mla_probs_transposed")
        b_th = sem("mla_probs_hi_ready")
        b_tl = sem("mla_probs_lo_ready")
        b_pv = sem("mla_pv_done")
        b_oh = sem("mla_out_hi_ready")
        b_ol = sem("mla_out_lo_ready")
        s_ga = sem("branches_gated")
        s_mg = sem("branches_merged")
        s_mgh = sem("merged_hi_ready")
        s_mgl = sem("merged_lo_ready")
        s_memin = sem("mem_landed")
        s_msq = sem("mem_squared")
        s_mr = sem("mem_root_ready")
        s_mst = sem("mem_newton_step")
        s_mn = sem("mem_normed")
        s_mt = sem("mem_transposed")
        s_mh = sem("mem_hi_ready")
        s_ml = sem("mem_lo_ready")
        s_x2 = sem("cross_q_scaled")
        s_x2h = sem("cross_q_hi_ready")
        s_x2l = sem("cross_q_lo_ready")
        s_k3h = sem("cross_k_hi_ready")
        s_k3l = sem("cross_k_lo_ready")
        s_v3h = sem("cross_v_hi_ready")
        s_v3l = sem("cross_v_lo_ready")
        d_sc = sem("cross_scores_done")
        d_mx = sem("cross_max_ready")
        d_ex = sem("cross_exp_done")
        d_rd = sem("cross_reciprocal_ready")
        d_pr = sem("cross_probs_ready")
        d_tt = sem("cross_probs_transposed")
        d_th = sem("cross_probs_hi_ready")
        d_tl = sem("cross_probs_lo_ready")
        d_pv = sem("cross_pv_done")
        d_oh = sem("cross_out_hi_ready")
        d_ol = sem("cross_out_lo_ready")
        m_r = sem("mlp_relu_done")
        m_sq = sem("mlp_squared")
        m_hi = sem("mlp_hi_ready")
        m_lo = sem("mlp_lo_ready")
        s_o = sem("out_scaled")
        s_ot = sem("out_transposed")
        s_oc = [sem(f"out_scaled_by_{e}") for e in ("vector", "scalar")]
        s_fv = sem("final_variance_step")
        s_out = [sem(f"out_written{i}") for i in range(2)]

        U_GU = 2 * FC
        U_FFN = U_GU + 3 * KC
        U_MIX = 8 + 3 * CC + KC
        U_LAYER = 2 * U_FFN + U_MIX
        C_IN = L * U_LAYER
        IN_UNITS = 2 * CC + QC + KVC + 1 + 2 * KC
        C_MLA = C_IN + IN_UNITS
        C_V2 = C_MLA + 1
        C_MRG = C_MLA + 1 + H2
        C_OUT = C_MRG + KC
        C_XQ = C_OUT + KC
        C_XK = C_XQ + H3
        C_XV = C_XK + H3
        C_XO = C_XV + KC // 2
        C_MLP = C_XO + KC // 2
        U_PASS = FP + 2 * KC
        C_END = C_MLP + 2 * U_PASS
        ORDER = [(k, i) for i in range(CC) for k in ("a", "g")] + [("q", i) for i in range(QC)] \
            + [("kv", i) for i in range(KVC)] + [("kr", 0)] + [("gate", i) for i in range(2 * KC)]
        U_KR = 2 * CC + QC + KVC
        U_GATE = U_KR + 1
        FINAL1, SUM7, LATQ, LATKV, LNVAR, XATTN, MLPN, FINAL2 = range(3 * L, 3 * L + 8)
        G67, GX, GM, G6, GF, GMEM, G7 = range(3 * L, 3 * L + 7)
        POOL_TAPS = [(i, k) for i in (1, 3) for k in range(1, TAPS)]
        LEAD = 12
        DVE_TAPS = [(0, k) for k in range(LEAD)]
        for k in range(TAPS):
            DVE_TAPS += [(2, k)] + ([(0, k + LEAD)] if k + LEAD < TAPS else [])
        TAP_LAST = IN_UNITS - 1
        LAT = U_GATE + 7
        LN_MEAN, LN_VAR, LN_Y = 2, 6, 7
        assert U_LAYER % RING == 0 and U_GU % RING == 0 and (3 * 4) % RING == 0

        def slot(c):
            return c % RING

        def wcols(buf, c, k, n=P):
            a = slot(c) * UNIT + k * P
            return buf[:, a:a + n]

        def chunk(buf, c, lo=0, n=S):
            return buf[:, c * S + lo:c * S + lo + n]

        PAR2 = 11

        ln_sq = (tmp[2], tmp[3], var, inv6)

        def head_unit(h):
            return C_MLA + h + (h > 0)

        def chunk_z(i, k):
            a = i * ZW + PADZ - (TAPS - 1) + k
            return zpad[:, a:a + S]

        block = ctx.enter_context(nc.Block())

        @block.sync
        def _(sp):
            def slot_free(c, q):
                sp.wait_ge(s_split, q + (c + 1))

            def dst(c, k0, k1):
                a = slot(c) * UNIT
                return raw[:, a + k0 * P:a + k1 * P].rearrange("p (k n) -> p k n", n=P)

            def load(c, q, src):
                slot_free(c, q)
                sp.dma_start(dst(c, 0, src.shape[1]), src).then_inc(landed[slot(c)], LANDED)

            def cols(w, l, k0, k1, j0):
                v = w[ds(l, 1), k0 * P:k1 * P, ds(j0, P)]
                return v.rearrange("o (k p) n -> p (o k) n", p=P)

            def ffn(c0, q0, l, wg, wu, wd):
                with sp.Fori(0, FC // 2) as it:
                    for p in range(2):
                        for j, w in enumerate((wg, wu)):
                            load(c0 + 2 * p + j, q0 + it * 4, cols(w, l, 0, KC, it * (2 * P) + p * P))
                with sp.Fori(0, 2) as mi:
                    for m in range(4):
                        for j in range(3):
                            load(c0 + U_GU + 3 * m + j, q0 + mi * 12,
                                 cols(wd, l, 8 * j, min(8 * j + 8, FC), mi * (4 * P) + m * P))

            XH = D // 2
            for i in range(2):
                sp.dma_start(xin[:, :].rearrange("p (i d) -> p i d", i=TB)[:, :, i * XH:(i + 1) * XH],
                             t["x"].rearrange("o (i p) d -> p (o i) d", p=P)[:, :, i * XH:(i + 1) * XH]
                             ).then_inc(s_xin[i], 16)
            with sp.Fori(0, L) as l:
                q = l * U_LAYER
                ffn(0, q, l, t["ffn1_wg"], t["ffn1_wu"], t["ffn1_wd"])
                c = U_FFN
                w = t["w_in"]
                for col in (V0, K0):
                    for k in (0, 4):
                        load(c, q, cols(w, l, k, k + 4, col))
                        c += 1
                for i in range(4):
                    slot_free(c, q)
                    d = dst(c, 0, KC)
                    for g in (1, 0):
                        src = w[ds(l, 1), :, Q0 + g * 4 * HD + i * HD:Q0 + g * 4 * HD + (i + 1) * HD]
                        sp.dma_start(d[:, :, g * HD:(g + 1) * HD],
                                     src.rearrange("o (k p) n -> p (o k) n", p=P)
                                     ).then_inc(landed[slot(c)], 32)
                    c += 1
                for i in range(CC):
                    for part in range(3):
                        load(c, q, cols(w, l, 0, KC, CB0 + part * CW + i * P))
                        c += 1
                for m in range(KC):
                    slot_free(c, q)
                    d = dst(c, 0, KC)
                    wo = t["w_out"]
                    for g in range(2):
                        src = wo[ds(l, 1), g * 4 * HD:(g + 1) * 4 * HD, m * P:(m + 1) * P]
                        sp.dma_start(d[g * HD:(g + 1) * HD, 0:4, :],
                                     src.rearrange("o (k p) n -> p (o k) n", p=HD)
                                     ).then_inc(landed[slot(c)], 16)
                    sp.dma_start(d[:, 4:8, :], cols(wo, l, 4, 8, m * P)).then_inc(landed[slot(c)], 32)
                    c += 1
                ffn(c, q, l, t["ffn2_wg"], t["ffn2_wu"], t["ffn2_wd"])


            def c2(w, k0, k1, j0, n=P):
                return w[0, k0 * P:k1 * P, ds(j0, n)].rearrange("(k p) n -> p k n", p=P)

            with nc.allow_non_contiguous_dma(reason="small vectors, one value per partition"):
                col = lambda v: v.rearrange("(c p) -> p c", p=P)
                gc = lambda j: gains[:, j * KC:(j + 1) * KC]
                for dest, v in ((gc(GX), t["norm_xattn_g_2"][0]),
                                (gc(GM), t["norm_mlp_g_2"][0]), (gc(GF), t["final_norm_g_2"]), (gc(GMEM), t["norm_mem_g_2"][0]),
                                (cvec[:, 0:CC], t["conv_b_2"][0]), (cvec[:, CC:2 * CC], t["conv_ln_g_2"][0]),
                                (cvec[:, 2 * CC:3 * CC], t["conv_ln_b_2"][0]), (lgain[:, 0:QC], t["q_norm_g_2"][0]),
                                (lgain[:, QC:QC + KVC], t["kv_norm_g_2"][0])):
                    sp.dma_start(dest, col(v)).then_inc(s_par2, 16)
                sp.dma_start(cw2[:, :], t["conv_w_2"][0].rearrange("t (c p) -> p (t c)", p=P)).then_inc(s_par2, 16)
                sp.dma_start(pos[:, :], t["positions_2"][0].partition_broadcast(P)).then_inc(s_par2, 16)
            w = t["w_in_2"]
            first = {"a": A0, "g": GT0, "q": CQ0, "kv": CKV0, "gate": GL0}
            for j, (kind, i) in enumerate(ORDER):
                c = C_IN + j
                if kind != "kr":
                    load(c, 0, c2(w, 0, KC, first[kind] + i * P))
                    continue
                slot_free(c, 0)
                d = dst(c, 0, KC)
                for a, col, n, inc in ((64, KR0, ROPE, 32), (96, KR0 + HALF, HALF, 16), (96 + HALF, KR0, HALF, 16)):
                    sp.dma_start(d[:, :, a:a + n], c2(w, 0, KC, col, n)).then_inc(landed[slot(c)], inc)
            vw = t["w_ukv_2"][0].rearrange("(k p) (h t n) -> p k h t n", p=P, t=2, n=HD)
            for h in range(H2):
                if h == 1:
                    slot_free(C_V2, 0)
                    a = slot(C_V2) * UNIT
                    for k in range(KVC):
                        sp.dma_start(raw[:, a + k * S:a + (k + 1) * S].rearrange("p (h n) -> p h n", n=HD),
                                     vw[:, k, :, 1, :]).then_inc(landed[slot(C_V2)], 32)
                c = head_unit(h)
                slot_free(c, 0)
                dq, dk = dst(c, 0, QC), dst(c, QC, QC + KVC)
                wq, r0 = t["w_uq_2"], h * QK + NOPE
                for a, col, n in ((0, h * QK, QK), (QK, r0 + HALF, HALF), (QK + HALF, r0, HALF)):
                    sp.dma_start(dq[:, :, a:a + n], c2(wq, 0, QC, col, n)).then_inc(landed[slot(c)], 16)
                sp.dma_start(dk, c2(t["w_ukv_2"], 0, KVC, h * P)).then_inc(landed[slot(c)], 16)
            for m in range(KC):
                c = C_MRG + m
                slot_free(c, 0)
                for a, w in ((0, "w_conv_out_2"), (4, "w_mla_out_2")):
                    sp.dma_start(dst(c, a, a + 4), c2(t[w], 0, 4, m * P)).then_inc(landed[slot(c)], 32)
            for m in range(KC):
                load(C_OUT + m, 0, c2(t["w_out_2"], 0, KC, m * P))
                if m == 0:
                    sp.wait_ge(s_used, C_MRG + 1)
                    sp.dma_start(memr[:, :].rearrange("p (i d) -> p i d", i=MB),
                                 t["mem_2"].rearrange("o (i p) d -> p (o i) d", p=P)).then_inc(s_memin, 16)
            for h in range(H3):
                load(C_XQ + h, 0, c2(t["w_xq_2"], 0, KC, h * P))
            for h in range(H3):
                load(C_XK + h, 0, c2(t["w_xkv_2"], 0, KC, h * P))
            for j in range(KC // 2):
                c = C_XV + j
                slot_free(c, 0)
                a = slot(c) * UNIT
                sp.dma_start(raw[:, a:a + UNIT].rearrange("p (k n) -> p k n", k=2),
                             c2(t["w_xkv_2"], 2 * j, 2 * j + 2, H3 * P, H3 * P)).then_inc(landed[slot(c)], LANDED)
            for j in range(KC // 2):
                c = C_XO + j
                slot_free(c, 0)
                for i in range(2):
                    sp.dma_start(dst(c, 4 * i, 4 * i + 4), c2(t["w_xo_2"], 0, 4, (2 * j + i) * P)
                                 ).then_inc(landed[slot(c)], 32)
            for ps in range(2):
                c0 = C_MLP + ps * U_PASS
                with sp.Fori(0, FP // 4) as it:
                    for j in range(4):
                        load(c0 + j, it * 4, c2(t["w_mlp1_2"], 0, KC, it * (4 * P) + (ps * FP + j) * P))
                with sp.Fori(0, KC // 2) as mi:
                    for m in range(2):
                        for j in range(2):
                            k0 = ps * FP + 8 * j
                            load(c0 + FP + 2 * m + j, mi * 4, c2(t["w_mlp2_2"], k0, k0 + 8, mi * (2 * P) + m * P))
            for j in range(AHEAD):
                load(C_END + j, 0, c2(t["w_out_2"], 0, KC, 0))

            ov = out.rearrange("o (i p) d -> p (o i) d", p=P)
            for n in range(2 * TB):
                hf, i = n // TB, n % TB
                sp.wait_ge(s_oc[n % 2], n // 2 + 1)
                sp.dma_start(ov[:, i, hf * 512:(hf + 1) * 512], yout[:, n * 512:(n + 1) * 512]).then_inc(s_out[n % 2], 16)
            for i in range(2):
                sp.wait_ge(s_out[i], 16 * TB)

        @block.tensor
        def _(pe):
            def unit(c, q, dest, tiles, rhs_hi, rhs_lo, start=True, stop=True, ready=None):
                pe.wait_ge(s_split, q + (c + 1 + RING))
                for k in range(tiles):
                    if ready is not None:
                        ready(k)
                    a, b_ = wcols(whi, c, k), wcols(wlo, c, k)
                    pe.matmul(dest, a, rhs_hi(k), start=start and k == 0, stop=False)
                    pe.matmul(dest, a, rhs_lo(k), start=False, stop=False)
                    mm = pe.matmul(dest, b_, rhs_hi(k), start=False, stop=stop and k == tiles - 1)
                mm.then_inc(s_used, 1)

            def norm_sum(N):
                pe.wait_ge(s_sq, N * KC + KC)
                pe.matmul(psO[:, :], ones[:, :], acc[:, :], start=True, stop=True).then_inc(s_ss, 1)

            def xk(k0=0):
                return (lambda k: chunk(xhi, k0 + k)), (lambda k: chunk(xlo, k0 + k))

            def ffn(c0, q0, N, fb):
                def pair(q, f, first):
                    for p in range(2):
                        c = c0 + 2 * p
                        ready = (lambda k: pe.wait_ge(s_xl, N * KC + (k + 1))) if first and p == 0 else None
                        unit(c, q, b(gate_b[p][:, :]), KC, *xk(), ready=ready)
                        if first and p == 0:
                            norm_sum(N)
                        unit(c + 1, q, b(up_b[p][:, :]), KC, *xk())
                pair(q0, fb, True)
                with pe.Fori(1, FC // 2) as it:
                    pair(q0 + it * 4, fb + it * 2, False)
                with pe.Fori(0, 2) as mi:
                    for m in range(4):
                        pe.wait_ge(s_x, (N + 1) * KC + mi * 4 + (m - 1) if m else (N + 1) * KC + mi * 4 - 1)
                        for j in range(3):
                            tiles = min(8, FC - 8 * j)
                            if m == 0:
                                pe.wait_ge(s_hl, fb + (8 * j + tiles))
                            unit(c0 + U_GU + 3 * m + j, q0 + mi * 12, down_b[m % 2], tiles,
                                 lambda k, j=j: chunk(hhi, 8 * j + k), lambda k, j=j: chunk(hlo, 8 * j + k),
                                 start=j == 0, stop=j == 2)

            def scores(l, s):
                blk, g = s // 2, s % 2
                n = P if blk == 0 else 2 * P
                k0 = max(blk - 1, 0) * P
                if s:
                    pe.wait_ge(a_bi, l * STEPS1 + s)
                for h in range(4):
                    dest = psS[:, h * 256:h * 256 + n]
                    rows = slice(g * HD, (g + 1) * HD)
                    qs = slice(h * S + blk * P, h * S + (blk + 1) * P)
                    ks = slice(k0, k0 + n)
                    pe.matmul(dest, qhi[rows, qs], khi[rows, ks], start=True, stop=False)
                    pe.matmul(dest, qhi[rows, qs], klo[rows, ks], start=False, stop=False)
                    mm = pe.matmul(dest, qlo[rows, qs], khi[rows, ks], start=False, stop=True)
                mm.then_inc(a_sc, 1)

            def turn(l, s):
                blk = s // 2
                n = 1 if blk == 0 else 2
                pe.wait_ge(a_pr, l * STEPS1 + s + 1)
                if s:
                    pe.wait_ge(a_tl, l * STEPS1 + s)
                for h in range(4):
                    for j in range(n):
                        mm = pe.transpose(psT[:, (h * n + j) * P:(h * n + j + 1) * P],
                                          sc[s % 2][:, h * 256 + j * P:h * 256 + (j + 1) * P], ident[:, :])
                mm.then_inc(a_tt, 1)

            def pv(l, s):
                blk = s // 2
                n = 1 if blk == 0 else 2
                pe.wait_ge(a_tl, l * STEPS1 + s + 1)
                if s:
                    pe.wait_ge(a_ol, l * STEPS1 + s)
                for h in range(4):
                    dest = psO[:, h * P:(h + 1) * P]
                    for j in range(n):
                        kb = blk - n + 1 + j
                        vs = slice(kb * P, (kb + 1) * P)
                        ps = slice((h * n + j) * P, (h * n + j + 1) * P)
                        pe.matmul(dest, vhi[:, vs], pthi[:, ps], start=j == 0, stop=False)
                        pe.matmul(dest, vhi[:, vs], ptlo[:, ps], start=False, stop=False)
                        mm = pe.matmul(dest, vlo[:, vs], pthi[:, ps], start=False, stop=j == n - 1)
                mm.then_inc(a_pv, 1)

            def mix(l, q, N):
                c = U_FFN
                ev = l * (6 + 3 * CC)
                for i, dest in ((0, bank[0]), (1, bank[1])):
                    for k0 in (0, 4):
                        ready = None
                        if i == 0:
                            ready = lambda k, k0=k0: pe.wait_ge(s_xl, N * KC + (k0 + k + 1))
                        unit(c, q, dest[:, :], 4, *xk(k0), start=k0 == 0, stop=k0 == 4, ready=ready)
                        c += 1
                        if i == 0 and k0 == 4:
                            norm_sum(N)
                for i in range(4):
                    if i == 1:
                        pe.wait_ge(s_vs, l + 1)
                    if i >= 2:
                        pe.wait_ge(s_qs, l * 5 + i - 1)
                    unit(c, q, bank[(2 + i) % 3][:, :], KC, *xk())
                    c += 1
                    if i == 1:
                        for j in range(TB):
                            mm = pe.transpose(psT[:, j * P:(j + 1) * P], tmp[0][:, j * P:(j + 1) * P], ident[:, :])
                        mm.then_inc(s_vt, 1)
                for u in range(3 * CC):
                    if u < 3:
                        pe.wait_ge(s_qs, l * 5 + min(3 + u, 5))
                    else:
                        pe.wait_ge(c_ev, l * 3 * CC + u - 2)
                    unit(c, q, bank[u % 3][:, :], KC, *xk())
                    c += 1
                    if 0 <= u - 3 < STEPS1:
                        pv(l, u - 3)
                    if 0 <= u - 2 < STEPS1:
                        turn(l, u - 2)
                    if u < STEPS1:
                        if u == 0:
                            pe.wait_ge(s_ql, l * 5 + 5)
                            pe.wait_ge(s_vl, l + 1)
                        scores(l, u)
                pe.wait_ge(a_ol, l * STEPS1 + STEPS1)
                for k0, k1 in ((0, KC - 1), (KC - 1, KC)):
                    for m in range(2):
                        pe.wait_ge(s_split, q + (c + m + 1 + RING))
                        for k in range(k0, k1):
                            if m == 0 and k >= 4:
                                pe.wait_ge(c_yl, l * CC + k - 3)
                            wh, wl = wcols(whi, c + m, k), wcols(wlo, c + m, k)
                            pe.matmul(down_b[m], wh, chunk(yhi, k), start=k == 0, stop=False)
                            pe.matmul(down_b[m], wh, chunk(ylo, k), start=False, stop=False)
                            mm = pe.matmul(down_b[m], wl, chunk(yhi, k), start=False, stop=k == KC - 1)
                        if k1 == KC:
                            mm.then_inc(s_used, 1)
                c += 2
                for m in range(2, KC):
                    pe.wait_ge(s_x, (N + 1) * KC + m - 1)
                    unit(c, q, down_b[m % 2], KC, lambda k: chunk(yhi, k), lambda k: chunk(ylo, k))
                    c += 1
                return c

            pe.wait_ge(s_const, 3)
            for c in range(KC):
                if c % 4 == 0:
                    pe.wait_ge(s_xin[c // 4], 16)
                if c >= 2:
                    pe.wait_ge(s_x, c - 1)
                for i in range(TB):
                    mm = pe.transpose(down_b[c % 2][:, i * P:(i + 1) * P],
                                      xin[:, i * D + c * P:i * D + (c + 1) * P], ident[:, :])
                mm.then_inc(s_xt, 1)
            with pe.Fori(0, L) as l:
                q = l * U_LAYER
                N = l * 3
                ffn(0, q, N, l * (2 * FC))
                c = mix(l, q, N + 1)
                ffn(c, q, N + 2, l * (2 * FC) + FC)

            def ones_sum(dest, terms):
                for i, a in enumerate(terms):
                    mm = pe.matmul(dest, ones[:, :], a, start=i == 0, stop=i == len(terms) - 1)
                return mm

            for u in range(IN_UNITS):
                ready = None
                if u == 0:
                    ready = lambda k: pe.wait_ge(s_xl, FINAL1 * KC + k + 1)
                unit(C_IN + u, 0, in_b[u % 5], KC, *xk(), ready=ready)
                if u == 0:
                    norm_sum(FINAL1)
                if u == 1:
                    pe.wait_ge(s_q7, KC)
                    ones_sum(psS[:, 0:S], [chunk(sq7, m) for m in range(KC)]).then_inc(s_ss, 1)
                if u == 6:
                    pe.wait_ge(s_fr, 3)
                    for i in range(2):
                        mm = pe.transpose(psS[:, 512 + i:513 + i], frow[0:1, i * P:(i + 1) * P], ident[0:1, 0:1])
                    mm.then_inc(s_ft, 1)
                if u == U_GATE + 2:
                    pe.wait_ge(s_lq, QC)
                    ones_sum(psO[:, :], [chunk(gates, KC + m) for m in range(QC)]).then_inc(s_ss, 1)
                if u == U_GATE + 3:
                    pe.wait_ge(s_lq, QC + KVC)
                    ones_sum(psS[:, 512:1024], [chunk(gates, KC + QC + m) for m in range(KVC)]).then_inc(s_ss, 1)

            pe.wait_ge(s_ll, QC + KVC)
            def project(h):
                c = head_unit(h)
                pe.wait_ge(s_split, c + 1 + RING)
                if h == 0:
                    pe.wait_ge(s_i2, IN_UNITS - 3)
                else:
                    pe.wait_ge(h_lo, h)
                for dest, k0, n, l0 in ((bank[0], 0, QC, 0), (bank[1], QC, KVC, QC)):
                    for k in range(n):
                        wh, wl = wcols(whi, c, k0 + k), wcols(wlo, c, k0 + k)
                        pe.matmul(dest[:, :], wh, chunk(lath, l0 + k), start=k == 0, stop=False)
                        pe.matmul(dest[:, :], wh, chunk(latl, l0 + k), start=False, stop=False)
                        mm = pe.matmul(dest[:, :], wl, chunk(lath, l0 + k), start=False, stop=k == n - 1)
                mm.then_inc(s_used, 1)

            def mla_scores(s):
                h, g = s // 2, s % 2 
                bb = h % 2 * S
                pe.wait_ge(h_lo, h + 1)
                if s == 0:
                    pe.wait_ge(s_mkr, 2)
                if s in (0, 2):
                    pe.wait_ge(s_krl, s + 2)
                if s:
                    pe.wait_ge(b_ex, s)
                for half, i in enumerate(BLOCKS[g]):
                    n = (i + 1) * P
                    dest = psS[:, half * 512:half * 512 + n]
                    qs, ks = slice(bb + i * P, bb + (i + 1) * P), slice(bb, bb + n)
                    pe.matmul(dest, q2h[:, qs], k2h[:, ks], start=True, stop=False)
                    pe.matmul(psS[:, half * 512 + i * P:half * 512 + (i + 1) * P], identr[:, :], maskr[:, :],
                              start=False, stop=False)
                    pe.matmul(dest, q2h[:, qs], k2l[:, ks], start=False, stop=False)
                    mm = pe.matmul(dest, q2l[:, qs], k2h[:, ks], start=False, stop=True)
                mm.then_inc(b_sc, 1)

            def mla_turn(s):
                pe.wait_ge(b_pr, s + 1)
                if s:
                    pe.wait_ge(b_tl, s)
                for j in range(TB + 1):
                    mm = pe.transpose(psT[:, j * P:(j + 1) * P], p2[s % 2][:, j * P:(j + 1) * P], ident[:, :])
                mm.then_inc(b_tt, 1)

            def mla_pv(s):
                h, g = s // 2, s % 2
                pe.wait_ge(b_tl, s + 1)
                if s:
                    pe.wait_ge(b_ol, s)
                j = 0
                for half, i in enumerate(BLOCKS[g]):
                    dest = psO[:, half * P:(half + 1) * P]
                    for k in range(i + 1):
                        vs = slice(k * S + h // 2 * P, k * S + (h // 2 + 1) * P)
                        ps = slice(j * P, (j + 1) * P)
                        pe.matmul(dest, v2h[:, vs], pt2h[:, ps], start=k == 0, stop=False)
                        pe.matmul(dest, v2h[:, vs], pt2l[:, ps], start=False, stop=False)
                        mm = pe.matmul(dest, v2l[:, vs], pt2h[:, ps], start=False, stop=k == i)
                        j += 1
                mm.then_inc(b_pv, 1)

            project(0)
            pe.wait_ge(s_split, C_V2 + 1 + RING)
            a = slot(C_V2) * UNIT
            for i in range(TB):
                if i >= 1:
                    pe.wait_ge(s_i2, IN_UNITS - 3 + i)
                dest = v2_b[i]
                for k in range(KVC):
                    lh, ll = chunk(lath, QC + k, i * P, P), chunk(latl, QC + k, i * P, P)
                    wh, wl = whi[:, a + k * S:a + (k + 1) * S], wlo[:, a + k * S:a + (k + 1) * S]
                    pe.matmul(dest, lh, wh, start=k == 0, stop=False)
                    pe.matmul(dest, lh, wl, start=False, stop=False)
                    mm = pe.matmul(dest, ll, wh, start=False, stop=k == KVC - 1)
                if i < TB - 1:
                    mm.then_inc(s_v2, 1)
            mm.then_inc(s_used, 1)

            for s in range(MLA_STEPS + 2):
                if s < MLA_STEPS:
                    mla_scores(s)
                if s == 2:
                    pe.wait_ge(s_v2l, TB)
                if s >= 2:
                    mla_pv(s - 2)
                if s % 2 == 0 and s // 2 + 1 < H2:
                    project(s // 2 + 1)
                if 1 <= s <= MLA_STEPS:
                    mla_turn(s - 1)
                if s == LN_MEAN - 1:
                    pe.wait_ge(s_tap, len(DVE_TAPS))
                    pe.wait_ge(s_pa, len(POOL_TAPS))
                    ones_sum(bank[2][:, :], [chunk(zc, i) for i in range(CC)]).then_inc(s_lsum, 1)
                if s == LN_VAR - 1:
                    for j, a in enumerate(ln_sq):
                        pe.wait_ge(s_lsq, j + 1)
                        mm = pe.matmul(bank[2][:, :], ones[:, :], a[:, :], start=j == 0, stop=j == CC - 1)
                    mm.then_inc(s_ss, 1)

            for m in range(KC):
                c = C_MRG + m
                pe.wait_ge(s_split, c + 1 + RING)
                if m == 0:
                    pe.wait_ge(s_cl, CC)
                    pe.wait_ge(b_ol, MLA_STEPS)
                else:
                    if m >= 2:
                        pe.wait_ge(s_ga, 2 * (m - 1))
                for j, dest, rh, rl in ((0, gate_b[m % 2], chi, clo), (1, up_b[m % 2], a2h, a2l)):
                    for k in range(4):
                        wh, wl = wcols(whi, c, 4 * j + k), wcols(wlo, c, 4 * j + k)
                        pe.matmul(b(dest[:, :]), wh, chunk(rh, k), start=k == 0, stop=False)
                        pe.matmul(b(dest[:, :]), wh, chunk(rl, k), start=False, stop=False)
                        mm = pe.matmul(b(dest[:, :]), wl, chunk(rh, k), start=False, stop=k == 3)
                mm.then_inc(s_used, 1)
            for m in range(KC):
                if m >= 2:
                    pe.wait_ge(s_x, (FINAL1 + 1) * KC + m - 1)
                ready = (lambda k: pe.wait_ge(s_mgl, k + 1)) if m == 0 else None
                unit(C_OUT + m, 0, down_b[m % 2], KC, lambda k: chunk(mgh, k), lambda k: chunk(mgl, k), ready=ready)
                if m in (2, 5):
                    r = m // 5
                    pe.wait_ge(s_mn, MB)
                    if r:
                        pe.wait_ge(s_ml, 4)
                    for i in range(4):
                        for j in range(MB):
                            cc = 4 * r + i
                            mm = pe.transpose(psS[:, i * ML + j * P:i * ML + (j + 1) * P],
                                              memr[:, j * D + cc * P:j * D + (cc + 1) * P], ident[:, :])
                    mm.then_inc(s_mt, 1)

            for j in range(H3):
                if j >= 3:
                    pe.wait_ge(s_x2, j - 2)
                ready = (lambda k: pe.wait_ge(s_xl, (FINAL1 + 1) * KC + k + 1)) if j == 0 else None
                unit(C_XQ + j, 0, bank[j % 3][:, :], KC, lambda k: chunk(xbh, k), lambda k: chunk(xbl, k), ready=ready)
                if j == 0:
                    pe.wait_ge(s_sq, (FINAL1 + 2) * KC)
                    pe.matmul(psO[:, :], ones[:, :], acc[:, :], start=True, stop=True).then_inc(s_ss, 1)
            pe.wait_ge(s_ml, KC)
            for j in range(H3):
                if j < 3:
                    pe.wait_ge(s_x2, 2 + j)
                else:
                    pe.wait_ge(s_k3l, j - 2)
                unit(C_XK + j, 0, bank[(H3 + j) % 3][:, 0:ML], KC,
                     lambda k: mth[:, k * ML:(k + 1) * ML], lambda k: mtl[:, k * ML:(k + 1) * ML])

            def cross_scores(s):
                if s:
                    pe.wait_ge(d_ex, s)
                else:
                    pe.wait_ge(s_k3l, H3)
                    pe.wait_ge(s_x2l, H3)
                for h in range(H3):
                    dest = psS[:, h * ML:(h + 1) * ML]
                    qs, ks = slice(h * S + s * P, h * S + (s + 1) * P), slice(h * ML, (h + 1) * ML)
                    pe.matmul(dest, q3h[:, qs], k3h[:, ks], start=True, stop=False)
                    pe.matmul(dest, q3h[:, qs], k3l[:, ks], start=False, stop=False)
                    mm = pe.matmul(dest, q3l[:, qs], k3h[:, ks], start=False, stop=True)
                mm.then_inc(d_sc, 1)

            def cross_v(j):
                c = C_XV + j
                pe.wait_ge(s_split, c + 1 + RING)
                a = slot(c) * UNIT
                for i in range(MB):
                    for k in range(2):
                        kk = 2 * j + k
                        ms = slice(kk * ML + i * P, kk * ML + (i + 1) * P)
                        ws = slice(a + k * S, a + (k + 1) * S)
                        dest = bank[2 * (1 - i)][:, :]
                        pe.matmul(dest, mth[:, ms], whi[:, ws], start=kk == 0, stop=False)
                        pe.matmul(dest, mth[:, ms], wlo[:, ws], start=False, stop=False)
                        mm = pe.matmul(dest, mtl[:, ms], whi[:, ws], start=False, stop=kk == KC - 1)
                mm.then_inc(s_used, 1)

            def cross_turn(s):
                pe.wait_ge(d_pr, s + 1)
                for j in range(8):
                    mm = pe.transpose(psT[:, j * P:(j + 1) * P], p3[s % 2][:, j * P:(j + 1) * P], ident[:, :])
                mm.then_inc(d_tt, 1)

            def cross_pv(s):
                pe.wait_ge(d_tl, s + 1)
                if s:
                    pe.wait_ge(d_ol, s)
                else:
                    pe.wait_ge(s_v3l, MB)
                for h in range(H3):
                    dest = psO[:, h * P:(h + 1) * P]
                    for j in range(MB):
                        vs = slice(j * S + h * P, j * S + (h + 1) * P)
                        ps = slice((h * MB + j) * P, (h * MB + j + 1) * P)
                        pe.matmul(dest, v3h[:, vs], pt3h[:, ps], start=j == 0, stop=False)
                        pe.matmul(dest, v3h[:, vs], pt3l[:, ps], start=False, stop=False)
                        mm = pe.matmul(dest, v3l[:, vs], pt3h[:, ps], start=False, stop=j == MB - 1)
                mm.then_inc(d_pv, 1)

            cross_scores(0)
            cross_v(0)
            cross_scores(1)
            cross_v(1)
            cross_v(2)
            cross_turn(0)
            cross_v(3)
            cross_scores(2)
            cross_pv(0)
            cross_turn(1)
            cross_scores(3)
            cross_pv(1)
            cross_turn(2)
            cross_pv(2)
            cross_turn(3)
            cross_pv(3)
            pe.wait_ge(d_ol, TB)
            for j in range(KC // 2):
                c = C_XO + j
                pe.wait_ge(s_split, c + 1 + RING)
                for i in range(2):
                    if j >= 2:
                        pe.wait_ge(s_x, (FINAL1 + 2) * KC + 2 * j + i - 3)
                    for k in range(4):
                        wh, wl = wcols(whi, c, 4 * i + k), wcols(wlo, c, 4 * i + k)
                        pe.matmul(xo_b[2 * (j % 2) + i], wh, chunk(a3h, k), start=k == 0, stop=False)
                        pe.matmul(xo_b[2 * (j % 2) + i], wh, chunk(a3l, k), start=False, stop=False)
                        mm = pe.matmul(xo_b[2 * (j % 2) + i], wl, chunk(a3h, k), start=False, stop=k == 3)
                mm.then_inc(s_used, 1)

            mlp_b = [bank[0][:, :], bank[1][:, :], bank[2][:, :], psS[:, 0:S]]
            for ps in range(2):
                c0 = C_MLP + ps * U_PASS

                def four(c, q, f, first):
                    for j in range(4):
                        ready = None
                        if first and ps == 0 and j == 0:
                            ready = lambda k: pe.wait_ge(s_xl, (FINAL1 + 2) * KC + k + 1)
                        unit(c + j, q, mlp_b[j], KC, *xk(), ready=ready)
                        if first and ps == 0 and j == 0:
                            pe.wait_ge(s_sq, (FINAL1 + 3) * KC)
                            pe.matmul(psO[:, :], ones[:, :], acc[:, :], start=True, stop=True).then_inc(s_ss, 1)
                four(c0, 0, ps * FP, True)
                with pe.Fori(1, FP // 4) as it:
                    four(c0, it * 4, it * 4 + ps * FP, False)
                with pe.Fori(0, KC // 2) as mi:
                    for m in range(2):
                        pe.wait_ge(s_x, mi * 2 + ((FINAL1 + 3 + ps) * KC + m - 1))
                        for j in range(2):
                            if m == 0:
                                pe.wait_ge(m_lo, ps * FP + 8 * j + 8)
                            unit(c0 + FP + 2 * m + j, mi * 4, down_b[m], 8,
                                 lambda k, j=j: chunk(mhi, 8 * j + k), lambda k, j=j: chunk(mlo, 8 * j + k),
                                 start=j == 0, stop=j == 1)
            for n in range(2 * TB):
                hf, i = n // TB, n % TB
                if n == 6:
                    pe.wait_ge(s_sq, (FINAL1 + 4) * KC)
                    for j in range(TB):
                        mm = pe.matmul(psO[:, j:j + 1], acc[:, j * P:(j + 1) * P], ones[:, 0:1], start=True, stop=True)
                    mm.then_inc(s_ss, 1)
                if n % TB == 0:
                    pe.wait_ge(s_o, 4 * hf + 4)
                if n == len(out_b):
                    pe.wait_ge(s_oc[0], 1)
                for c in range(4):
                    mm = pe.transpose(out_b[n % len(out_b)][:, c * P:(c + 1) * P],
                                      xg[:, (4 * hf + c) * S + i * P:(4 * hf + c) * S + (i + 1) * P], ident[:, :])
                mm.then_inc(s_ot, 1)

        @block.scalar
        def _(act):
            def split(c, q):
                act.wait_ge(landed[slot(c)], q * (LANDED // RING) + LANDED * (c // RING + 1))
                if c >= RING:
                    act.wait_ge(s_used, q + (c - RING + 1))
                a = slot(c) * UNIT
                act.activation(whi[:, a:a + UNIT], raw[:, a:a + UNIT], ACT.Copy).then_inc(s_hi, 1)

            def root(N, dest=inv):
                act.wait_ge(s_var, N + 1)
                act.activation(dest[:, :], var[:, :], ACT.Sqrt).then_inc(s_rt, 1)

            def x_hi(N, m, dest=xhi):
                act.wait_ge(s_x, N * KC + m + 1)
                act.activation(dest[:, ds(m * S, S)], x[:, ds(m * S, S)], ACT.Copy,
                               scale=gains[:, ds(N * KC + m, 1)]).then_inc(s_xh, 1)

            def ffn(c0, q0, N, fb):
                def pair(q, f, fi, first):
                    for p in range(2):
                        c = c0 + 2 * p
                        split(c + AHEAD, q)
                        if first and p == 0:
                            root(N)
                        act.wait_ge(s_gs, f + p + 1)
                        act.activation(tmp[p][:, :], tmp[p][:, :], ACT.Silu).then_inc(s_si, 1)
                        split(c + 1 + AHEAD, q)
                        act.wait_ge(s_h, f + p + 1)
                        act.activation(hhi[:, ds((fi + p) * S, S)], tmp[2 + p][:, :], ACT.Copy).then_inc(s_hh, 1)
                pair(q0, fb, 0, True)
                with act.Fori(1, FC // 2) as it:
                    pair(q0 + it * 4, fb + it * 2, it * 2, False)
                act.wait_ge(s_par, 16 * 8)
                with act.Fori(0, 2) as mi:
                    for m in range(4):
                        for j in range(3):
                            split(c0 + U_GU + 3 * m + j + AHEAD, q0 + mi * 12)
                        x_hi(N + 1, mi * 4 + m)

            def mix(l, q, N):
                act.wait_ge(s_g67, l + 1)
                c = U_FFN
                split(c + AHEAD, q)
                split(c + 1 + AHEAD, q)
                root(N)
                c += 2
                for i in range(5):
                    for _ in range(2 if i == 0 else 1):
                        split(c + AHEAD, q)
                        c += 1
                    if i == 2:
                        act.wait_ge(s_vt, l + 1)
                        act.activation(vhi[:, :], psT[:, 0:S], ACT.Copy).then_inc(s_vh, 1)
                    act.wait_ge(s_qs, l * 5 + i + 1)
                    dest = khi[:, :] if i == 0 else chunk(qhi, i - 1)
                    act.activation(dest, tmp[1 + i % 2][:, :], ACT.Copy).then_inc(s_qh, 1)
                for u in range(3 * CC + 1):
                    if u < 3 * CC:
                        split(c + AHEAD, q)
                        c += 1
                    if 0 <= u - 3 < STEPS1:
                        s = u - 3
                        blk, g = s // 2, s % 2
                        act.wait_ge(a_pv, l * STEPS1 + s + 1)
                        rows = slice(g * HD, (g + 1) * HD)
                        act.activation(yhi[rows, 0:4 * S].rearrange("p (c n) -> p c n", c=4)[:, :, blk * P:(blk + 1) * P],
                                       psO[rows, :].rearrange("p (c n) -> p c n", c=4), ACT.Copy).then_inc(a_oh, 1)
                    if 0 <= u - 2 < STEPS1:
                        s = u - 2
                        n = 512 if s < 2 else 1024
                        act.wait_ge(a_tt, l * STEPS1 + s + 1)
                        act.activation(pthi[:, 0:n], psT[:, 0:n], ACT.Copy).then_inc(a_th, 1)
                    if u < STEPS1:
                        n = P if u < 2 else 2 * P
                        act.wait_ge(a_sd, l * STEPS1 + u + 1)
                        for h in range(4):
                            a = sc[u % 2][:, h * 256:h * 256 + n]
                            act.activation(a, a, ACT.Exp, bias=st[:, 4 + h:5 + h], accum_out=st[:, 12 + h:13 + h])
                        act.activation(st[:, 16:20], st[:, 8:12], ACT.Exp).then_inc(a_ex, 1)
                    if u % 3 == 0 and u >= 3:
                        i = u // 3 - 1
                        act.wait_ge(c_u, l * CC + i + 1)
                        act.activation(cy[i % 2][:, :], upad[i % 2][:, 2:2 + S], ACT.Copy,
                                       scale=cw1[:, ds(l * (3 * CC) + 2 * CC + i, 1)]).then_inc(c_t2, 1)
                    if (u % 3 == 1 and u >= 4) or u == 3 * CC:
                        i = u // 3 - 1
                        act.wait_ge(c_y, l * CC + i + 1)
                        act.activation(chunk(yhi, 4 + i), cy[i % 2][:, :], ACT.Copy).then_inc(c_yh, 1)
                for m in range(KC):
                    split(c + AHEAD, q)
                    c += 1
                    x_hi(N + 1, m)
                return c

            with nc.allow_non_contiguous_dma(reason="small vectors, one value per partition"):
                gv = gains[:, 0:6 * KC].rearrange("p (l j c) -> p l j c", l=L, j=3)
                names = ("ffn1_norm", "mix_norm", "ffn2_norm")
                gain = lambda l, j: act.dma_start(gv[:, l, j, :], t[names[j]][l, :].rearrange("(c p) -> p c", p=P))
                gain(0, 0).then_inc(s_first, 16)
                act.dma_start(sink[:, :], t["attn_sink"].rearrange("l h -> (l h)").partition_broadcast(P)).then_inc(s_first, 16)
                for l, j in ((0, 1), (0, 2), (1, 0), (1, 1), (1, 2)):
                    gain(l, j).then_inc(s_par, 16)
                for j, v in ((G6, t["final_norm"]), (G7, t["norm_mix_g_2"][0])):
                    act.dma_start(gains[:, j * KC:(j + 1) * KC], v.rearrange("(c p) -> p c", p=P)).then_inc(s_par, 16)
                act.dma_start(cw1[:, :], t["conv_w"].rearrange("l t (c p) -> p (l t c)", p=P)).then_inc(s_par, 16)
            for c in range(AHEAD):
                act.wait_ge(landed[c], LANDED)
                a = c * UNIT
                act.activation(whi[:, a:a + UNIT], raw[:, a:a + UNIT], ACT.Copy).then_inc(s_hi, 1)
            act.wait_ge(s_first, 16 * 2)
            for m in range(KC):
                x_hi(0, m)
            with act.Fori(0, L) as l:
                q = l * U_LAYER
                N = l * 3
                ffn(0, q, N, l * (2 * FC))
                c = mix(l, q, N + 1)
                ffn(c, q, N + 2, l * (2 * FC) + FC)

            act.wait_ge(s_par2, 16 * PAR2)
            for m in range(KC):
                act.activation(chunk(sq7, m), chunk(x, m), ACT.Square,
                               scale=gains[:, G6 * KC + m:G6 * KC + m + 1]).then_inc(s_q7, 1)
            taps = [(i, k) for i in (1, 3) for k in range(TAPS)]
            done = adds = 0
            for u, (kind, i) in enumerate(ORDER):
                if u == 0:
                    split(C_IN + AHEAD, 0)
                    split(C_IN + 1 + AHEAD, 0)
                    root(FINAL1, inv6)
                    root(SUM7)
                if u >= 2:
                    split(C_IN + u + AHEAD, 0)
                if 4 <= u <= TAP_LAST:
                    left = TAP_LAST + 1 - u
                    for _ in range(-(-(len(taps) - done) // left)):
                        ci, k = taps[done]
                        if k == 0:
                            act.wait_ge(s_z, ci + 1)
                            act.wait_ge(s_zp, 1)
                        z = chunk_z(ci, k)
                        wk = cw2[:, k * CC + ci:k * CC + ci + 1]
                        if k == 0:
                            act.activation(chunk(zc, ci), z, ACT.Identity, bias=cvec[:, ci:ci + 1], scale=wk).then_inc(s_pm, 1)
                        else:
                            if adds >= 2:
                                act.wait_ge(s_pa, adds - 1)
                            prod = (acc, sqt)[adds % 2]
                            act.activation(prod[:, :], z, ACT.Copy, scale=wk).then_inc(s_pm, 1)
                            adds += 1
                        done += 1
                if kind in ("g", "q", "kv", "gate"):
                    act.wait_ge(s_i2, u + 1)
                if kind == "g":
                    g = tmp[2 + i % 2][:, :]
                    act.activation(g, g, ACT.Tanh, scale=0.5).then_inc(s_th, 1)
                if kind in ("q", "kv"):
                    j = i + (QC if kind == "kv" else 0)
                    act.activation(chunk(gates, KC + j), chunk(latf, j), ACT.Square).then_inc(s_lq, 1)
                if kind == "gate":
                    act.activation(chunk(gates, i), chunk(gates, i), ACT.Tanh, scale=0.5).then_inc(s_gt, 1)
                if u in (4, 5):
                    for m in range(4 * (u - 4), 4 * (u - 3)):
                        act.activation(chunk(x, m), chunk(x, m), ACT.Copy,
                                       scale=gains[:, G6 * KC + m:G6 * KC + m + 1]).then_inc(s_xg, 1)
                if u == 10:
                    act.wait_ge(s_rr, 1)
                    for r in (64, 96):
                        act.activation(rope[r:r + 32, :], rope[r:r + 32, :], ACT.Sin).then_inc(s_rs, 1)
                if u == U_GATE + 3:
                    root(LATQ, tmp[2])
                if u == U_GATE + 5:
                    root(LATKV, tmp[3])
                if LAT <= u < LAT + QC + KVC:
                    j = u - LAT
                    act.wait_ge(s_ln, j + 1)
                    act.activation(chunk(lath, j), chunk(latf, j), ACT.Copy).then_inc(s_lh, 1)

            act.wait_ge(s_kr, 3)
            def k_rope(j):
                for r in (NOPE, QK):
                    act.activation(k2h[r:r + ROPE, j * S:(j + 1) * S], tmp[1][NOPE:QK, :], ACT.Copy).then_inc(s_krh, 1)

            k_rope(0)

            def head(h):
                bb = h % 2 * S
                split(head_unit(h) + AHEAD, 0)
                act.wait_ge(s_used, head_unit(h) + 1)
                act.activation(tmp[0][0:NOPE, :], bank[0][0:NOPE, :], ACT.Copy).then_inc(h_cp, 1)
                act.activation(k2h[0:NOPE, bb:bb + S], bank[1][0:NOPE, :], ACT.Copy).then_inc(h_hi, 1)

            def head_q(h):
                bb = h % 2 * S
                act.wait_ge(h_rp, h + 1)
                act.wait_ge(h_cp, h + 1)
                act.activation(q2h[:, bb:bb + S], tmp[0][:, :], ACT.Copy, scale=QK ** -0.5).then_inc(h_hi, 1)

            head(0)
            head_q(0)
            split(C_V2 + AHEAD, 0)
            for i in range(TB):
                if i < TB - 1:
                    act.wait_ge(s_v2, i + 1)
                else:
                    act.wait_ge(s_used, C_V2 + 1)
                act.activation(chunk(v2h, i), v2_b[i], ACT.Copy).then_inc(s_v2h, 1)
            k_rope(1)
            act.wait_ge(s_mk, 2)
            for a, dest in ((ident, identr), (mask, maskr)):
                act.activation(dest[:, :], a[:, :], ACT.Copy).then_inc(s_mkr, 1)
            act.wait_ge(s_pa, len(POOL_TAPS))
            for s in range(MLA_STEPS + 2):
                if s < MLA_STEPS:
                    o, pc = 0, s % 2 * 8
                    act.wait_ge(b_mx, s + 1)
                    for half, i in enumerate(BLOCKS[s % 2]):
                        n = (i + 1) * P
                        e = act.activation(p2[s % 2][:, o:o + n], psS[:, half * 512:half * 512 + n], ACT.Exp,
                                           bias=st2[:, pc + half:pc + half + 1], accum_out=st2[:, pc + 2 + half:pc + 3 + half])
                        o += n
                    e.then_inc(b_ex, 1)
                if s >= 2:
                    r = s - 2
                    h, (i1, i2) = r // 2, BLOCKS[r % 2]
                    rows = slice(h % 2 * HD, h % 2 * HD + HD)
                    act.wait_ge(b_pv, r + 1)
                    act.activation(chunk(a2h, h // 2)[rows].rearrange("p (i n) -> p i n", n=P)[:, i1:i2 + 1:i2 - i1, :],
                                   psO[rows, 0:2 * P].rearrange("p (i n) -> p i n", n=P), ACT.Copy).then_inc(b_oh, 1)
                if s % 2 == 0 and s // 2 + 1 < H2:
                    head(s // 2 + 1)
                if 1 <= s <= MLA_STEPS:
                    act.wait_ge(b_tt, s)
                    act.activation(pt2h[:, :], psT[:, 0:(TB + 1) * P], ACT.Copy).then_inc(b_th, 1)
                if s % 2 == 0 and s // 2 + 1 < H2:
                    head_q(s // 2 + 1)
                if s == LN_MEAN + 1:
                    for j, d in enumerate(ln_sq):
                        act.wait_ge(s_ld, j + 1)
                        act.activation(d[:, :], chunk(zc, j), ACT.Square).then_inc(s_lsq, 1)
                if s == LN_VAR:
                    root(LNVAR, inv6)
                if s == LN_Y + 2:
                    for i in range(CC):
                        z = chunk(zc, i)
                        act.wait_ge(s_ly, i + 1)
                        act.activation(z, z, ACT.Silu, bias=cvec[:, 2 * CC + i:2 * CC + i + 1],
                                       scale=cvec[:, CC + i:CC + i + 1]).then_inc(s_lc, 1)
                if s == LN_Y + 3:
                    for i in range(CC):
                        act.wait_ge(s_lc, i + 1)
                        act.activation(chunk(chi, i), chunk(zc, i), ACT.Copy).then_inc(s_ch, 1)

            for m in range(KC):
                split(C_MRG + m + AHEAD, 0)
                act.wait_ge(s_mg, m + 1)
                act.activation(chunk(mgh, m), tmp[2 + m % 2][:, :], ACT.Copy, scale=0.5).then_inc(s_mgh, 1)
            for m in range(KC):
                split(C_OUT + m + AHEAD, 0)
                if m == 1:
                    act.wait_ge(s_memin, 16)
                    for i in range(MB):
                        e = act.activation(mscr[:, i * D:(i + 1) * D], memr[:, i * D:(i + 1) * D], ACT.Square,
                                           accum_out=st2[:, 16 + i:17 + i])
                    e.then_inc(s_msq, 1)
                    act.wait_ge(s_mst, 1)
                    act.activation(st2[:, 20:22], st2[:, 18:20], ACT.Sqrt).then_inc(s_mr, 1)
                if m in (3, 6):
                    r = m // 6
                    act.wait_ge(s_mt, r + 1)
                    for i in range(4):
                        cc = 4 * r + i
                        act.activation(mth[:, cc * ML:(cc + 1) * ML], psS[:, i * ML:(i + 1) * ML], ACT.Copy,
                                       scale=gains[:, GMEM * KC + cc:GMEM * KC + cc + 1]).then_inc(s_mh, 1)
                x_hi(FINAL1 + 1, m, xbh)

            for j in range(H3):
                split(C_XQ + j + AHEAD, 0)
                if j == 0:
                    root(XATTN)
                act.wait_ge(s_x2, j + 1)
                act.activation(chunk(q3h, j), tmp[j % 2][:, :], ACT.Copy).then_inc(s_x2h, 1)
            for j in range(H3):
                split(C_XK + j + AHEAD, 0)
                act.wait_ge(s_used, C_XK + j + 1)
                act.activation(k3h[:, j * ML:(j + 1) * ML], bank[(H3 + j) % 3][:, 0:ML], ACT.Copy).then_inc(s_k3h, 1)

            def cross_exp(s):
                pc = s % 2 * 16
                act.wait_ge(d_mx, s + 1)
                for h in range(H3):
                    hs = slice(h * ML, (h + 1) * ML)
                    e = act.activation(p3[s % 2][:, hs], psS[:, hs], ACT.Exp, bias=st[:, pc + h:pc + h + 1],
                                       accum_out=st[:, pc + 4 + h:pc + 5 + h])
                e.then_inc(d_ex, 1)

            def cross_hi(s):
                act.wait_ge(d_tt, s + 1)
                act.activation(pt3h[:, :], psT[:, :], ACT.Copy).then_inc(d_th, 1)

            def cross_out(s):
                act.wait_ge(d_pv, s + 1)
                act.activation(a3h[:, :].rearrange("p (h n) -> p h n", h=H3)[:, :, s * P:(s + 1) * P],
                               psO[:, :].rearrange("p (h n) -> p h n", h=H3), ACT.Copy).then_inc(d_oh, 1)

            cross_exp(0)
            split(C_XV + AHEAD, 0)
            cross_exp(1)
            split(C_XV + 1 + AHEAD, 0)
            split(C_XV + 2 + AHEAD, 0)
            cross_hi(0)
            split(C_XV + 3 + AHEAD, 0)
            act.wait_ge(s_used, C_XV + KC // 2)
            for i in range(MB):
                act.activation(chunk(v3h, i), bank[2 * (1 - i)][:, :], ACT.Copy).then_inc(s_v3h, 1)
            cross_exp(2)
            cross_out(0)
            cross_hi(1)
            cross_exp(3)
            cross_out(1)
            cross_hi(2)
            cross_out(2)
            cross_hi(3)
            cross_out(3)
            for j in range(KC // 2):
                split(C_XO + j + AHEAD, 0)
                for i in range(2):
                    x_hi(FINAL1 + 2, 2 * j + i)

            for ps in range(2):
                c0 = C_MLP + ps * U_PASS

                def four(c, q, fi, first):
                    for j in range(4):
                        split(c + j + AHEAD, q)
                        if first and ps == 0 and j == 0:
                            root(MLPN)
                        f = fi + (ps * FP + j)
                        act.wait_ge(m_r, f + 1)
                        act.activation(tmp[2 + j % 2][:, :], tmp[j % 2][:, :], ACT.Square).then_inc(m_sq, 1)
                        act.wait_ge(m_sq, f + 1)
                        act.activation(mhi[:, ds((fi + j) * S, S)], tmp[2 + j % 2][:, :], ACT.Copy).then_inc(m_hi, 1)
                four(c0, 0, 0, True)
                with act.Fori(1, FP // 4) as it:
                    four(c0, it * 4, it * 4, False)
                with act.Fori(0, KC // 2) as mi:
                    for j in range(4):
                        split(c0 + FP + j + AHEAD, mi * 4)
                        if ps and j % 2:
                            act.wait_ge(s_x, mi * 2 + ((FINAL1 + 4) * KC + j // 2 + 1))
                            act.activation(xg[:, ds(mi * (2 * S) + j // 2 * S, S)], x[:, ds(mi * (2 * S) + j // 2 * S, S)],
                                           ACT.Copy, scale=gains[:, ds(mi * 2 + (GF * KC + j // 2), 1)]).then_inc(s_o, 1)
            act.wait_ge(s_fv, 1)
            act.activation(fin[:, TB:2 * TB], fin[:, 0:TB], ACT.Sqrt).then_inc(s_rt, 1)
            act.wait_ge(s_fv, 6)
            for n in range(1, 2 * TB, 2):
                act.wait_ge(s_ot, n + 1)
                act.activation(yout[:, n * 512:(n + 1) * 512], out_b[n % len(out_b)], ACT.Copy,
                               scale=fin[:, TB + n % TB:TB + n % TB + 1]).then_inc(s_oc[1], 1)

        @block.vector
        def _(dve):
            def split(c, q):
                dve.wait_ge(s_hi, q + c + 1)
                a = slot(c) * UNIT
                dve.tensor_tensor(wlo[:, a:a + UNIT], raw[:, a:a + UNIT], whi[:, a:a + UNIT].bitcast(F32),
                                  ALU.subtract).then_inc(s_split, 1)

            def variance(N, total, n):
                dve.wait_ge(s_ss, N + 1)
                dve.tensor_scalar(var[:, :], total, 1.0 / n, EPS, ALU.mult, ALU.add).then_inc(s_var, 1)

            def inverse(N, dest=inv):
                variance(N, psO[:, :], D)
                newton(N, dest)

            def newton(N, dest):
                dve.wait_ge(s_rt, N + 1)
                dve.reciprocal(dest[:, :], dest[:, :]).then_inc(s_nst, 1)
                dve.wait_ge(s_nst, N * 4 + 1)
                dve.tensor_tensor(var[:, :], var[:, :], dest[:, :], ALU.mult).then_inc(s_nst, 1)
                dve.wait_ge(s_nst, N * 4 + 2)
                dve.tensor_tensor(var[:, :], var[:, :], dest[:, :], ALU.mult).then_inc(s_nst, 1)
                dve.wait_ge(s_nst, N * 4 + 3)
                dve.tensor_scalar(var[:, :], var[:, :], -0.5, 1.5, ALU.mult, ALU.add).then_inc(s_nst, 1)
                dve.wait_ge(s_nst, N * 4 + 4)
                dve.tensor_tensor(dest[:, :], var[:, :], dest[:, :], ALU.mult).then_inc(s_inv, 1)
                dve.wait_ge(s_inv, N + 1)

            def x_lo(N, m, lo=xlo, hi=xhi):
                dve.wait_ge(s_xh, N * KC + m + 1)
                dve.scalar_tensor_tensor(lo[:, ds(m * S, S)], x[:, ds(m * S, S)], gains[:, ds(N * KC + m, 1)],
                                         hi[:, ds(m * S, S)].bitcast(F32), ALU.mult, ALU.subtract).then_inc(s_xl, 1)

            def ffn(c0, q0, N, fb):
                def pair(q, f, fi, first):
                    for p in range(2):
                        c = c0 + 2 * p
                        split(c + AHEAD, q)
                        if first and p == 0:
                            inverse(N)
                        dve.wait_ge(s_used, q + c + 1)
                        dve.tensor_tensor(tmp[p][:, :], b(gate_b[p][:, :]), inv[:, :], ALU.mult).then_inc(s_gs, 1)
                        split(c + 1 + AHEAD, q)
                        dve.wait_ge(s_used, q + c + 2)
                        dve.tensor_tensor(tmp[2 + p][:, :], b(up_b[p][:, :]), inv[:, :], ALU.mult).then_inc(s_us, 1)
                        dve.wait_ge(s_us, f + p + 1)
                        dve.wait_ge(s_si, f + p + 1)
                        dve.tensor_tensor(tmp[2 + p][:, :], tmp[2 + p][:, :], tmp[p][:, :], ALU.mult).then_inc(s_h, 1)
                        dve.wait_ge(s_hh, f + p + 1)
                        dve.tensor_tensor(hlo[:, ds((fi + p) * S, S)], tmp[2 + p][:, :],
                                          hhi[:, ds((fi + p) * S, S)].bitcast(F32), ALU.subtract).then_inc(s_hl, 1)
                pair(q0, fb, 0, True)
                with dve.Fori(1, FC // 2) as it:
                    pair(q0 + it * 4, fb + it * 2, it * 2, False)
                dve.wait_ge(s_par, 16 * 8)
                with dve.Fori(0, 2) as mi:
                    for m in range(4):
                        for j in range(3):
                            split(c0 + U_GU + 3 * m + j + AHEAD, q0 + mi * 12)
                        dve.wait_ge(s_used, q0 + mi * 12 + (c0 + U_GU + 3 * m + 3))
                        xm = x[:, ds((mi * 4 + m) * S, S)]
                        dve.scalar_tensor_tensor(xm, down_b[m % 2], 0.5, xm, ALU.mult, ALU.add).then_inc(s_x, 1)
                        x_lo(N + 1, mi * 4 + m)

            def mix(l, q, N):
                dve.tensor_tensor(gains[:, G67 * KC:(G67 + 1) * KC], gains[:, G6 * KC:(G6 + 1) * KC],
                                  gains[:, G7 * KC:(G7 + 1) * KC], ALU.mult).then_inc(s_g67, 1)
                c = U_FFN
                split(c + AHEAD, q)
                split(c + 1 + AHEAD, q)
                inverse(N)
                dve.wait_ge(s_used, q + c + 2)
                dve.tensor_tensor(tmp[0][:, :], bank[0][:, :], inv[:, :], ALU.mult).then_inc(s_vs, 1)
                c += 2
                for i in range(5):
                    for _ in range(2 if i == 0 else 1):
                        split(c + AHEAD, q)
                        c += 1
                    dve.wait_ge(s_used, q + c)
                    dve.scalar_tensor_tensor(tmp[1 + i % 2][:, :], bank[(1 + i) % 3][:, :], HD ** -0.5 if i else 1.0,
                                             inv[:, :], ALU.mult, ALU.mult).then_inc(s_qs, 1)
                    if i == 2:
                        dve.wait_ge(s_vh, l + 1)
                        dve.tensor_tensor(vlo[:, :], psT[:, 0:S], vhi[:, :].bitcast(F32), ALU.subtract).then_inc(s_vl, 1)
                    dve.wait_ge(s_qh, l * 5 + i + 1)
                    hi = khi[:, :] if i == 0 else chunk(qhi, i - 1)
                    lo = klo[:, :] if i == 0 else chunk(qlo, i - 1)
                    dve.tensor_tensor(lo, tmp[1 + i % 2][:, :], hi.bitcast(F32), ALU.subtract).then_inc(s_ql, 1)
                for i in range(2):
                    last = dve.memset(upad[i][:, 0:2], 0.0)
                last.then_inc(s_pad, 1)
                for u in range(3 * CC + 1):
                    if u < 3 * CC:
                        split(c + AHEAD, q)
                    if 1 <= u and u - 1 < STEPS1:
                        s = l * STEPS1 + (u - 1)
                        dve.wait_ge(a_ex, s + 1)
                        dve.tensor_tensor(st[:, 20:24], st[:, 12:16], st[:, 16:20], ALU.add).then_inc(a_dn, 1)
                        dve.wait_ge(a_dn, s + 1)
                        r = 24 + 4 * ((u - 1) % 2)
                        dve.reciprocal(st[:, r:r + 4], st[:, 20:24]).then_inc(a_rd, 1)
                    if u < 3 * CC:
                        dve.wait_ge(s_used, q + c + 1)
                        c += 1
                        if u % 3 == 0 and u >= 6:
                            dve.wait_ge(c_y, l * CC + u // 3 - 1)
                        dest = tmp[(0, 1)[u // 3 % 2] if u % 3 == 0 else 1 + u % 3]
                        if u % 3 and u >= 3:
                            dve.wait_ge(c_u, l * CC + u // 3)
                        dve.tensor_tensor(dest[:, :], bank[u % 3][:, :], inv[:, :], ALU.mult).then_inc(c_ev, 1)
                    if 0 <= u - 3 < STEPS1:
                        s = u - 3
                        blk, g = s // 2, s % 2
                        dve.wait_ge(a_oh, l * STEPS1 + s + 1)
                        rows = slice(g * HD, (g + 1) * HD)
                        ys = slice(blk * P, (blk + 1) * P)
                        dve.tensor_tensor(ylo[rows, 0:4 * S].rearrange("p (c n) -> p c n", c=4)[:, :, ys],
                                          psO[rows, :].rearrange("p (c n) -> p c n", c=4),
                                          yhi[rows, 0:4 * S].bitcast(F32).rearrange("p (c n) -> p c n", c=4)[:, :, ys],
                                          ALU.subtract).then_inc(a_ol, 1)
                    if 0 <= u - 2 < STEPS1:
                        s = u - 2
                        n = 512 if s < 2 else 1024
                        dve.wait_ge(a_th, l * STEPS1 + s + 1)
                        dve.tensor_tensor(ptlo[:, 0:n], psT[:, 0:n], pthi[:, 0:n].bitcast(F32),
                                          ALU.subtract).then_inc(a_tl, 1)
                    if u < STEPS1:
                        s = l * STEPS1 + u
                        g = u % 2
                        n = P if u < 2 else 2 * P
                        dve.wait_ge(a_sc, s + 1)
                        for h in range(4):
                            slope = 2.0 ** (-8.0 * (g * 4 + h + 1) / H1)
                            a = sc[u % 2][:, h * 256:h * 256 + n]
                            last = dve.scalar_tensor_tensor(a, dist[:, 2 * P - n:2 * P], -slope, psS[:, h * 256:h * 256 + n],
                                                            ALU.mult, ALU.add)
                        last.then_inc(a_bi, 1)
                        dve.wait_ge(a_bi, s + 1)
                        dve.tensor_reduce(st[:, 0:4], sc[u % 2][:, :].rearrange("p (h n) -> p h n", h=4)[:, :, 0:n],
                                          AX.X, ALU.max, negate=True).then_inc(a_rm, 1)
                        dve.wait_ge(a_rm, s + 1)
                        ns = nsink[:, ds(l * H1 + g * 4, 4)]
                        dve.tensor_tensor(st[:, 4:8], st[:, 0:4], ns, ALU.min).then_inc(a_mx, 1)
                        dve.wait_ge(a_mx, s + 1)
                        dve.tensor_tensor(st[:, 8:12], st[:, 4:8], ns, ALU.subtract).then_inc(a_sd, 1)
                    if u % 3 == 0 and u >= 3:
                        i = u // 3 - 1
                        y = cy[i % 2][:, :]
                        dve.wait_ge(c_t2, l * CC + i + 1)
                        dve.scalar_tensor_tensor(y, upad[i % 2][:, 1:1 + S], cw1[:, ds(l * (3 * CC) + CC + i, 1)], y,
                                                 ALU.mult, ALU.add).then_inc(c_t1, 1)
                        dve.wait_ge(c_t1, l * CC + i + 1)
                        dve.scalar_tensor_tensor(y, upad[i % 2][:, 0:S], cw1[:, ds(l * (3 * CC) + i, 1)], y,
                                                 ALU.mult, ALU.add).then_inc(c_t0, 1)
                    if (u % 3 == 1 and u >= 4) or u == 3 * CC:
                        i = u // 3 - 1
                        y = cy[i % 2][:, :]
                        dve.wait_ge(c_yh, l * CC + i + 1)
                        dve.tensor_tensor(chunk(ylo, 4 + i), y, chunk(yhi, 4 + i).bitcast(F32),
                                          ALU.subtract).then_inc(c_yl, 1)
                for m in range(KC):
                    split(c + AHEAD, q)
                    c += 1
                    dve.wait_ge(s_used, q + c)
                    dve.tensor_tensor(chunk(x, m), down_b[m % 2], chunk(x, m), ALU.add).then_inc(s_x, 1)
                    x_lo(N + 1, m)
                return c

            dve.memset(ones[:, :], 1.0).then_inc(s_const, 1)
            dve.memset(st[:, :], 0.0).then_inc(s_split, RING)
            for c in range(KC):
                dve.wait_ge(s_xt, c + 1)
                dve.tensor_copy(chunk(x, c), down_b[c % 2]).then_inc(s_x, 1)
            for c in range(AHEAD):
                split(c, 0)
            dve.wait_ge(s_first, 16 * 2)
            dve.tensor_scalar(nsink[:, :], sink[:, :], -1.0, None, ALU.mult).then_inc(s_ns, 1)
            dve.wait_ge(s_ns, 1)
            dve.wait_ge(s_const, 3)
            for m in range(KC):
                x_lo(0, m)
            with dve.Fori(0, L) as l:
                q = l * U_LAYER
                N = l * 3
                ffn(0, q, N, l * (2 * FC))
                c = mix(l, q, N + 1)
                ffn(c, q, N + 2, l * (2 * FC) + FC)

            dve.wait_ge(s_par2, 16 * PAR2)
            split(C_IN + AHEAD, 0)
            split(C_IN + 1 + AHEAD, 0)
            inverse(FINAL1, dest=inv6)
            dve.wait_ge(s_ss, SUM7 + 1)
            dve.tensor_scalar(var[:, :], psS[:, 0:S], 1.0 / D, None, ALU.mult).then_inc(s_v7, 1)
            for j in range(2):
                dve.wait_ge(s_v7, j + 1)
                dve.tensor_tensor(var[:, :], var[:, :], inv6[:, :], ALU.mult).then_inc(s_v7, 1)
            dve.wait_ge(s_v7, 3)
            dve.tensor_scalar(var[:, :], var[:, :], EPS, None, ALU.add).then_inc(s_var, 1)
            newton(SUM7, inv)
            dve.tensor_tensor(inv[:, :], inv[:, :], inv6[:, :], ALU.mult).then_inc(s_v7, 1)
            dve.wait_ge(s_v7, 4)
            done = 0
            busy = (9, 10, U_GATE + 4, U_GATE + 6)
            for u, (kind, i) in enumerate(ORDER):
                if u >= 2:
                    split(C_IN + u + AHEAD, 0)
                dve.wait_ge(s_used, C_IN + u + 1)
                ps = in_b[u % 5]
                if kind == "a":
                    dve.scalar_tensor_tensor(tmp[i % 2][:, :], ps, 0.5, inv[:, :], ALU.mult, ALU.mult).then_inc(s_i2, 1)
                else:
                    dest = {"g": tmp[2 + i % 2][:, :], "q": chunk(latf, i % QC), "kv": chunk(latf, QC + i % KVC),
                            "kr": tmp[0][:, :], "gate": chunk(gates, i)}[kind]
                    dve.tensor_tensor(dest, ps, inv[:, :], ALU.mult).then_inc(s_i2, 1)
                if kind == "g":
                    dve.wait_ge(s_th, i + 1)
                    dve.scalar_tensor_tensor(zpad[:, i * ZW + PADZ:(i + 1) * ZW], tmp[2 + i % 2][:, :], 1.0,
                                             tmp[i % 2][:, :], ALU.add, ALU.mult).then_inc(s_z, 1)
                if u == 7:
                    dve.wait_ge(s_ft, 1)
                    dve.tensor_copy(fcol[:, :], psS[:, 512:514]).then_inc(s_fc, 1)
                    dve.wait_ge(s_fc, 1)
                if u == 9:
                    r, n = rope[64:128, :], var[64:128, :]
                    MAGIC = 1.5 * 2.0 ** 23
                    C1, C2 = 6.28125, 1.93500518798828125e-3
                    C3 = 6.283185307179586 - C1 - C2
                    dve.tensor_scalar(r, pos[64:128, :], fcol[64:128, 0:1], None, ALU.mult).then_inc(s_ro, 1)
                    dve.wait_ge(s_ro, 1)
                    dve.tensor_scalar(n, r, 1.0 / 6.283185307179586, MAGIC, ALU.mult, ALU.add).then_inc(s_ro, 1)
                    dve.wait_ge(s_ro, 2)
                    dve.tensor_scalar(n, n, -MAGIC, None, ALU.add).then_inc(s_ro, 1)
                    for j, cst in enumerate((C1, C2, C3)):
                        dve.wait_ge(s_ro, 3 + j)
                        dve.scalar_tensor_tensor(r, n, -cst, r, ALU.mult, ALU.add).then_inc(s_ro, 1)
                    dve.wait_ge(s_ro, 6)
                    dve.tensor_scalar(r, r, 3.1415925, -3.1415925, ALU.min, ALU.max).then_inc(s_ro, 1)
                    c, nn = rope[64:96, :], var[64:96, :]
                    dve.wait_ge(s_ro, 7)
                    dve.scalar_tensor_tensor(nn, c, -1.0, c, ALU.mult, ALU.max).then_inc(s_ro, 1)
                    dve.wait_ge(s_ro, 8)
                    dve.tensor_scalar(c, nn, -1.0, 1.5707963267948966, ALU.mult, ALU.add).then_inc(s_rr, 1)
                if u == 11:
                    dve.wait_ge(s_rs, 2)
                    dve.tensor_scalar(rope[96:128, :], rope[96:128, :], fcol[96:128, 1:2], None, ALU.mult).then_inc(s_rs, 1)
                    dve.wait_ge(s_rs, 3)
                if u == U_KR + 1:
                    kr, kx = tmp[0][NOPE:QK, :], tmp[1][NOPE:QK, :]
                    dve.wait_ge(s_i2, u)
                    dve.tensor_tensor(kx, tmp[0][QK:P, :], rope[QK:P, :], ALU.mult).then_inc(s_kr, 1)
                    dve.tensor_tensor(kr, kr, rope[NOPE:QK, :], ALU.mult).then_inc(s_kr, 1)
                    dve.wait_ge(s_kr, 2)
                    dve.tensor_tensor(kx, kr, kx, ALU.add).then_inc(s_kr, 1)
                if u == U_GATE + 3:
                    variance(LATQ, psO[:, :], QL)
                if u == U_GATE + 4:
                    newton(LATQ, tmp[2])
                if u == U_GATE + 5:
                    variance(LATKV, psS[:, 512:1024], KVL)
                if u == U_GATE + 6:
                    newton(LATKV, tmp[3])
                if LAT <= u < LAT + QC + KVC:
                    j = u - LAT
                    f = chunk(latf, j)
                    dve.scalar_tensor_tensor(f, f, lgain[:, j:j + 1], (tmp[2] if j < QC else tmp[3])[:, :],
                                             ALU.mult, ALU.mult).then_inc(s_ln, 1)
                if LAT < u <= LAT + QC + KVC:
                    j = u - LAT - 1
                    dve.wait_ge(s_lh, j + 1)
                    dve.tensor_tensor(chunk(latl, j), chunk(latf, j), chunk(lath, j).bitcast(F32),
                                      ALU.subtract).then_inc(s_ll, 1)
                if 3 <= u <= TAP_LAST and u not in busy:
                    left = len([v for v in range(u, TAP_LAST + 1) if v not in busy])
                    for _ in range(-(-(len(DVE_TAPS) - done) // left)):
                        ci, k = DVE_TAPS[done]
                        if k == 0:
                            dve.wait_ge(s_zp, 1)
                            dve.wait_ge(s_z, ci + 1)
                            dve.tensor_scalar(chunk(zc, ci), chunk_z(ci, k), cw2[:, k * CC + ci:k * CC + ci + 1],
                                              cvec[:, ci:ci + 1], ALU.mult, ALU.add).then_inc(s_tap, 1)
                        else:
                            dve.wait_ge(s_tap, DVE_TAPS.index((ci, k - 1)) + 1)
                            dve.scalar_tensor_tensor(chunk(zc, ci), chunk_z(ci, k), cw2[:, k * CC + ci:k * CC + ci + 1],
                                                     chunk(zc, ci), ALU.mult, ALU.add).then_inc(s_tap, 1)
                        done += 1

            def k_rope(j):
                ks = slice(j * S, (j + 1) * S)
                for n, r in enumerate((NOPE, QK)):
                    dve.wait_ge(s_krh, 2 * j + n + 1)
                    dve.tensor_tensor(k2l[r:r + ROPE, ks], tmp[1][NOPE:QK, :], k2h[r:r + ROPE, ks].bitcast(F32),
                                      ALU.subtract).then_inc(s_krl, 1)

            k_rope(0)

            def head(h):
                bb = h % 2 * S
                split(head_unit(h) + AHEAD, 0)
                dve.wait_ge(s_used, head_unit(h) + 1)
                dve.tensor_tensor(tmp[0][NOPE:P, :], bank[0][NOPE:P, :], rope[NOPE:P, :], ALU.mult).then_inc(h_rp, 1)
                dve.wait_ge(h_hi, 2 * h + 1)
                dve.tensor_tensor(k2l[0:NOPE, bb:bb + S], bank[1][0:NOPE, :], k2h[0:NOPE, bb:bb + S].bitcast(F32),
                                  ALU.subtract)

            def head_q(h):
                bb = h % 2 * S
                dve.wait_ge(h_hi, 2 * h + 2)
                dve.scalar_tensor_tensor(q2l[:, bb:bb + S], tmp[0][:, :], QK ** -0.5,
                                         q2h[:, bb:bb + S].bitcast(F32), ALU.mult, ALU.subtract).then_inc(h_lo, 1)

            head(0)
            head_q(0)
            split(C_V2 + AHEAD, 0)
            for i in range(TB):
                dve.wait_ge(s_v2h, i + 1)
                dve.tensor_tensor(chunk(v2l, i), v2_b[i], chunk(v2h, i).bitcast(F32), ALU.subtract).then_inc(s_v2l, 1)
            k_rope(1)
            for s in range(MLA_STEPS + 2):
                if s < MLA_STEPS:
                    pc = s % 2 * 8
                    dve.wait_ge(b_sc, s + 1)
                    for half, i in enumerate(BLOCKS[s % 2]):
                        e = dve.tensor_reduce(st2[:, pc + half:pc + half + 1], psS[:, half * 512:half * 512 + (i + 1) * P],
                                              AX.X, ALU.max, negate=True)
                    e.then_inc(b_mx, 1)
                    dve.wait_ge(b_ex, s + 1)
                    dve.reciprocal(st2[:, pc + 4:pc + 6], st2[:, pc + 2:pc + 4]).then_inc(b_rd, 1)
                if s >= 2:
                    r = s - 2
                    h, (i1, i2) = r // 2, BLOCKS[r % 2]
                    rows = slice(h % 2 * HD, h % 2 * HD + HD)
                    dve.wait_ge(b_oh, r + 1)
                    view = lambda a: chunk(a, h // 2)[rows].rearrange("p (i n) -> p i n", n=P)[:, i1:i2 + 1:i2 - i1, :]
                    dve.tensor_tensor(view(a2l), psO[rows, 0:2 * P].rearrange("p (i n) -> p i n", n=P),
                                      view(a2h).bitcast(F32), ALU.subtract).then_inc(b_ol, 1)
                if s % 2 == 0 and s // 2 + 1 < H2:
                    head(s // 2 + 1)
                if 1 <= s <= MLA_STEPS:
                    dve.wait_ge(b_th, s)
                    dve.tensor_tensor(pt2l[:, :], psT[:, 0:(TB + 1) * P], pt2h[:, :].bitcast(F32),
                                      ALU.subtract).then_inc(b_tl, 1)
                if s % 2 == 0 and s // 2 + 1 < H2:
                    head_q(s // 2 + 1)
                if s == LN_MEAN:
                    dve.wait_ge(s_lsum, 1)
                    dve.tensor_scalar(inv6[:, :], bank[2][:, :], 1.0 / CW, None, ALU.mult).then_inc(s_lm, 1)
                if s == LN_VAR:
                    variance(LNVAR, bank[2][:, :], CW)
                if s == LN_VAR + 1:
                    newton(LNVAR, inv6)
                if LN_Y + 3 <= s < LN_Y + 3 + CC:
                    i = s - LN_Y - 3
                    dve.wait_ge(s_ch, i + 1)
                    dve.tensor_tensor(chunk(clo, i), chunk(zc, i), chunk(chi, i).bitcast(F32), ALU.subtract).then_inc(s_cl, 1)

            dve.wait_ge(s_gt, 2 * KC)
            for m in range(KC):
                split(C_MRG + m + AHEAD, 0)
                dve.wait_ge(s_used, C_MRG + m + 1)
                t1, t2 = tmp[m % 2][:, :], tmp[2 + m % 2][:, :]
                dve.scalar_tensor_tensor(t1, chunk(gates, m), 1.0, b(gate_b[m % 2][:, :]), ALU.add, ALU.mult).then_inc(s_ga, 1)
                dve.scalar_tensor_tensor(t2, chunk(gates, KC + m), 1.0, b(up_b[m % 2][:, :]), ALU.add, ALU.mult).then_inc(s_ga, 1)
                dve.wait_ge(s_ga, 2 * m + 2)
                dve.tensor_tensor(t2, t2, t1, ALU.add).then_inc(s_mg, 1)
                dve.wait_ge(s_mgh, m + 1)
                dve.scalar_tensor_tensor(chunk(mgl, m), t2, 0.5, chunk(mgh, m).bitcast(F32), ALU.mult,
                                         ALU.subtract).then_inc(s_mgl, 1)
            for m in range(KC):
                split(C_OUT + m + AHEAD, 0)
                if m == 1:
                    v, y = st2[:, 18:20], st2[:, 20:22]
                    dve.wait_ge(s_msq, 1)
                    dve.tensor_scalar(v, st2[:, 16:18], 1.0 / D, EPS, ALU.mult, ALU.add).then_inc(s_mst, 1)
                    dve.wait_ge(s_mr, 1)
                    dve.reciprocal(y, y).then_inc(s_mst, 1)
                    for j in range(2):
                        dve.wait_ge(s_mst, j + 2)
                        dve.tensor_tensor(v, v, y, ALU.mult).then_inc(s_mst, 1)
                    dve.wait_ge(s_mst, 4)
                    dve.tensor_scalar(v, v, -0.5, 1.5, ALU.mult, ALU.add).then_inc(s_mst, 1)
                    dve.wait_ge(s_mst, 5)
                    dve.tensor_tensor(y, v, y, ALU.mult).then_inc(s_mst, 1)
                    dve.wait_ge(s_mst, 6)
                    for i in range(MB):
                        mr = memr[:, i * D:(i + 1) * D]
                        dve.tensor_scalar(mr, mr, st2[:, 20 + i:21 + i], None, ALU.mult).then_inc(s_mn, 1)
                if m in (3, 6):
                    r = m // 6
                    for i in range(4):
                        cc = 4 * r + i
                        ms = slice(cc * ML, (cc + 1) * ML)
                        dve.wait_ge(s_mh, cc // 2 * 2 + 2)
                        dve.scalar_tensor_tensor(mtl[:, ms], psS[:, i * ML:(i + 1) * ML],
                                                 gains[:, GMEM * KC + cc:GMEM * KC + cc + 1], mth[:, ms].bitcast(F32),
                                                 ALU.mult, ALU.subtract).then_inc(s_ml, 1)
                dve.wait_ge(s_used, C_OUT + m + 1)
                dve.tensor_tensor(chunk(x, m), down_b[m % 2], chunk(x, m), ALU.add).then_inc(s_x, 1)
                x_lo(FINAL1 + 1, m, xbl, xbh)

            for j in range(H3):
                split(C_XQ + j + AHEAD, 0)
                if j == 0:
                    inverse(XATTN)
                dve.wait_ge(s_used, C_XQ + j + 1)
                dve.scalar_tensor_tensor(tmp[j % 2][:, :], bank[j % 3][:, :], P ** -0.5, inv[:, :], ALU.mult,
                                         ALU.mult).then_inc(s_x2, 1)
                dve.wait_ge(s_x2h, j + 1)
                dve.tensor_tensor(chunk(q3l, j), tmp[j % 2][:, :], chunk(q3h, j).bitcast(F32), ALU.subtract).then_inc(s_x2l, 1)
            for j in range(H3):
                split(C_XK + j + AHEAD, 0)
                dve.wait_ge(s_k3h, j + 1)
                ks = slice(j * ML, (j + 1) * ML)
                dve.tensor_tensor(k3l[:, ks], bank[(H3 + j) % 3][:, 0:ML], k3h[:, ks].bitcast(F32), ALU.subtract).then_inc(s_k3l, 1)

            def cross_max(s):
                pc = s % 2 * 16
                dve.wait_ge(d_sc, s + 1)
                dve.tensor_reduce(st[:, pc:pc + 4], psS[:, :].rearrange("p (h n) -> p h n", h=H3), AX.X, ALU.max,
                                  negate=True).then_inc(d_mx, 1)

            def cross_rden(s):
                pc = s % 2 * 16
                dve.wait_ge(d_ex, s + 1)
                dve.reciprocal(st[:, pc + 8:pc + 12], st[:, pc + 4:pc + 8]).then_inc(d_rd, 1)

            def cross_lo(s):
                dve.wait_ge(d_th, s + 1)
                dve.tensor_tensor(pt3l[:, :], psT[:, :], pt3h[:, :].bitcast(F32), ALU.subtract).then_inc(d_tl, 1)

            def cross_out(s):
                dve.wait_ge(d_oh, s + 1)
                view = lambda a: a[:, :].rearrange("p (h n) -> p h n", h=H3)[:, :, s * P:(s + 1) * P]
                dve.tensor_tensor(view(a3l), psO[:, :].rearrange("p (h n) -> p h n", h=H3), view(a3h).bitcast(F32),
                                  ALU.subtract).then_inc(d_ol, 1)

            cross_max(0)
            split(C_XV + AHEAD, 0)
            cross_rden(0)
            cross_max(1)
            split(C_XV + 1 + AHEAD, 0)
            split(C_XV + 2 + AHEAD, 0)
            cross_rden(1)
            cross_lo(0)
            split(C_XV + 3 + AHEAD, 0)
            for i in range(MB):
                dve.wait_ge(s_v3h, i + 1)
                dve.tensor_tensor(chunk(v3l, i), bank[2 * (1 - i)][:, :], chunk(v3h, i).bitcast(F32),
                                  ALU.subtract).then_inc(s_v3l, 1)
            cross_max(2)
            cross_rden(2)
            cross_out(0)
            cross_lo(1)
            cross_max(3)
            cross_rden(3)
            cross_out(1)
            cross_lo(2)
            cross_out(2)
            cross_lo(3)
            cross_out(3)
            for j in range(KC // 2):
                split(C_XO + j + AHEAD, 0)
                dve.wait_ge(s_used, C_XO + j + 1)
                for i in range(2):
                    m = 2 * j + i
                    dve.tensor_tensor(chunk(x, m), xo_b[2 * (j % 2) + i], chunk(x, m), ALU.add).then_inc(s_x, 1)
                    x_lo(FINAL1 + 2, m)

            mlp_b = [bank[0][:, :], bank[1][:, :], bank[2][:, :], psS[:, 0:S]]
            for ps in range(2):
                c0 = C_MLP + ps * U_PASS

                def four(c, q, fi, first):
                    for j in range(4):
                        split(c + j + AHEAD, q)
                        if first and ps == 0 and j == 0:
                            inverse(MLPN)
                        f = fi + (ps * FP + j)
                        dve.wait_ge(s_used, q + (c + j + 1))
                        dve.scalar_tensor_tensor(tmp[j % 2][:, :], mlp_b[j], 0.0, inv[:, :], ALU.max, ALU.mult).then_inc(m_r, 1)
                        dve.wait_ge(m_hi, f + 1)
                        hs = ds((fi + j) * S, S)
                        dve.tensor_tensor(mlo[:, hs], tmp[2 + j % 2][:, :], mhi[:, hs].bitcast(F32), ALU.subtract).then_inc(m_lo, 1)
                four(c0, 0, 0, True)
                with dve.Fori(1, FP // 4) as it:
                    four(c0, it * 4, it * 4, False)
                with dve.Fori(0, KC // 2) as mi:
                    for m in range(2):
                        for j in range(2):
                            split(c0 + FP + 2 * m + j + AHEAD, mi * 4)
                        dve.wait_ge(s_used, mi * 4 + (c0 + FP + 2 * m + 2))
                        xm = x[:, ds(mi * (2 * S) + m * S, S)]
                        dve.tensor_tensor(xm, down_b[m], xm, ALU.add).then_inc(s_x, 1)
            v, y = fin[:, 0:TB], fin[:, TB:2 * TB]
            dve.wait_ge(s_ss, FINAL2 + 1)
            dve.tensor_scalar(v, psO[:, 0:TB], 1.0 / D, EPS, ALU.mult, ALU.add).then_inc(s_fv, 1)
            dve.wait_ge(s_rt, FINAL2 + 1)
            dve.reciprocal(y, y).then_inc(s_fv, 1)
            for j in range(2):
                dve.wait_ge(s_fv, j + 2)
                dve.tensor_tensor(v, v, y, ALU.mult).then_inc(s_fv, 1)
            dve.wait_ge(s_fv, 4)
            dve.tensor_scalar(v, v, -0.5, 1.5, ALU.mult, ALU.add).then_inc(s_fv, 1)
            dve.wait_ge(s_fv, 5)
            dve.tensor_tensor(y, v, y, ALU.mult).then_inc(s_fv, 1)
            dve.wait_ge(s_fv, 6)
            for n in range(0, 2 * TB, 2):
                dve.wait_ge(s_ot, n + 1)
                dve.tensor_scalar(yout[:, n * 512:(n + 1) * 512], out_b[n % len(out_b)],
                                  fin[:, TB + n % TB:TB + n % TB + 1], None, ALU.mult).then_inc(s_oc[0], 1)

        @block.gpsimd
        def _(pool):
            def squares(N, r=None):
                r = N if r is None else r
                for m in range(KC):
                    pool.wait_ge(s_x, N * KC + m + 1)
                    xm = chunk(x, m)
                    if m == 0:
                        pool.tensor_tensor(acc[:, :], xm, xm, ALU.mult).then_inc(s_sq, 1)
                        continue
                    pool.wait_ge(s_sq, r * KC + m)
                    pool.tensor_tensor(sqt[:, :], xm, xm, ALU.mult).then_inc(s_sqm, 1)
                    pool.wait_ge(s_sqm, r * (KC - 1) + m)
                    pool.tensor_tensor(acc[:, :], acc[:, :], sqt[:, :], ALU.add).then_inc(s_sq, 1)

            def mix(l):
                for u in range(3 * CC + 1):
                    if 1 <= u and u - 1 < STEPS1:
                        s = u - 1
                        n = P if s < 2 else 2 * P
                        pool.wait_ge(a_rd, l * STEPS1 + s + 1)
                        a = sc[s % 2][:, :].rearrange("p (h n) -> p h n", h=4)[:, :, 0:n]
                        r = 24 + 4 * (s % 2)
                        pool.tensor_tensor(a, a, st[:, r:r + 4].unsqueeze(2).to_broadcast([P, 4, n]),
                                           ALU.mult).then_inc(a_pr, 1)
                    if u % 3 == 2:
                        i = u // 3
                        if i == 0:
                            pool.wait_ge(s_pad, l + 1)
                        if i >= 2:
                            pool.wait_ge(c_t0, l * CC + i - 1)
                        pool.wait_ge(c_ev, l * 3 * CC + 3 * i + 3)
                        pool.tensor_tensor(upad[i % 2][:, 2:2 + S], tmp[2][:, :], tmp[3][:, :], ALU.mult).then_inc(c_u, 1)
                    if u % 3 == 0 and u >= 3:
                        i = u // 3 - 1
                        pool.wait_ge(c_t0, l * CC + i + 1)
                        pool.tensor_tensor(cy[i % 2][:, :], cy[i % 2][:, :], tmp[i % 2][:, :], ALU.mult).then_inc(c_y, 1)

            pool.memset(ident[:, :], 0.0).then_inc(s_ident, 1)
            pool.wait_ge(s_ident, 1)
            pool.affine_select(out=ident[:, :], in_=ident[:, :], compare_op=ALU.not_equal, fill=1.0,
                               base=0, pattern=[[-1, P]], channel_multiplier=1).then_inc(s_const, 1)
            pool.iota(dist[:, :], [[-1, 2 * P]], base=P, channel_multiplier=1,
                      allow_small_or_imprecise_dtypes=True).then_inc(s_ident, 1)
            pool.wait_ge(s_ident, 2)
            pool.affine_select(out=dist[:, :], in_=dist[:, :], compare_op=ALU.is_ge, fill=MASKED,
                               base=P, pattern=[[-1, 2 * P]], channel_multiplier=1).then_inc(s_ident, 1)
            pool.wait_ge(s_ident, 3)
            pool.affine_select(out=dist[:, :], in_=dist[:, :], compare_op=ALU.is_gt, fill=MASKED,
                               base=0, pattern=[[1, 2 * P]], channel_multiplier=-1).then_inc(s_const, 1)
            for i in range(HALF):
                f = pool.memset(frow[0:1, i:P:HALF], 10000.0 ** (-i / HALF))
            f.then_inc(s_fr, 1)
            pool.memset(frow[0:1, P:2 * P], 1.0).then_inc(s_fr, 1)
            pool.wait_ge(s_fr, 2)
            pool.memset(frow[0:1, P + QK:P + QK + HALF], -1.0).then_inc(s_fr, 1)
            pool.memset(mask[:, :], 0.0).then_inc(s_mk, 1)
            pool.wait_ge(s_mk, 1)
            pool.affine_select(out=mask[:, :], in_=mask[:, :], compare_op=ALU.is_ge, fill=-MASKED,
                               base=0, pattern=[[-1, P]], channel_multiplier=1).then_inc(s_mk, 1)
            with pool.Fori(0, L) as l:
                squares(l * 3)
                squares(l * 3 + 1)
                mix(l)
                squares(l * 3 + 2)
            squares(FINAL1)
            pool.memset(zpad[:, :].rearrange("p (i n) -> p i n", i=CC)[:, :, 0:PADZ], 0.0).then_inc(s_zp, 1)
            for a, (i, k) in enumerate(POOL_TAPS):
                if 8 <= a < 8 + KC:
                    m = a - 8
                    pool.wait_ge(s_xg, m + 1)
                    pool.tensor_tensor(chunk(x, m), chunk(x, m), inv6[:, :], ALU.mult)
                pool.wait_ge(s_pm, a + 2 + (i == 3))
                if k >= 2:
                    pool.wait_ge(s_pa, a)
                pool.tensor_tensor(chunk(zc, i), chunk(zc, i), (acc, sqt)[a % 2][:, :], ALU.add).then_inc(s_pa, 1)
            for s in range(MLA_STEPS):
                o, pc = 0, s % 2 * 8
                pool.wait_ge(b_rd, s + 1)
                for half, i in enumerate(BLOCKS[s % 2]):
                    a = p2[s % 2][:, o:o + (i + 1) * P]
                    e = pool.tensor_tensor(a, a, st2[:, pc + 4 + half:pc + 5 + half].to_broadcast([P, (i + 1) * P]), ALU.mult)
                    o += (i + 1) * P
                e.then_inc(b_pr, 1)
                if s == LN_MEAN:
                    pool.wait_ge(s_lm, 1)
                    for j in range(CC):
                        pool.tensor_tensor(chunk(zc, j), chunk(zc, j), inv6[:, :], ALU.subtract).then_inc(s_ld, 1)
                if s == LN_VAR + 1:
                    pool.wait_ge(s_inv, LNVAR + 1)
                    for i in range(CC):
                        pool.tensor_tensor(chunk(zc, i), chunk(zc, i), inv6[:, :], ALU.mult).then_inc(s_ly, 1)
            squares(FINAL1 + 1)
            for s in range(TB):
                pc = s % 2 * 16
                pool.wait_ge(d_rd, s + 1)
                a = p3[s % 2][:, :].rearrange("p (h n) -> p h n", h=H3)
                pool.tensor_tensor(a, a, st[:, pc + 8:pc + 12].unsqueeze(2).to_broadcast([P, H3, ML]), ALU.mult).then_inc(d_pr, 1)
            squares(FINAL1 + 2)
            squares(FINAL1 + 4, FINAL1 + 3)



_NAMES = ["x", "ffn1_norm", "ffn1_wg", "ffn1_wu", "ffn1_wd", "mix_norm", "w_in", "conv_w", "attn_sink", "w_out",
          "ffn2_norm", "ffn2_wg", "ffn2_wu", "ffn2_wd", "final_norm", "mem_2", "positions_2", "norm_mix_g_2", "w_in_2",
          "conv_w_2", "conv_b_2", "conv_ln_g_2", "conv_ln_b_2", "w_conv_out_2", "q_norm_g_2", "w_uq_2", "kv_norm_g_2",
          "w_ukv_2", "w_mla_out_2", "w_out_2", "norm_xattn_g_2", "norm_mem_g_2", "w_xq_2", "w_xkv_2", "w_xo_2",
          "norm_mlp_g_2", "w_mlp1_2", "w_mlp2_2", "final_norm_g_2"]


def kernel(**inputs):
    import numpy as _np
    import concourse.bacc as _bacc
    from concourse import mybir as _mybir
    from concourse.bass_utils import run_bass_kernel_spmd as _run

    nc = _bacc.Bacc("TRN2", target_bir_lowering=False, num_devices=1,
                    dynamic_dma_scratch_size=2048)
    arrays, t = {}, {}
    for name in _NAMES:
        a = _np.ascontiguousarray(inputs[name])
        arrays[f"in_{name}"] = a
        t[name] = nc.dram_tensor(f"in_{name}", a.shape, _mybir.dt.from_np(a.dtype), kind="ExternalInput").ap()
    out = nc.dram_tensor("out_0", inputs["x"].shape, _mybir.dt.float32, kind="ExternalOutput").ap()
    build(nc, t, out)
    r = _run(nc, [arrays], core_ids=[0])
    return r.results[0]["out_0"]
```
